# Optimizing a Trainium2 kernel written in Bass

```python
import math
import jax, jax.numpy as jnp
from jax import lax
import numpy as np

D_MODEL = 1024
BATCH = 1
SEQ = 256
DEPTH = 1

MEM_LEN = 256
MLA_NOPE = 128
MLA_ROPE = 64
MLA_V = 128
MLA_HEADS = D_MODEL // MLA_V
MLA_KV_RANK = 256
GLA_HEADS = 4
GLA_DK = D_MODEL // 2 // GLA_HEADS
GLA_DV = D_MODEL // GLA_HEADS
GLA_GATE_RANK = 16
GLA_GATE_NORMALIZER = 16.0
GLA_CHUNK = 64
MEM_HEADS = 4
MEM_DQK = 64
MEM_DV = D_MODEL // MEM_HEADS
N_BRANCHES = 3
D_FF = 4 * D_MODEL
ATTN_BLOCK = 128
ROPE_THETA = 10000.0
EPS = 1e-6

IN_SPLITS = (
    MLA_HEADS * (MLA_NOPE + MLA_ROPE),
    MLA_KV_RANK,
    MLA_ROPE,
    GLA_HEADS * GLA_DK,
    GLA_HEADS * GLA_DK,
    GLA_HEADS * GLA_DV,
    GLA_GATE_RANK,
    GLA_HEADS * GLA_DV,
    MEM_HEADS * MEM_DQK,
    N_BRANCHES * D_MODEL,
)
D_IN = sum(IN_SPLITS)


def rms_norm(t, g):
    tf = t.astype(jnp.float32)
    y = tf * lax.rsqrt(jnp.mean(tf * tf, axis=-1, keepdims=True) + EPS)
    return (y * g.astype(jnp.float32)).astype(t.dtype)

def rope_tables(positions):
    inv = 1.0 / (ROPE_THETA ** (jnp.arange(0, MLA_ROPE, 2, dtype=jnp.float32) / MLA_ROPE))
    ang = positions.astype(jnp.float32)[..., None] * inv
    return jnp.cos(ang), jnp.sin(ang)

def apply_rope(t, cos, sin):
    tf = t.astype(jnp.float32)
    t1, t2 = jnp.split(tf, 2, axis=-1)
    c = cos[:, :, None, :]
    s = sin[:, :, None, :]
    return jnp.concatenate([t1 * c - t2 * s, t1 * s + t2 * c], axis=-1).astype(t.dtype)

def causal_block_attention(q, k, v, scale):
    B, S, H, D = q.shape
    Dv = v.shape[-1]
    nb = S // ATTN_BLOCK
    qb = q.reshape(B, nb, ATTN_BLOCK, H, D).transpose(1, 0, 3, 2, 4)
    kh = k.transpose(0, 2, 1, 3)
    vh = v.transpose(0, 2, 1, 3)
    kpos = jnp.arange(S)

    def one_block(args):
        qi, i = args
        s = jnp.einsum('bhqd,bhkd->bhqk', qi, kh).astype(jnp.float32) * scale
        qpos = i * ATTN_BLOCK + jnp.arange(ATTN_BLOCK)
        s = jnp.where(kpos[None, :] <= qpos[:, None], s, -1e30)
        p = jax.nn.softmax(s, axis=-1).astype(vh.dtype)
        return jnp.einsum('bhqk,bhkd->bhqd', p, vh)

    o = lax.map(one_block, (qb, jnp.arange(nb)))
    return o.transpose(1, 0, 3, 2, 4).reshape(B, S, H, Dv)

def gla_chunked(q, k, v, log_a):
    B, S, H, DK = q.shape
    DV = v.shape[-1]
    C = GLA_CHUNK
    nc = S // C

    def to_chunks(t):
        return t.astype(jnp.float32).reshape(B, nc, C, H, t.shape[-1]).transpose(1, 0, 3, 2, 4)

    qc, kc, vc = to_chunks(q), to_chunks(k), to_chunks(v)
    bc = jnp.cumsum(to_chunks(log_a), axis=3)
    mask = jnp.tril(jnp.ones((C, C), dtype=bool))[None, None, :, :, None]

    def step(state, inp):
        qi, ki, vi, bi = inp
        diff = bi[:, :, :, None, :] - bi[:, :, None, :, :]
        decay = jnp.where(mask, jnp.exp(jnp.where(mask, diff, 0.0)), 0.0)
        a = jnp.einsum('bhid,bhjd,bhijd->bhij', qi, ki, decay)
        o_intra = jnp.einsum('bhij,bhje->bhie', a, vi)
        o_inter = jnp.einsum('bhid,bhde->bhie', qi * jnp.exp(bi), state)
        b_last = bi[:, :, -1, :]
        k_dec = ki * jnp.exp(b_last[:, :, None, :] - bi)
        new_state = jnp.exp(b_last)[..., None] * state + jnp.einsum('bhjd,bhje->bhde', k_dec, vi)
        return new_state, o_intra + o_inter

    state0 = jnp.zeros((B, H, DK, DV), jnp.float32)
    _, o = lax.scan(step, state0, (qc, kc, vc, bc))
    return o.transpose(1, 0, 3, 2, 4).reshape(B, S, H, DV).astype(q.dtype)

def hybrid_layer(x, mem, cos, sin, g_mix, w_in, b_gate, g_ckv, w_ukv, g_q_nope, g_k_nope,
                 g_q_rope, g_k_rope, w_gla_gate, b_gla_gate, g_gla_out, g_mem, w_mem_kv,
                 g_q_mem, g_k_mem, w_o, g_ffn, w_up, w_down):
    B, S, _ = x.shape
    M = mem.shape[1]
    h = rms_norm(x, g_mix)
    proj = h @ w_in
    offsets = []
    acc = 0
    for n in IN_SPLITS[:-1]:
        acc += n
        offsets.append(acc)
    (q_mla, c_kv, k_rope, q_gla, k_gla, v_gla, a_gla, r_gla, q_mem,
     gate_logits) = jnp.split(proj, offsets, axis=-1)

    q_mla = q_mla.reshape(B, S, MLA_HEADS, MLA_NOPE + MLA_ROPE)
    q_nope = rms_norm(q_mla[..., :MLA_NOPE], g_q_nope)
    q_pe = apply_rope(rms_norm(q_mla[..., MLA_NOPE:], g_q_rope), cos, sin)
    kv = (rms_norm(c_kv, g_ckv) @ w_ukv).reshape(B, S, MLA_HEADS, MLA_NOPE + MLA_V)
    k_nope = rms_norm(kv[..., :MLA_NOPE], g_k_nope)
    v_mla = kv[..., MLA_NOPE:]
    k_pe = apply_rope(rms_norm(k_rope, g_k_rope)[:, :, None, :], cos, sin)
    q_full = jnp.concatenate([q_nope, q_pe], axis=-1)
    k_full = jnp.concatenate([k_nope, jnp.broadcast_to(k_pe, (B, S, MLA_HEADS, MLA_ROPE))], axis=-1)
    o_mla = causal_block_attention(q_full, k_full, v_mla,
                                   (MLA_NOPE + MLA_ROPE) ** -0.5).reshape(B, S, MLA_HEADS * MLA_V)

    qg = q_gla.reshape(B, S, GLA_HEADS, GLA_DK) * (GLA_DK ** -0.5)
    kg = k_gla.reshape(B, S, GLA_HEADS, GLA_DK)
    vg = v_gla.reshape(B, S, GLA_HEADS, GLA_DV)
    log_a = jax.nn.log_sigmoid((a_gla @ w_gla_gate + b_gla_gate).astype(jnp.float32)) / GLA_GATE_NORMALIZER
    log_a = log_a.reshape(B, S, GLA_HEADS, GLA_DK)
    og = gla_chunked(qg, kg, vg, log_a)
    o_gla = rms_norm(og, g_gla_out).reshape(B, S, GLA_HEADS * GLA_DV) * jax.nn.silu(r_gla)

    kv_m = rms_norm(mem, g_mem) @ w_mem_kv
    k_m = rms_norm(kv_m[..., :MEM_HEADS * MEM_DQK].reshape(B, M, MEM_HEADS, MEM_DQK), g_k_mem)
    v_m = kv_m[..., MEM_HEADS * MEM_DQK:].reshape(B, M, MEM_HEADS, MEM_DV)
    q_m = rms_norm(q_mem.reshape(B, S, MEM_HEADS, MEM_DQK), g_q_mem)
    s_m = jnp.einsum('bshd,bmhd->bhsm', q_m, k_m).astype(jnp.float32) * (MEM_DQK ** -0.5)
    p_m = jax.nn.softmax(s_m, axis=-1).astype(v_m.dtype)
    o_mem = jnp.einsum('bhsm,bmhd->bshd', p_m, v_m).reshape(B, S, MEM_HEADS * MEM_DV)

    gates = jax.nn.sigmoid(gate_logits + b_gate).reshape(B, S, N_BRANCHES, D_MODEL)
    y = gates[..., 0, :] * o_mla + gates[..., 1, :] * o_gla + gates[..., 2, :] * o_mem
    x = x + y @ w_o

    h2 = rms_norm(x, g_ffn)
    return x + jnp.square(jax.nn.relu(h2 @ w_up)) @ w_down

def first_inputs(seed: int = 0) -> dict:
    key = jax.random.key(seed)
    ks = jax.random.split(key, 24)
    L = DEPTH

    def w(k, shape, fan_in):
        return jax.random.normal(k, (L,) + shape, jnp.float32) * (fan_in ** -0.5)

    def gain(k, n):
        return 1.0 + 0.02 * jax.random.normal(k, (L, n), jnp.float32)

    def bias(k, n):
        return 0.01 * jax.random.normal(k, (L, n), jnp.float32)

    x = jax.random.normal(ks[0], (BATCH, SEQ, D_MODEL), jnp.float32)
    mem = jax.random.normal(ks[1], (BATCH, MEM_LEN, D_MODEL), jnp.float32)
    positions = (jax.random.randint(ks[2], (BATCH, 1), 0, 4096, dtype=jnp.int32)
                 + jnp.arange(SEQ, dtype=jnp.int32)[None, :])
    return {
        'x': x,
        'mem': mem,
        'positions': positions,
        'g_mix': gain(ks[3], D_MODEL),
        'w_in': w(ks[4], (D_MODEL, D_IN), D_MODEL),
        'b_gate': bias(ks[5], N_BRANCHES * D_MODEL),
        'g_ckv': gain(ks[6], MLA_KV_RANK),
        'w_ukv': w(ks[7], (MLA_KV_RANK, MLA_HEADS * (MLA_NOPE + MLA_V)), MLA_KV_RANK),
        'g_q_nope': gain(ks[8], MLA_NOPE),
        'g_k_nope': gain(ks[9], MLA_NOPE),
        'g_q_rope': gain(ks[10], MLA_ROPE),
        'g_k_rope': gain(ks[11], MLA_ROPE),
        'w_gla_gate': w(ks[12], (GLA_GATE_RANK, GLA_HEADS * GLA_DK), GLA_GATE_RANK),
        'b_gla_gate': bias(ks[13], GLA_HEADS * GLA_DK),
        'g_gla_out': gain(ks[14], GLA_DV),
        'g_mem': gain(ks[15], D_MODEL),
        'w_mem_kv': w(ks[16], (D_MODEL, MEM_HEADS * (MEM_DQK + MEM_DV)), D_MODEL),
        'g_q_mem': gain(ks[17], MEM_DQK),
        'g_k_mem': gain(ks[18], MEM_DQK),
        'w_o': w(ks[19], (D_MODEL, D_MODEL), D_MODEL),
        'g_ffn': gain(ks[20], D_MODEL),
        'w_up': w(ks[21], (D_MODEL, D_FF), D_MODEL),
        'w_down': w(ks[22], (D_FF, D_MODEL), D_FF),
    }

def first_block(x, mem, positions, g_mix, w_in, b_gate, g_ckv, w_ukv, g_q_nope, g_k_nope,
              g_q_rope, g_k_rope, w_gla_gate, b_gla_gate, g_gla_out, g_mem, w_mem_kv,
              g_q_mem, g_k_mem, w_o, g_ffn, w_up, w_down):
    cos, sin = rope_tables(positions)
    for l in range(DEPTH):
        x = hybrid_layer(x, mem, cos, sin, g_mix[l], w_in[l], b_gate[l], g_ckv[l], w_ukv[l],
                         g_q_nope[l], g_k_nope[l], g_q_rope[l], g_k_rope[l], w_gla_gate[l],
                         b_gla_gate[l], g_gla_out[l], g_mem[l], w_mem_kv[l], g_q_mem[l],
                         g_k_mem[l], w_o[l], g_ffn[l], w_up[l], w_down[l])
    return x


SSM_WIDTH = D_MODEL
SSM_GROUP = 16
SSM_GROUPS = SSM_WIDTH // SSM_GROUP
SSM_STATE = 64
SSM_CHUNK = 128
DT_MIN = 1e-3
DT_MAX = 1e-1
HEAD_DIM = 64
HEADS_PER_GROUP = D_MODEL // 128
DILATED_GROUPS = ((128, 1), (512, 4), (2048, 16))
N_DIL = len(DILATED_GROUPS)
ATTN_WIDTH = HEADS_PER_GROUP * HEAD_DIM
QKV_WIDTH = N_DIL * ATTN_WIDTH
ROPE_DIM = HEAD_DIM // 4
ROPE_THETA_2 = 500000.0
Q_BLOCK = 128
NEG_INF = -1e30
SPLITS = (SSM_WIDTH, SSM_WIDTH, QKV_WIDTH, QKV_WIDTH, QKV_WIDTH, ATTN_WIDTH, D_MODEL, D_MODEL)
IN_WIDTH = sum(SPLITS)


def rms_norm_2(x, w):
    xf = x.astype(jnp.float32)
    y = xf * lax.rsqrt(jnp.mean(xf * xf, axis=-1, keepdims=True) + EPS)
    return y * w.astype(jnp.float32)

def apply_partial_rope(x, positions):
    half = ROPE_DIM // 2
    inv_freq = ROPE_THETA_2 ** (-jnp.arange(0, ROPE_DIM, 2, dtype=jnp.float32) / ROPE_DIM)
    ang = positions.astype(jnp.float32)[..., None] * inv_freq
    cos = jnp.cos(ang)[:, :, None, None, :]
    sin = jnp.sin(ang)[:, :, None, None, :]
    x1 = x[..., :half]
    x2 = x[..., half:ROPE_DIM]
    return jnp.concatenate([x1 * cos - x2 * sin, x2 * cos + x1 * sin, x[..., ROPE_DIM:]], axis=-1)

def _complex_diag_combine(e1, e2):
    a1r, a1i, b1r, b1i = e1
    a2r, a2i, b2r, b2i = e2
    ar = a2r * a1r - a2i * a1i
    ai = a2r * a1i + a2i * a1r
    br = a2r * b1r - a2i * b1i + b2r
    bi = a2r * b1i + a2i * b1r + b2i
    return (ar, ai, br, bi)

def s5_branch(u, lam_re, lam_im, log_dt, b_re, b_im, c_re, c_im, d_skip, w_glu):
    f32 = jnp.float32
    uf = u.astype(f32)
    lr, li = lam_re.astype(f32), lam_im.astype(f32)
    dt = jnp.exp(log_dt.astype(f32))[:, None]
    mag = jnp.exp(lr * dt)
    ab_re = mag * jnp.cos(li * dt)
    ab_im = mag * jnp.sin(li * dt)
    den = lr * lr + li * li
    nr = ab_re - 1.0
    f_re = (nr * lr + ab_im * li) / den
    f_im = (ab_im * lr - nr * li) / den
    br, bi = b_re.astype(f32), b_im.astype(f32)
    bb_re = f_re[..., None] * br - f_im[..., None] * bi
    bb_im = f_re[..., None] * bi + f_im[..., None] * br
    cr, ci = c_re.astype(f32), c_im.astype(f32)

    bsz, length, _ = u.shape
    n_chunks = length // SSM_CHUNK
    uc = uf.reshape(bsz, n_chunks, SSM_CHUNK, SSM_GROUPS, SSM_GROUP).transpose(1, 0, 2, 3, 4)

    def chunk_step(carry, u_c):
        h0_re, h0_im = carry
        bu_re = jnp.einsum('blgp,gnp->blgn', u_c, bb_re)
        bu_im = jnp.einsum('blgp,gnp->blgn', u_c, bb_im)
        a_re = jnp.broadcast_to(ab_re, bu_re.shape)
        a_im = jnp.broadcast_to(ab_im, bu_im.shape)
        pa_re, pa_im, hs_re, hs_im = lax.associative_scan(
            _complex_diag_combine, (a_re, a_im, bu_re, bu_im), axis=1)
        h_re = hs_re + pa_re * h0_re[:, None] - pa_im * h0_im[:, None]
        h_im = hs_im + pa_re * h0_im[:, None] + pa_im * h0_re[:, None]
        y = jnp.einsum('blgn,gpn->blgp', h_re, cr) - jnp.einsum('blgn,gpn->blgp', h_im, ci)
        return (h_re[:, -1], h_im[:, -1]), y

    zeros = jnp.zeros((bsz, SSM_GROUPS, SSM_STATE), f32)
    _, y = lax.scan(chunk_step, (zeros, zeros), uc)
    y = y.transpose(1, 0, 2, 3, 4).reshape(bsz, length, SSM_WIDTH)
    y = y + d_skip.astype(f32) * uf
    g = jax.nn.gelu(y)
    return g * jax.nn.sigmoid(g @ w_glu.astype(f32))

def dilated_attention(q, k, v):
    bsz, length = q.shape[0], q.shape[1]
    n_blocks = length // Q_BLOCK
    scale = 1.0 / math.sqrt(HEAD_DIM)
    k_groups = [k[:, :, g] for g in range(N_DIL)]
    v_groups = [v[:, :, g] for g in range(N_DIL)]

    def one_block(i):
        t = i * Q_BLOCK + jnp.arange(Q_BLOCK)
        q_blk = lax.dynamic_slice_in_dim(q, i * Q_BLOCK, Q_BLOCK, axis=1)
        outs, lses = [], []
        for g, (window, dil) in enumerate(DILATED_GROUPS):
            j = jnp.arange(window // dil + 1)
            idx = t[:, None] - dil * j[None, :]
            valid = idx >= 0
            idxc = jnp.maximum(idx, 0)
            kg = k_groups[g][:, idxc]
            vg = v_groups[g][:, idxc]
            s = jnp.einsum('bqhd,bqjhd->bqhj', q_blk[:, :, g], kg) * scale
            s = jnp.where(valid[None, :, None, :], s, NEG_INF)
            lse = jax.nn.logsumexp(s, axis=-1)
            p = jnp.exp(s - lse[..., None])
            outs.append(jnp.einsum('bqhj,bqjhd->bqhd', p, vg))
            lses.append(lse)
        w = jax.nn.softmax(jnp.stack(lses), axis=0)
        return jnp.einsum('gbqh,gbqhd->bqhd', w, jnp.stack(outs))

    o = lax.map(one_block, jnp.arange(n_blocks))
    return o.transpose(1, 0, 2, 3, 4).reshape(bsz, length, HEADS_PER_GROUP * HEAD_DIM)

def second_inputs(seed: int = 0) -> dict:
    key = jax.random.key(seed)
    ks = jax.random.split(key, 20)
    f32 = jnp.float32
    x = jax.random.normal(ks[0], (BATCH, SEQ, D_MODEL), f32)
    start = jax.random.randint(ks[1], (BATCH, 1), 0, 1024, dtype=jnp.int32)
    positions = (start + jnp.arange(SEQ, dtype=jnp.int32)[None, :]).astype(jnp.int32)
    norm_w = 1.0 + 0.02 * jax.random.normal(ks[2], (DEPTH, D_MODEL), f32)
    w_in = jax.random.normal(ks[3], (DEPTH, D_MODEL, IN_WIDTH), f32) * D_MODEL ** -0.5
    n_idx = jnp.arange(SSM_STATE, dtype=f32)
    lam_re = -0.5 + 0.01 * jax.random.normal(ks[4], (DEPTH, SSM_GROUPS, SSM_STATE), f32)
    lam_im = math.pi * n_idx + 0.01 * jax.random.normal(ks[5], (DEPTH, SSM_GROUPS, SSM_STATE), f32)
    log_dt = jax.random.uniform(ks[6], (DEPTH, SSM_GROUPS), f32, math.log(DT_MIN), math.log(DT_MAX))
    b_scale = (2.0 * SSM_GROUP) ** -0.5
    b_re = jax.random.normal(ks[7], (DEPTH, SSM_GROUPS, SSM_STATE, SSM_GROUP), f32) * b_scale
    b_im = jax.random.normal(ks[8], (DEPTH, SSM_GROUPS, SSM_STATE, SSM_GROUP), f32) * b_scale
    c_scale = (2.0 * SSM_STATE) ** -0.5
    c_re = jax.random.normal(ks[9], (DEPTH, SSM_GROUPS, SSM_GROUP, SSM_STATE), f32) * c_scale
    c_im = jax.random.normal(ks[10], (DEPTH, SSM_GROUPS, SSM_GROUP, SSM_STATE), f32) * c_scale
    d_skip = jax.random.normal(ks[11], (DEPTH, SSM_WIDTH), f32)
    w_glu = jax.random.normal(ks[12], (DEPTH, SSM_WIDTH, SSM_WIDTH), f32) * SSM_WIDTH ** -0.5
    q_norm_w = 1.0 + 0.02 * jax.random.normal(ks[13], (DEPTH, N_DIL, HEAD_DIM), f32)
    k_norm_w = 1.0 + 0.02 * jax.random.normal(ks[14], (DEPTH, N_DIL, HEAD_DIM), f32)
    w_ssm_out = jax.random.normal(ks[15], (DEPTH, SSM_WIDTH, D_MODEL), f32) * SSM_WIDTH ** -0.5
    w_attn_out = jax.random.normal(ks[16], (DEPTH, ATTN_WIDTH, D_MODEL), f32) * ATTN_WIDTH ** -0.5
    w_o = jax.random.normal(ks[17], (DEPTH, D_MODEL, D_MODEL), f32) * D_MODEL ** -0.5
    return {"x": x, "positions": positions, "norm_w": norm_w, "w_in": w_in,
            "lam_re": lam_re, "lam_im": lam_im, "log_dt": log_dt,
            "b_re": b_re, "b_im": b_im, "c_re": c_re, "c_im": c_im,
            "d_skip": d_skip, "w_glu": w_glu, "q_norm_w": q_norm_w, "k_norm_w": k_norm_w,
            "w_ssm_out": w_ssm_out, "w_attn_out": w_attn_out, "w_o": w_o}

def second_block(x, positions, norm_w, w_in, lam_re, lam_im, log_dt, b_re, b_im, c_re, c_im,
              d_skip, w_glu, q_norm_w, k_norm_w, w_ssm_out, w_attn_out, w_o):
    f32 = jnp.float32
    bsz, length, _ = x.shape
    offsets = np.cumsum(SPLITS)[:-1].tolist()
    for layer in range(DEPTH):
        h = rms_norm_2(x, norm_w[layer])
        proj = h @ w_in[layer].astype(f32)
        u_s, z_s, q, k, v, z_a, r_s, r_a = jnp.split(proj, offsets, axis=-1)

        y_s = s5_branch(u_s, lam_re[layer], lam_im[layer], log_dt[layer], b_re[layer], b_im[layer],
                        c_re[layer], c_im[layer], d_skip[layer], w_glu[layer])
        y_s = (y_s * jax.nn.silu(z_s)) @ w_ssm_out[layer].astype(f32)

        head_shape = (bsz, length, N_DIL, HEADS_PER_GROUP, HEAD_DIM)
        q = rms_norm_2(q.reshape(head_shape), q_norm_w[layer][None, None, :, None, :])
        k = rms_norm_2(k.reshape(head_shape), k_norm_w[layer][None, None, :, None, :])
        v = v.reshape(head_shape)
        q = apply_partial_rope(q, positions)
        k = apply_partial_rope(k, positions)
        y_a = dilated_attention(q, k, v)
        y_a = (y_a * jax.nn.silu(z_a)) @ w_attn_out[layer].astype(f32)

        m = jax.nn.sigmoid(r_s) * y_s + jax.nn.sigmoid(r_a) * y_a
        x = (x.astype(f32) + m @ w_o[layer].astype(f32)).astype(x.dtype)
    return x


def setup_inputs(seed=0):
    out = dict(first_inputs(seed))
    for name, value in second_inputs(seed + 1).items():
        if name != "x":
            out[name + "_2"] = value
    return out


def reference(
    x, mem, positions, g_mix, w_in, b_gate, g_ckv, w_ukv, g_q_nope, g_k_nope, g_q_rope,
    g_k_rope, w_gla_gate, b_gla_gate, g_gla_out, g_mem, w_mem_kv, g_q_mem, g_k_mem, w_o, g_ffn,
    w_up, w_down, positions_2, norm_w_2, w_in_2, lam_re_2, lam_im_2, log_dt_2, b_re_2, b_im_2,
    c_re_2, c_im_2, d_skip_2, w_glu_2, q_norm_w_2, k_norm_w_2, w_ssm_out_2, w_attn_out_2, w_o_2,
):
    x = first_block(
        x, mem, positions, g_mix, w_in, b_gate, g_ckv, w_ukv, g_q_nope, g_k_nope, g_q_rope,
        g_k_rope, w_gla_gate, b_gla_gate, g_gla_out, g_mem, w_mem_kv, g_q_mem, g_k_mem, w_o,
        g_ffn, w_up, w_down,
    )
    return second_block(
        x, positions_2, norm_w_2, w_in_2, lam_re_2, lam_im_2, log_dt_2, b_re_2, b_im_2, c_re_2,
        c_im_2, d_skip_2, w_glu_2, q_norm_w_2, k_norm_w_2, w_ssm_out_2, w_attn_out_2, w_o_2,
    )


_drawn_inputs = setup_inputs


def setup_inputs(seed=0):
    import zlib

    import numpy as np

    out = dict(_drawn_inputs(seed))
    spreads = {}
    factors = {'g_mix': 4.056,
     'b_gate': 8.0,
     'g_ckv': 8.0,
     'g_q_nope': 8.0,
     'g_k_nope': 8.0,
     'g_q_rope': 8.0,
     'g_k_rope': 8.0,
     'b_gla_gate': 8.0,
     'g_gla_out': 8.0,
     'g_mem': 8.0,
     'g_q_mem': 8.0,
     'g_k_mem': 8.0,
     'g_ffn': 3.342,
     'norm_w_2': 8.0,
     'lam_re_2': 64.0,
     'lam_im_2': 64.0,
     'log_dt_2': 64.0,
     'b_re_2': 64.0,
     'b_im_2': 64.0,
     'c_re_2': 64.0,
     'c_im_2': 64.0,
     'q_norm_w_2': 8.0,
     'k_norm_w_2': 8.0}
    for name, (base, spread) in spreads.items():
        noise = np.random.default_rng([zlib.crc32(name.encode()), seed]).standard_normal(out[name].shape)
        drawn = base * np.exp(spread * noise) if base else spread * noise
        out[name] = __import__('jax').numpy.asarray(drawn.astype(out[name].dtype))
    for name, factor in factors.items():
        out[name] = (out[name] * factor).astype(out[name].dtype)
    return out
```

```python
from contextlib import ExitStack

import concourse.bass as bass
from concourse import mybir
import numpy as np

F32 = mybir.dt.float32
I32 = mybir.dt.int32
ACT = mybir.ActivationFunctionType
ALU = mybir.AluOpType
AX = mybir.AxisListType

P = 128
SEQ = 256
TT = SEQ // P
DM = 1024
KD = DM // P
EPS = 1e-6

MH, NOPE, ROPE, DV = 8, 128, 64, 128
QW = NOPE + ROPE
RANK = 256
GH, GK, GV, GR = 4, 128, 256, 16
EH, EQ, EV = 4, 64, 256
FF = 4 * DM
C_Q = 0
C_CKV = MH * QW
C_GQ = C_CKV + RANK + ROPE
C_GK = C_GQ + GH * GK
C_GV = C_GK + GH * GK
C_GA = C_GV + GH * GV
C_GR = C_GA + GR
C_MQ = C_GR + GH * GV
C_GATE = C_MQ + EH * EQ

SG, SP_, SN = 64, 16, 64
ST = SG // 2
CH = 128
NDIL, DH, DD = 3, 8, 64
DW = DH * DD
RD = DD // 4
C_US = 0
C_ZS = DM
C_DQ = 2 * DM
C_DK = C_DQ + NDIL * DW
C_DVV = C_DK + NDIL * DW
C_ZA = C_DVV + NDIL * DW
C_RS = C_ZA + DW
C_RA = C_RS + DM

RING = 3
NEG = -1e30
ROUND = 12582912.0
TWO_PI_A = 6.28125
TWO_PI_B = 0.0019350051879882812
TWO_PI_C = 3.019916e-07
PI_IN = 3.1415925

COLS = {}
for _name, _n in (("g_mix", 8), ("g_mem", 8), ("g_ffn", 8), ("norm_w_2", 8), ("g_ckv", 2), ("g_q_nope", 1),
                  ("g_k_nope", 1), ("b_gla_gate", 4), ("d_skip_2", 8)):
    COLS[_name] = (sum(n for _, n in COLS.values()), _n)
NCOLS = sum(n for _, n in COLS.values())

GAINS = (("g_q_rope", 64), ("g_k_rope", 64), ("g_q_mem", 64), ("g_k_mem", 64), ("g_gla_out", 256),
         ("q_norm_w_2", 192), ("k_norm_w_2", 192))
LEVELS = (64, 32, 16, 8, 4, 2, 1)
T_LANE = 44
T_C = T_LANE + 8


def jobs_table():
    j = [("ckv", "w_in", C_CKV, RANK + ROPE), ("gq", "w_in", C_GQ, 512), ("gk", "w_in", C_GK, 512),
         ("ga", "w_in", C_GA, GR), ("gg", None, 0, 0)]
    j += [(f"q{i}", "w_in", C_Q + 512 * i, 512) for i in range(3)]
    j += [(f"kv{i}", "w_ukv", 512 * i, 512) for i in range(4)]
    j += [(f"gv{i}", "w_in", C_GV + 512 * i, 512) for i in range(2)]
    j += [(f"gr{i}", "w_in", C_GR + 512 * i, 512) for i in range(2)]
    j += [("mq", "w_in", C_MQ, 256), ("mk", "w_mem_kv", 0, 256)]
    j += [(f"mv{i}", "w_mem_kv", 256 + 512 * i, 512) for i in range(2)]
    j += [(f"gate{i}", "w_in", C_GATE + 512 * i, 512) for i in (0, 1, 4, 5, 2, 3)]
    j += [(f"wo{i}", "w_o", 512 * i, 512) for i in range(2)]
    out = [(n, n, w, 0, RANK if w == "w_ukv" else DM, c, m) for n, w, c, m in j]
    out += [(f"up{i}", f"up{i}", "w_up", 0, DM, 512 * i, 512) for i in range(8)]
    out += [(f"down{h}{k}", f"down{h}", "w_down", DM * k, DM, 512 * h, 512) for h in range(2) for k in range(4)]
    j = [(f"us{i}", "w_in_2", C_US + 512 * i, 512) for i in range(2)]
    j += [(f"dv{g}", "w_in_2", C_DVV + DW * g, DW) for g in range(NDIL)]
    j += [(f"zs{i}", "w_in_2", C_ZS + 512 * i, 512) for i in range(2)]
    j += [("za", "w_in_2", C_ZA, DW)]
    j += [(f"dq{g}", "w_in_2", C_DQ + DW * g, DW) for g in range(NDIL)]
    j += [(f"dk{g}", "w_in_2", C_DK + DW * g, DW) for g in range(NDIL)]
    j += [(f"rs{i}", "w_in_2", C_RS + 512 * i, 512) for i in range(2)]
    j += [(f"ra{i}", "w_in_2", C_RA + 512 * i, 512) for i in range(2)]
    j += [(f"glu{i}", "w_glu_2", 512 * i, 512) for i in range(2)]
    j += [(f"so{i}", "w_ssm_out_2", 512 * i, 512) for i in range(2)]
    j += [(f"ao{i}", "w_attn_out_2", 512 * i, 512) for i in range(2)]
    j += [(f"wp{i}", "w_o_2", 512 * i, 512) for i in range(2)]
    out += [(n, n, w, 0, DW if w == "w_attn_out_2" else DM, c, m) for n, w, c, m in j]
    return out


JOBS = jobs_table()
JOB = {job[0]: n for n, job in enumerate(JOBS)}
OUTS = list(dict.fromkeys(job[1] for job in JOBS))
LAST_JOB = {job[1]: n for n, job in enumerate(JOBS)}
BY_DVE = {"gg", "wo0", "wo1", "down0", "down1", "so0", "so1", "ao0", "ao1", "wp0", "wp1"} | {f"gate{i}" for i in range(6)}
CHANNEL_MAJOR = {"gq", "gk", "ga", "us0", "us1", "zs0", "zs1", "glu0", "glu1"} | {f"up{i}" for i in range(8)}
STREAMED = [n for n, job in enumerate(JOBS) if job[2]]
GATES = (0, 1, 4, 5, 2, 3)


def taken(name):
    by = "dve" if name in BY_DVE else "act"
    return by, sum((o in BY_DVE) == (name in BY_DVE) for o in OUTS[:OUTS.index(name) + 1])


def build(nc, d, out):
    with ExitStack() as ctx:
        def sb(name, shape, dt=F32):
            return ctx.enter_context(nc.sbuf_tensor(name, shape, dt))

        sems = {}

        def sem(name):
            if name not in sems:
                sems[name] = ctx.enter_context(nc.semaphore(name))
            return sems[name]

        ident = sb("ident", [P, P])
        masks = sb("masks", [P, 1 + NDIL, SEQ])
        pcol = sb("pcol", [P, NCOLS])
        prow = sb("prow", [NCOLS, P])
        inv = sb("inv", [P, 40])
        ring = sb("ring", [P, RING, KD * 512])
        hT = sb("hT", [P, KD, SEQ])
        xres = sb("xres", [P, TT, DM])
        st = sb("stats", [P, 400])
        gains = sb("gains", [P, sum(w for _, w in GAINS)])
        rope = sb("rope", [P, 2, TT, 40])
        posi = sb("posi", [P, 2 * TT], I32)
        posf = sb("posf", [P, 2 * TT])
        carry = sb("carry", [P, 4])
        AR = 33700
        arena = sb("arena", [P, AR])

        gain, at = {}, 0
        for name, w in GAINS:
            gain[name] = gains[:, at:at + w]
            at += w

        def col(name, i=0, n=1):
            a = COLS[name][0] + i
            return pcol[:, a:a + n]

        class Place:
            def __init__(self, at=0):
                self.at = at

            def __call__(self, n):
                a = self.at
                self.at += n
                assert self.at <= AR, self.at
                return arena[:, a:a + n]

        a1 = Place()
        mem_tok = a1(2048); o_mla = mem_tok
        memT = a1(2048)
        q_tok = a1(3072)
        vg, mq_tok, mk_tok = q_tok[:, 0:2048], q_tok[:, 2048:2560], q_tok[:, 2560:3072]
        kv_tok = a1(4096)
        vm, gate_buf = kv_tok[:, 0:2048], kv_tok[:, 2048:4096]
        qnT = a1(2048); o_gla = qnT
        qpT = a1(1024)
        kmT, qmT = qpT[:, 0:512], qpT[:, 512:1024]
        knT = a1(2048); o_mem = knT
        kpeT = a1(256)
        kpe = a1(256)
        ckv = a1(640)
        ckvT = a1(512)
        qgT, kgT, bT, dec = a1(1024), a1(1024), a1(1024), a1(1024)
        qdec, kdec = a1(1024), a1(1024)
        amat = a1(1024); qpe = amat
        across = a1(512)
        r_gla = a1(2048); xn1 = r_gla
        soft = a1(1024)
        softT = a1(1024)
        aT = a1(256)
        wgate = a1(512)
        junk = a1(1024)

        levels = a1(1024)
        bgate = a1(1024)

        a2 = Place()
        cs = a2(ST * 2 * CH)
        bt = a2(2048)
        cc = a2(2048)
        lane = a2(288)
        p2 = a2.at
        hup = a2(8192)
        xn2 = a2(2048)
        bnat = a2(1024)
        bexp = a2(2048)
        cnat = a2(2048)
        srow = a2(1536)
        tmp_cs = a2(4096)

        a3 = Place(p2)
        uT = a3(2048)
        zs = a3(2048); xn3 = zs
        za = a3(1024)
        vd = a3(3072)
        qdT = a3(3072)
        kdT = a3(3072)
        raw = a3(1024)
        raw2 = a3(1024)
        wrot = a3(1024)
        gst = a3(1024)
        hrot = a3(1024)
        hst = a3(1536)
        a4 = Place()
        dsoft = a4(2304)
        dsoftT = a4(2304)
        ya = a4(1024)
        gz = a4(2048)
        sig_glu = a4(2048); yssT = sig_glu
        yaT = a4(1024)
        assert a4.at <= p2
        a5 = Place(a3.at - 6656)
        m_tok, rsig, asig = a5(2048), a5(2048), a5(2048)

        lam = {}
        for i, name in enumerate(("cos", "sin", "mag", "fre", "fim", "ere", "eim", "sq", "sq2")):
            lam[name] = lane[:, 32 * i:32 * i + 32]

        pair = [ctx.enter_context(nc.psum_tensor(f"pair{i}", [P, 1024], F32)) for i in range(2)]
        bank = {k: [ctx.enter_context(nc.psum_tensor(f"{k}{i}", [P, 512], F32)) for i in range(2)]
                for k in ("turned", "score")}

        block = ctx.enter_context(nc.Block())
        small = {}

        @block.sync
        def _(sp):
            for t in range(TT):
                sp.dma_start(xres[:, t, :], d["x"][0, P * t:P * t + P, :]).then_inc(sem("x_in"), 16)
            for n, j in enumerate(STREAMED):
                name, _, w, r0, rows, c0, cols = JOBS[j]
                slot = n % RING
                if n >= RING:
                    sp.wait_ge(sem("job_done"), STREAMED[n - RING] + 1)
                dst = ring[:, slot, 0:rows // P * cols].rearrange("p (k n) -> p k n", n=cols)
                src = d[w][0, r0:r0 + rows, c0:c0 + cols].rearrange("(k p) n -> p k n", p=P)
                sp.dma_start(dst, src).then_inc(sem(f"weights{slot}"), 16)
            for i in range(2):
                sp.wait_ge(sem("taken_dve"), taken(f"wp{i}")[1])
                for t in range(TT):
                    sp.dma_start(out[0, P * t:P * t + P, 512 * i:512 * i + 512],
                                 xres[:, t, 512 * i:512 * i + 512]).then_inc(sem("stored"), 16)
            sp.wait_ge(sem("stored"), 64)

        @block.gpsimd
        def _(pool):
            count = [0]

            def link(ins):
                count[0] += 1
                ins.then_inc(sem("pool_step"), 1)
                pool.wait_ge(sem("pool_step"), count[0])

            pool.dma_start(ident[:, :], d["c_ident"]).then_inc(sem("ident_in"), 16)
            for name, (a, n) in COLS.items():
                pool.dma_start(prow[a:a + n, :], d[name].rearrange("o (a b) -> (o a) b", b=P)).then_inc(sem("rows_in"), 16)
            pool.dma_start(masks[:, :, :], d["c_masks"]).then_inc(sem("consts_in"), 16)
            pool.dma_start(levels.rearrange("p (l n) -> p l n", n=P), d["c_levels"]).then_inc(sem("consts_in"), 16)
            pool.dma_start(inv[:, :], d["c_inv"]).then_inc(sem("consts_in"), 16)
            for i, name in enumerate(("positions", "positions_2")):
                for t in range(TT):
                    pool.dma_start(posi[:, TT * i + t:TT * i + t + 1],
                                   d[name][:, P * t:P * t + P].rearrange("o (p a) -> (o p) a", a=1)).then_inc(sem("consts_in"), 16)
            pool.dma_start(wgate[0:GR, :], d["w_gla_gate"][0]).then_inc(sem("consts_in"), 16)
            for name, w in GAINS:
                src = d[name].rearrange("o a b -> o (a b)") if len(d[name].shape) == 3 else d[name]
                pool.dma_start(gain[name], src.to_broadcast([P, w])).then_inc(sem("consts_in"), 16)
            for n, i in enumerate(GATES):
                if n >= 2:
                    pool.wait_ge(sem("taken_dve"), taken(f"gate{GATES[n - 2]}")[1])
                pool.dma_start(bgate[:, 512 * (n % 2):512 * (n % 2) + 512],
                               d["b_gate"][:, 512 * i:512 * i + 512].to_broadcast([P, 512])).then_inc(sem(f"bgate{n % 2}"), 16)

            pool.wait_ge(sem("taken_dve"), taken("wo1")[1])
            link(pool.memset(bexp, 0.0))
            for i, name in enumerate(("b_re_2", "b_im_2")):
                pool.dma_start(bnat[:, 512 * i:512 * i + 512].rearrange("p (j c) -> p j c", c=SP_),
                               d[name][0].rearrange("(j a) n c -> (a n) j c", a=2)).then_inc(sem("ssm_in"), 16)
            for i, name in enumerate(("c_re_2", "c_im_2")):
                for half in range(2):
                    pool.dma_start(cnat[:, 1024 * i:1024 * i + 1024].rearrange("p (j h n) -> p j h n", h=2, n=SN)[:, :, half, :],
                                   d[name][0].rearrange("(j g) c n -> (g c) j n", g=8)).then_inc(sem("ssm_in"), 16)
            pool.dma_start(srow[0:ST, 0:128], d["lam_re_2"][0].rearrange("(j a) n -> j (a n)", a=2)).then_inc(sem("ssm_in"), 16)
            pool.dma_start(srow[0:ST, 128:256], d["lam_im_2"][0].rearrange("(j a) n -> j (a n)", a=2)).then_inc(sem("ssm_in"), 16)
            pool.dma_start(srow[0:ST, 256:258], d["log_dt_2"][0:1, :].rearrange("o (j a) -> (o j) a", a=2)).then_inc(sem("ssm_in"), 16)
            pool.wait_ge(sem("ssm_in"), 16 * 9)
            for i in range(2):
                for a in range(2):
                    last = pool.tensor_copy(
                        bexp[64 * a:64 * a + 64, 1024 * i:1024 * i + 1024].rearrange("p (j h c) -> p j h c", h=2, c=SP_)[:, :, a, :],
                        bnat[64 * a:64 * a + 64, 512 * i:512 * i + 512].rearrange("p (j c) -> p j c", c=SP_))
                    last.then_inc(sem("bexp_ready"), 1)

            for j in range(ST):
                pool.wait_ge(sem("g_ready"), j + 1)
                g = gst[:, 512 * (j % 2):512 * (j % 2) + 512]
                gv = g.rearrange("p (c t) -> p c t", t=CH)
                tab = cs.rearrange("p (j r t) -> p j r t", r=2, t=CH)[:, j]
                n1, n2 = hrot[:, 0:512], hrot[:, 512:1024]
                h = hst[:, 512 * (j % 3):512 * (j % 3) + 512]
                pool.tensor_tensor(n1.rearrange("p (c t) -> p c t", t=CH), gv,
                                   tab[:, 0:1, :].to_broadcast([P, 4, CH]), ALU.mult).then_inc(sem("pool_step"), 1)
                pool.tensor_tensor(n2.rearrange("p (c t) -> p c t", t=CH), gv,
                                   tab[:, 1:2, :].to_broadcast([P, 4, CH]), ALU.mult).then_inc(sem("pool_step"), 1)
                count[0] += 2
                pool.wait_ge(sem("pool_step"), count[0])
                pool.tensor_tensor(h[:, 0:256], n1[:, 0:256], n2[:, 256:512], ALU.subtract).then_inc(sem("h_ready"), 1)
                pool.tensor_tensor(h[:, 256:512], n1[:, 256:512], n2[:, 0:256], ALU.add).then_inc(sem("h_ready"), 1)
                pool.wait_ge(sem("h_ready"), 2 * j + 2)

        @block.scalar
        def _(act):
            n_out, n_turn, count = [0], [0], [0]

            def link(ins):
                count[0] += 1
                ins.then_inc(sem("act_step"), 1)
                act.wait_ge(sem("act_step"), count[0])

            def arrived(name):
                act.wait_ge(sem("job_done"), LAST_JOB[name] + 1)
                return pair[OUTS.index(name) % 2]

            def take(name, dst, func=ACT.Copy, scale=1.0, cols=512):
                p = arrived(name)
                for t in range(TT):
                    ins = act.activation(dst(t), p[:, 512 * t:512 * t + cols], func, scale=scale)
                ins.then_inc(sem("taken_act"), 1)

            def turned(dst, n, scale=None, rows=P):
                i = n_turn[0]
                n_turn[0] += 1
                act.wait_ge(sem("turned_ready"), i + 1)
                src = bank["turned"][i % 2][0:rows, 0:n]
                if scale is None:
                    act.activation(dst, src, ACT.Copy).then_inc(sem("turned_taken"), 1)
                else:
                    w = n // len(scale)
                    for k, s in enumerate(scale):
                        ins = act.activation(dst[:, w * k:w * k + w], src[:, w * k:w * k + w], ACT.Copy, scale=s)
                    ins.then_inc(sem("turned_taken"), 1)

            def root(lo, n, name):
                act.wait_ge(sem(name + "_var"), root.seen.setdefault(name, 0) + 1)
                root.seen[name] += 1
                link(act.activation(st[:, lo + n:lo + 2 * n], st[:, lo:lo + n], ACT.Ln))
                act.activation(st[:, lo + n:lo + 2 * n], st[:, lo + n:lo + 2 * n], ACT.Exp, scale=-0.5).then_inc(sem(name + "_guess"), 1)
            root.seen = {}

            act.dma_start(mem_tok.rearrange("p (t c) -> p t c", c=DM), d["mem"][0].rearrange("(t p) c -> p t c", p=P)).then_inc(sem("mem_in"), 16)

            def squares(src, lo, name, sink):
                for t in range(TT):
                    ins = act.activation(sink[t], src(t), ACT.Square, accum_out=st[:, lo + t:lo + t + 1])
                    ins.then_inc(sem(name), 1)

            act.wait_ge(sem("x_in"), 32)
            squares(lambda t: xres[:, t, :], 280, "x_ss", (junk, qpe))
            root(0, 2, "x")
            turned(pcol[:, :], NCOLS)
            act.wait_ge(sem("turned_taken"), 1)
            hflat = hT[:, :, :].rearrange("p k s -> p (k s)")
            for g in range(4):
                turned(hflat[:, 512 * g:512 * g + 512], 512, [col("g_mix", 2 * g), col("g_mix", 2 * g + 1)])
            act.wait_ge(sem("mem_in"), 16)
            squares(lambda t: mem_tok[:, DM * t:DM * t + DM], 282, "mem_ss", (junk, qpe))
            act.wait_ge(sem("angle"), 1)
            link(act.activation(rope[:, 1, :, :], rope[:, 1, :, :], ACT.Sin))
            act.activation(rope[:, 0, :, :], rope[:, 0, :, :], ACT.Sin).then_inc(sem("rope_ready"), 1)
            root(4, 2, "mem")
            ck = ckv.rearrange("p (t c) -> p t c", c=RANK + ROPE)
            take("ckv", lambda t: ck[:, t, :], cols=RANK + ROPE)
            for g in range(4):
                turned(memT[:, 512 * g:512 * g + 512], 512, [col("g_mem", 2 * g), col("g_mem", 2 * g + 1)])
            take("gq", lambda t: qgT[:, 512 * t:512 * t + 512], scale=GK ** -0.5)
            take("gk", lambda t: kgT[:, 512 * t:512 * t + 512])
            p = arrived("ga")
            act.activation(aT[0:GR, :], p[0:GR, 0:SEQ], ACT.Copy).then_inc(sem("taken_act"), 1)
            root(8, 4, "ckv")
            turned(ckvT, 512, [col("g_ckv", 0), col("g_ckv", 1)])
            turned(kpeT, 256)
            act.wait_ge(sem("taken_dve"), taken("gg")[1])
            link(act.activation(dec, bT, ACT.Abs))
            link(act.activation(dec, dec, ACT.Exp, scale=-1.0))
            act.activation(dec, dec, ACT.Ln, bias=1.0).then_inc(sem("gate_ln"), 1)
            q3 = q_tok.rearrange("p (t c) -> p t c", c=MH * QW)
            for i in range(3):
                take(f"q{i}", lambda t: q3[:, t, 512 * i:512 * i + 512])
            k3 = kv_tok.rearrange("p (t c) -> p t c", c=MH * (NOPE + DV))
            for i in range(4):
                take(f"kv{i}", lambda t: k3[:, t, 512 * i:512 * i + 512])
            root(16, 32, "q")
            for g in range(4):
                turned(qnT[:, 512 * g:512 * g + 512], 512, [col("g_q_nope")])
            for g in range(2):
                turned(qpT[:, 512 * g:512 * g + 512], 512)
            root(80, 16, "k")
            for g in range(4):
                turned(knT[:, 512 * g:512 * g + 512], 512, [col("g_k_nope")])

            vg3 = vg.rearrange("p (t c) -> p t c", c=DM)
            rg3 = r_gla.rearrange("p (t c) -> p t c", c=DM)

            def exps(tag, n, parts):
                act.wait_ge(sem(tag + "_scores"), n + 1)
                for k, (a, w, t) in enumerate(parts):
                    s = (soft if tag != "dil" else dsoft)
                    half = (512 if tag != "dil" else 1152) * (n % 2)
                    ins = act.activation(s[:, half + a:half + a + w], s[:, half + a:half + a + w], ACT.Exp,
                                         bias=st[:, 340 + 2 * (n % 4) + t:341 + 2 * (n % 4) + t],
                                         accum_out=st[:, 350 + 2 * (n % 4) + t:351 + 2 * (n % 4) + t])
                ins.then_inc(sem(tag + "_exp"), 1)

            for h in range(MH + 2):
                if h in (1, 3):
                    i = (h - 1) // 2
                    take(f"gv{i}", lambda t: vg3[:, t, 512 * i:512 * i + 512])
                if h in (5, 7):
                    i = (h - 5) // 2
                    take(f"gr{i}", lambda t: rg3[:, t, 512 * i:512 * i + 512])
                if h < MH:
                    exps("mla", h, ((0, 128, 0), (128, 256, 1)))
                if 1 <= h <= MH:
                    turned(softT[:, 512 * ((h - 1) % 2):512 * ((h - 1) % 2) + 384], 384)
            mq3 = mq_tok.rearrange("p (t c) -> p t c", c=EH * EQ)
            mk3 = mk_tok.rearrange("p (t c) -> p t c", c=EH * EQ)
            take("mq", lambda t: mq3[:, t, :], cols=256)
            take("mk", lambda t: mk3[:, t, :], cols=256)
            root(144, 16, "m")
            for t in range(TT):
                if t:
                    act.wait_ge(sem("silu_done"), t)
                act.activation(junk, rg3[:, t, :], ACT.Sigmoid).then_inc(sem("silu_sig"), 1)
            turned(qmT, 512)
            turned(kmT, 512)
            vm3 = vm.rearrange("p (t c) -> p t c", c=DM)
            take("mv0", lambda t: vm3[:, t, 0:512])

            def gate_sigmoid(n):
                act.wait_ge(sem("taken_dve"), taken(f"gate{GATES[n]}")[1])
                g = gate_buf[:, 1024 * (n % 2):1024 * (n % 2) + 1024]
                act.activation(g, g, ACT.Sigmoid).then_inc(sem("gate_sig"), 1)

            def level_exp(lv):
                act.wait_ge(sem("level_diff"), lv + 1)
                act.activation(dec, dec, ACT.Exp, scale=1.0 / 16.0).then_inc(sem("level_exp"), 1)

            for i in range(9):
                if i < 8:
                    level_exp(i)
                if i == 2:
                    take("mv1", lambda t: vm3[:, t, 512:1024])
                if i < EH:
                    exps("mem", i, ((0, 256, 0), (256, 256, 1)))
                if 1 <= i <= EH:
                    turned(softT[:, 512 * ((i - 1) % 2):512 * ((i - 1) % 2) + 512], 512)
                if i in (4, 6, 8):
                    gate_sigmoid((i - 4) // 2)
            root(176, 8, "og")
            gate_sigmoid(3)
            gate_sigmoid(4)
            gate_sigmoid(5)
            for g in range(4):
                turned(hflat[:, 512 * g:512 * g + 512], 512)

            act.wait_ge(sem("taken_dve"), taken("wo1")[1])
            squares(lambda t: xres[:, t, :], 280, "x_ss", (hup[:, 0:1024], hup[:, 1024:2048]))
            root(0, 2, "x")
            for g in range(4):
                turned(hflat[:, 512 * g:512 * g + 512], 512, [col("g_ffn", 2 * g), col("g_ffn", 2 * g + 1)])

            R = srow[0:ST, :].rearrange("p (k n) -> p k n", n=128)
            for i in range(8):
                take(f"up{i}", lambda t: hup[:, 1024 * i + 512 * t:1024 * i + 512 * t + 512], func=ACT.Relu)
                if i == 0:
                    act.wait_ge(sem("ssm_in"), 16 * 9)
                    act.activation(srow[0:ST, 258:260], srow[0:ST, 256:258], ACT.Exp).then_inc(sem("dt_ready"), 1)
                    act.wait_ge(sem("theta"), 1)
                    link(act.activation(R[:, 3, :], R[:, 3, :], ACT.Exp))
                    link(act.activation(R[:, 5, :], R[:, 5, :], ACT.Sin))
                    act.activation(R[:, 4, :], R[:, 4, :], ACT.Sin).then_inc(sem("trig"), 1)
                if i == 2:
                    turned(lane[:, 0:160], 160)
                if i == 4:
                    for k in range(4):
                        turned(bt[:, 512 * k:512 * k + 512], 512)
            act.wait_ge(sem("tables"), 1)
            for k in range(4):
                turned(tmp_cs[:, 512 * k:512 * k + 512], 512)

            act.wait_ge(sem("taken_dve"), taken("down1")[1])
            squares(lambda t: xres[:, t, :], 280, "x_ss", (raw, raw2))
            root(0, 2, "x")
            for g in range(4):
                turned(hflat[:, 512 * g:512 * g + 512], 512, [col("norm_w_2", 2 * g), col("norm_w_2", 2 * g + 1)])
            for i in range(2):
                take(f"us{i}", lambda t: uT[:, 1024 * i + 512 * t:1024 * i + 512 * t + 512])
            vd4 = vd.rearrange("p (g t c) -> p g t c", g=NDIL, t=TT)
            for g in range(NDIL):
                take(f"dv{g}", lambda t: vd4[:, g, t, :])
            for i in range(2):
                if i == 1:
                    act.wait_ge(sem("z_silu"), 1)
                p = arrived(f"zs{i}")
                for t in range(2):
                    act.activation(zs[:, 1024 * i + 512 * t:1024 * i + 512 * t + 512], p[:, 512 * t:512 * t + 512], ACT.Copy)
                for t in range(2):
                    ins = act.activation(raw[:, 512 * t:512 * t + 512], p[:, 512 * t:512 * t + 512], ACT.Sigmoid)
                ins.then_inc(sem("taken_act"), 1)
            act.wait_ge(sem("z_silu"), 2)
            p = arrived("za")
            za3 = za.rearrange("p (t c) -> p t c", c=DW)
            for t in range(2):
                act.activation(za3[:, t, :], p[:, 512 * t:512 * t + 512], ACT.Copy)
            for t in range(2):
                ins = act.activation(raw[:, 512 * t:512 * t + 512], p[:, 512 * t:512 * t + 512], ACT.Sigmoid)
            ins.then_inc(sem("taken_act"), 1)
            for n in range(6):
                name = f"dq{n}" if n < 3 else f"dk{n - 3}"
                act.wait_ge(sem("z_silu"), 3)
                if n:
                    for _k in range(2):
                        turned((qdT if n - 1 < 3 else kdT)[:, 1024 * ((n - 1) % 3) + 512 * _k:1024 * ((n - 1) % 3) + 512 * _k + 512], 512)
                p = arrived(name)
                for t in range(2):
                    act.activation(raw[:, 512 * t:512 * t + 512], p[:, 512 * t:512 * t + 512], ACT.Copy)
                for t in range(2):
                    ins = act.activation(raw2[:, 512 * t:512 * t + 512], p[:, 512 * t:512 * t + 512], ACT.Square)
                ins.then_inc(sem("taken_act"), 1)
                root(192, 16, "dqk")
                if n == 2:
                    for i in range(2):
                        act.wait_ge(sem("gelu_z"), i + 1)
                        act.activation(gz[:, 1024 * i:1024 * i + 1024], gz[:, 1024 * i:1024 * i + 1024], ACT.Sigmoid,
                                       scale=1.5957691216057308).then_inc(sem("gelu_sig"), 1)
            take("rs0", lambda t: rsig[:, DM * t:DM * t + 512], func=ACT.Sigmoid)
            for k in range(2):
                turned(kdT[:, 2048 + 512 * k:2048 + 512 * k + 512], 512)
            for h in range(DH + 2):
                if h == 2:
                    take("rs1", lambda t: rsig[:, DM * t + 512:DM * t + 1024], func=ACT.Sigmoid)
                if h in (4, 6):
                    i = (h - 4) // 2
                    take(f"ra{i}", lambda t: asig[:, DM * t + 512 * i:DM * t + 512 * i + 512], func=ACT.Sigmoid)
                if h == 8:
                    take("glu0", lambda t: sig_glu[:, 512 * t:512 * t + 512], func=ACT.Sigmoid)
                if h < DH:
                    exps("dil", h, ((0, 384, 0), (384, 768, 1)))
                if 1 <= h <= DH:
                    for g in range(NDIL):
                        b = 1152 * ((h - 1) % 2) + 384 * g
                        turned(dsoftT[:, b:b + 384], 384)
            take("glu1", lambda t: sig_glu[:, 1024 + 512 * t:1024 + 512 * t + 512], func=ACT.Sigmoid)
            for k in range(2):
                turned(yaT[:, 512 * k:512 * k + 512], 512)
            for g in range(4):
                turned(hflat[:, 512 * g:512 * g + 512], 512)

        @block.vector
        def _(dve):
            count, n_score, own = [0], [0], {}

            def link(ins):
                count[0] += 1
                ins.then_inc(sem("dve_step"), 1)
                dve.wait_ge(sem("dve_step"), count[0])

            def mark(ins, name):
                own[name] = own.get(name, 0) + 1
                ins.then_inc(sem(name), 1)
                dve.wait_ge(sem(name), own[name])

            def arrived(name):
                dve.wait_ge(sem("job_done"), LAST_JOB[name] + 1)
                return pair[OUTS.index(name) % 2]

            def scored():
                i = n_score[0]
                n_score[0] += 1
                dve.wait_ge(sem("score_ready"), i + 1)
                return bank["score"][i % 2]

            def tt(o, a, b, op):
                return dve.tensor_tensor(o, a, b, op)

            def bc(x, shape):
                return x.to_broadcast(shape)

            def newton(lo, n, name):
                own[name + "_g"] = own.get(name + "_g", 0) + 1
                dve.wait_ge(sem(name + "_guess"), own[name + "_g"])
                v, y, a = st[:, lo:lo + n], st[:, lo + n:lo + 2 * n], st[:, 300:300 + n]
                link(tt(a, y, y, ALU.mult))
                link(tt(a, a, v, ALU.mult))
                link(dve.tensor_scalar(a, a, -0.5, 1.5, ALU.mult, ALU.add))
                link(tt(y, y, a, ALU.mult))

            def var(dst, src, n, name=None):
                ins = dve.tensor_scalar(dst, src, 1.0 / n, EPS, ALU.mult, ALU.add)
                if name:
                    mark(ins, name + "_var")
                else:
                    link(ins)

            def rms_rows(src, dst, lo, ss, name, need):
                dve.wait_ge(sem(name + "_ss"), need)
                var(st[:, lo:lo + 2], st[:, ss:ss + 2], DM, name)
                newton(lo, 2, name)
                for t in range(TT):
                    mark(dve.tensor_scalar(dst(t), src(t), st[:, lo + 2 + t:lo + 3 + t], None, ALU.mult), name + "_rows")

            def reduce_angle(x, k, rows):
                link(dve.tensor_scalar(k, x, 1.0 / (2 * np.pi), ROUND, ALU.mult, ALU.add))
                link(dve.tensor_scalar(k, k, -ROUND, None, ALU.add))
                for part in (TWO_PI_A, TWO_PI_B, TWO_PI_C):
                    link(dve.scalar_tensor_tensor(x, k, -part, x, ALU.mult, ALU.add))
                link(dve.tensor_scalar(x, x, PI_IN, -PI_IN, ALU.min, ALU.max))
                link(dve.tensor_scalar(k, x, -1.0, None, ALU.mult))
                link(tt(k, k, x, ALU.min))
                return dve.tensor_scalar(k, k, np.pi / 2, None, ALU.add)

            link(dve.memset(st[:, 399:400], 1.0))
            rms_rows(lambda t: xres[:, t, :], lambda t: xn1[:, DM * t:DM * t + DM], 0, 280, "x", 2)
            dve.wait_ge(sem("consts_in"), 16 * (8 + len(GAINS)))
            link(dve.tensor_copy(posf[:, :], posi[:, :]))
            ang, turns = rope[:, 1, :, :], rope[:, 0, :, :]
            for t in range(TT):
                link(dve.tensor_scalar(ang[:, t, 0:32], inv[:, 0:32], posf[:, t:t + 1], None, ALU.mult))
                link(dve.tensor_scalar(ang[:, t, 32:40], inv[:, 32:40], posf[:, TT + t:TT + t + 1], None, ALU.mult))
            mark(reduce_angle(ang, turns, P), "angle")
            rms_rows(lambda t: mem_tok[:, DM * t:DM * t + DM], lambda t: mem_tok[:, DM * t:DM * t + DM], 4, 282, "mem", 2)

            dve.wait_ge(sem("taken_act"), taken("ckv")[1])
            ck = ckv.rearrange("p (t c) -> p t c", c=RANK + ROPE)
            for t in range(TT):
                link(tt(qdec[:, 0:320], ck[:, t, :], ck[:, t, :], ALU.mult))
                link(dve.tensor_reduce(st[:, 284 + t:285 + t], qdec[:, 0:RANK], AX.X, ALU.add))
                link(dve.tensor_reduce(st[:, 286 + t:287 + t], qdec[:, RANK:RANK + ROPE], AX.X, ALU.add))
            var(st[:, 8:10], st[:, 284:286], RANK)
            var(st[:, 10:12], st[:, 286:288], ROPE, "ckv")
            newton(8, 4, "ckv")
            for t in range(TT):
                mark(dve.tensor_scalar(ck[:, t, 0:RANK], ck[:, t, 0:RANK], st[:, 12 + t:13 + t], None, ALU.mult), "ckv_rows")
                link(dve.tensor_scalar(ck[:, t, RANK:RANK + ROPE], ck[:, t, RANK:RANK + ROPE], st[:, 14 + t:15 + t], None, ALU.mult))
            kr = ck[:, :, RANK:RANK + ROPE]
            link(tt(kr, kr, bc(gain["g_k_rope"].unsqueeze(1), [P, TT, ROPE]), ALU.mult))
            dve.wait_ge(sem("rope_ready"), 1)
            kp = kpe.rearrange("p (t c) -> p t c", c=2 * ROPE)
            cos_a, sin_a = rope[:, 0, :, 0:32], rope[:, 1, :, 0:32]
            tmp = [kdec[:, 64 * i:64 * i + 64].rearrange("p (t c) -> p t c", c=32) for i in range(4)]
            x1, x2 = kr[:, :, 0:32], kr[:, :, 32:64]
            link(tt(tmp[0], x1, cos_a, ALU.mult))
            link(tt(tmp[1], x2, sin_a, ALU.mult))
            link(tt(tmp[2], x1, sin_a, ALU.mult))
            link(tt(tmp[3], x2, cos_a, ALU.mult))
            for i in range(2):
                link(tt(kp[:, :, 64 * i:64 * i + 32], tmp[0], tmp[1], ALU.subtract))
                mark(tt(kp[:, :, 64 * i + 32:64 * i + 64], tmp[2], tmp[3], ALU.add), "kpe_rows")

            p = arrived("gg")
            b4 = bT.rearrange("p (h s) -> p h s", s=SEQ)
            for i in range(2):
                ins = tt(b4[:, 2 * i:2 * i + 2, :], p[:, 512 * i:512 * i + 512].rearrange("p (h s) -> p h s", s=SEQ),
                         bc(col("b_gla_gate", 2 * i, 2).unsqueeze(2), [P, 2, SEQ]), ALU.add)
            mark(ins, "taken_dve")
            dve.wait_ge(sem("gate_ln"), 1)
            link(dve.scalar_tensor_tensor(dec, bT, 0.0, dec, ALU.min, ALU.subtract))
            for i in range(2 * GH):
                link(dve.tensor_tensor_scan(bT[:, P * i:P * i + P], bc(st[:, 399:400], [P, P]), dec[:, P * i:P * i + P],
                                            0.0, ALU.mult, ALU.add))

            dve.wait_ge(sem("taken_act"), taken("q2")[1])
            for t in range(TT):
                qt = q_tok[:, MH * QW * t:MH * QW * (t + 1)]
                link(tt(knT[:, 0:1536], qt, qt, ALU.mult))
                s3 = knT[:, 0:1536].rearrange("p (h c) -> p h c", c=QW)
                link(dve.tensor_reduce(st[:, 16 + 8 * t:24 + 8 * t], s3[:, :, 0:NOPE], AX.X, ALU.add))
                link(dve.tensor_reduce(st[:, 32 + 8 * t:40 + 8 * t], s3[:, :, NOPE:QW], AX.X, ALU.add))
            var(st[:, 16:32], st[:, 16:32], NOPE)
            var(st[:, 32:48], st[:, 32:48], ROPE, "q")
            newton(16, 32, "q")
            q16 = q_tok.rearrange("p (g c) -> p g c", c=QW)
            mark(tt(q16[:, :, 0:NOPE], q16[:, :, 0:NOPE], bc(st[:, 48:64].unsqueeze(2), [P, 16, NOPE]), ALU.mult), "q_rows")
            link(tt(q16[:, :, NOPE:QW], q16[:, :, NOPE:QW], bc(st[:, 64:80].unsqueeze(2), [P, 16, ROPE]), ALU.mult))
            link(tt(q16[:, :, NOPE:QW], q16[:, :, NOPE:QW], bc(gain["g_q_rope"].unsqueeze(1), [P, 16, ROPE]), ALU.mult))
            q4 = q_tok.rearrange("p (t h c) -> p t h c", t=TT, c=QW)
            x1, x2 = q4[:, :, :, NOPE:NOPE + 32], q4[:, :, :, NOPE + 32:QW]
            cosb = bc(cos_a.unsqueeze(2), [P, TT, MH, 32])
            sinb = bc(sin_a.unsqueeze(2), [P, TT, MH, 32])
            tmp = [(qdec, kdec)[i // 2][:, 512 * (i % 2):512 * (i % 2) + 512].rearrange("p (t h c) -> p t h c", t=TT, c=32)
                   for i in range(4)]
            link(tt(tmp[0], x1, cosb, ALU.mult))
            link(tt(tmp[1], x2, sinb, ALU.mult))
            link(tt(tmp[2], x1, sinb, ALU.mult))
            link(tt(tmp[3], x2, cosb, ALU.mult))
            qp4 = qpe.rearrange("p (t h c) -> p t h c", t=TT, c=ROPE)
            link(tt(qp4[:, :, :, 0:32], tmp[0], tmp[1], ALU.subtract))
            mark(tt(qp4[:, :, :, 32:64], tmp[2], tmp[3], ALU.add), "qpe_rows")

            dve.wait_ge(sem("taken_act"), taken("kv3")[1])
            k16 = kv_tok.rearrange("p (g c) -> p g c", c=NOPE + DV)
            kn = k16[:, :, 0:NOPE]
            link(tt(knT.rearrange("p (g c) -> p g c", c=NOPE), kn, kn, ALU.mult))
            link(dve.tensor_reduce(st[:, 80:96], knT.rearrange("p (g c) -> p g c", c=NOPE), AX.X, ALU.add))
            var(st[:, 80:96], st[:, 80:96], NOPE, "k")
            newton(80, 16, "k")
            mark(tt(kn, kn, bc(st[:, 96:112].unsqueeze(2), [P, 16, NOPE]), ALU.mult), "k_rows")

            def scores(buf, n, parts, scale, name):
                for src, dst, mask, a in parts:
                    ins = dve.tensor_tensor_reduce(dst, src, mask, scale, -3e38, ALU.add, ALU.max, st[:, a:a + 1])
                return ins

            def minus(n, name):
                c = 340 + 2 * (n % 4)
                mark(dve.tensor_scalar(st[:, c:c + 2], st[:, c:c + 2], -1.0, None, ALU.mult), name + "_scores")

            def taken_score(ins):
                mark(ins, "score_taken")

            def attend(name, n, dst):
                p = scored()
                dve.wait_ge(sem(name + "_exp"), n + 1)
                c = 350 + 2 * (n % 4)
                link(dve.reciprocal(st[:, 360 + 2 * (n % 4):362 + 2 * (n % 4)], st[:, c:c + 2]))
                for t in range(TT):
                    o = dst(t)
                    w = o.shape[-1]
                    ins = dve.tensor_scalar(o, p[:, w * t:w * t + w], st[:, 360 + 2 * (n % 4) + t:361 + 2 * (n % 4) + t], None, ALU.mult)
                    if t == 0:
                        link(ins)
                mark(ins, "score_taken")

            om3 = o_mla.rearrange("p (t c) -> p t c", c=DM)
            for h in range(MH + 2):
                if h < MH:
                    p = scored()
                    s = soft[:, 512 * (h % 2):512 * (h % 2) + 512]
                    c = 340 + 2 * (h % 4)
                    link(scores(s, h, ((p[:, 0:128], s[:, 0:128], masks[:, 0, 128:256], c),), QW ** -0.5, None))
                    taken_score(scores(s, h, ((p[:, 128:384], s[:, 128:384], masks[:, 0, :], c + 1),), QW ** -0.5, None))
                    minus(h, "mla")
                if h >= 2:
                    attend("mla", h - 2, lambda t: om3[:, t, DV * (h - 2):DV * (h - 1)])

            dve.wait_ge(sem("taken_act"), taken("mk")[1])
            for i, (x, g) in enumerate(((mq_tok, "g_q_mem"), (mk_tok, "g_k_mem"))):
                x8 = x.rearrange("p (g c) -> p g c", c=EQ)
                q8 = qdec[:, 0:512].rearrange("p (g c) -> p g c", c=EQ)
                link(tt(q8, x8, x8, ALU.mult))
                link(dve.tensor_reduce(st[:, 144 + 8 * i:152 + 8 * i], q8, AX.X, ALU.add))
            var(st[:, 144:160], st[:, 144:160], EQ, "m")
            newton(144, 16, "m")
            for i, (x, g) in enumerate(((mq_tok, "g_q_mem"), (mk_tok, "g_k_mem"))):
                x8 = x.rearrange("p (g c) -> p g c", c=EQ)
                link(tt(x8, x8, bc(st[:, 160 + 8 * i:168 + 8 * i].unsqueeze(2), [P, 8, EQ]), ALU.mult))
                mark(tt(x8, x8, bc(gain[g].unsqueeze(1), [P, 8, EQ]), ALU.mult), "m_rows")

            rg3 = r_gla.rearrange("p (t c) -> p t c", c=DM)
            for t in range(TT):
                dve.wait_ge(sem("silu_sig"), t + 1)
                mark(tt(rg3[:, t, :], rg3[:, t, :], junk, ALU.mult), "silu_done")
                g4 = rg3[:, t, :].rearrange("p (h c) -> p h c", c=GV)
                link(tt(g4, g4, bc(gain["g_gla_out"].unsqueeze(1), [P, GH, GV]), ALU.mult))

            def level_diff(i):
                if i < len(LEVELS):
                    s = LEVELS[i]
                    b, dd = (x.rearrange("p (b u s) -> p b u s", u=2, s=s) for x in (bT, dec))
                    nb = 1024 // (2 * s)
                    ref = bc(b[:, :, 0, s - 1:s], [P, nb, s])
                    link(tt(dd[:, :, 0, :], ref, b[:, :, 0, :], ALU.subtract))
                    mark(tt(dd[:, :, 1, :], b[:, :, 1, :], ref, ALU.subtract), "level_diff")
                else:
                    b, dd = (x.rearrange("p (h t s) -> p h t s", t=TT, s=P) for x in (bT, dec))
                    link(tt(dd[:, :, 0, :], bc(b[:, :, 0, P - 1:P], [P, GH, P]), b[:, :, 0, :], ALU.subtract))
                    mark(dve.tensor_copy(dd[:, :, 1, :], b[:, :, 1, :]), "level_diff")

            om_mem = o_mem.rearrange("p (t c) -> p t c", c=DM)
            og3 = o_gla.rearrange("p (t c) -> p t c", c=DM)

            def gate_take(n):
                i = GATES[n]
                p = arrived(f"gate{i}")
                dve.wait_ge(sem(f"bgate{n % 2}"), 16 * (n // 2 + 1))
                g = gate_buf[:, 1024 * (n % 2):1024 * (n % 2) + 1024]
                for t in range(TT):
                    ins = tt(g[:, 512 * t:512 * t + 512], p[:, 512 * t:512 * t + 512], bgate[:, 512 * (n % 2):512 * (n % 2) + 512], ALU.add)
                    if t == 0:
                        link(ins)
                mark(ins, "taken_dve")

            def gate_apply(n):
                dve.wait_ge(sem("gate_sig"), n + 1)
                i = GATES[n]
                o = (om3, og3, om_mem)[i // 2][:, :, 512 * (i % 2):512 * (i % 2) + 512]
                g = gate_buf[:, 1024 * (n % 2):1024 * (n % 2) + 1024].rearrange("p (t c) -> p t c", c=512)
                link(tt(o, o, g, ALU.mult))

            lv3 = levels.rearrange("p (l n) -> p l n", n=P)
            level_diff(0)
            for i in range(9):
                if i < 8:
                    dve.wait_ge(sem("level_exp"), i + 1)
                    link(tt(qdec, qgT, dec, ALU.mult))
                    mark(tt(kdec, kgT, dec, ALU.mult), "level_ready")
                    if i + 1 < 8:
                        level_diff(i + 1)
                if i < EH:
                    p = scored()
                    s = soft[:, 512 * (i % 2):512 * (i % 2) + 512]
                    c = 340 + 2 * (i % 4)
                    zero = bc(masks[:, 0, 0:1], [P, 256])
                    link(scores(s, i, ((p[:, 0:256], s[:, 0:256], zero, c),), EQ ** -0.5, None))
                    taken_score(scores(s, i, ((p[:, 256:512], s[:, 256:512], zero, c + 1),), EQ ** -0.5, None))
                    minus(i, "mem")
                if 2 <= i < EH + 2:
                    attend("mem", i - 2, lambda t: om_mem[:, t, EV * (i - 2):EV * (i - 1)])
                if i == 7:
                    p = scored()
                    taken_score(dve.tensor_copy(across, p[:, :]))
                else:
                    for u in range(2):
                        p = scored()
                        mask = bc(lv3[:, i if i < 7 else 7:(i if i < 7 else 7) + 1, :], [P, 4, P])
                        src = p[:, :].rearrange("p (b n) -> p b n", n=P)
                        am = amat[:, 512 * u:512 * u + 512]
                        if i == 0:
                            taken_score(tt(am.rearrange("p (b n) -> p b n", n=P), src, mask, ALU.mult))
                        else:
                            taken_score(tt(wgate.rearrange("p (b n) -> p b n", n=P), src, mask, ALU.mult))
                            ins = tt(am, am, wgate, ALU.add)
                            if i == 8:
                                mark(ins, "amat")
                            else:
                                link(ins)
                if i in (4, 6, 8):
                    gate_take((i - 4) // 2)
                if i in (6, 8):
                    gate_apply((i - 6) // 2)
            for n in range(4):
                p = scored()
                taken_score(dve.tensor_copy(og3[:, n // 2, 512 * (n % 2):512 * (n % 2) + 512], p[:, :]))
            for t in range(TT):
                link(tt(junk, og3[:, t, :], og3[:, t, :], ALU.mult))
                link(dve.tensor_reduce(st[:, 176 + 4 * t:180 + 4 * t], junk.rearrange("p (h c) -> p h c", c=GV), AX.X, ALU.add))
            var(st[:, 176:184], st[:, 176:184], GV, "og")
            newton(176, 8, "og")
            o8 = o_gla.rearrange("p (g c) -> p g c", c=GV)
            link(tt(o8, o8, bc(st[:, 184:192].unsqueeze(2), [P, 8, GV]), ALU.mult))
            link(tt(o_gla, o_gla, r_gla, ALU.mult))
            gate_apply(2)
            gate_take(3)
            gate_take(4)
            gate_apply(3)
            link(tt(o_mla, o_mla, o_mem, ALU.add))
            gate_take(5)
            for n in (4, 5):
                gate_apply(n)
                c = 512 * (GATES[n] % 2)
                mark(tt(om3[:, :, c:c + 512], om3[:, :, c:c + 512], og3[:, :, c:c + 512], ALU.add), "y_rows")

            def residual(name, i):
                p = arrived(name)
                for t in range(TT):
                    x = xres[:, t, 512 * i:512 * i + 512]
                    ins = tt(x, p[:, 512 * t:512 * t + 512], x, ALU.add)
                    if t == 0:
                        link(ins)
                mark(ins, "taken_dve")

            for i in range(2):
                residual(f"wo{i}", i)
            rms_rows(lambda t: xres[:, t, :], lambda t: xn2[:, DM * t:DM * t + DM], 0, 280, "x", 4)

            R = srow[0:ST, :].rearrange("p (k n) -> p k n", n=128)
            lr, li, mag, cosr, sinr, kk, fre, fim, den, t1, t2 = (R[:, i, :] for i in (0, 1, 3, 4, 5, 6, 7, 8, 9, 10, 11))
            dve.wait_ge(sem("ssm_in"), 16 * 9)
            dve.wait_ge(sem("dt_ready"), 1)
            dtb = bc(srow[0:ST, 258:260].unsqueeze(2), [ST, 2, SN])
            h2 = lambda x: x.rearrange("p (a n) -> p a n", n=SN)
            link(tt(h2(mag), h2(lr), dtb, ALU.mult))
            link(tt(h2(sinr), h2(li), dtb, ALU.mult))
            mark(reduce_angle(sinr, cosr, ST), "theta")
            link(tt(t1, lr, lr, ALU.mult))
            link(tt(den, li, li, ALU.mult))
            link(tt(den, den, t1, ALU.add))
            link(dve.reciprocal(den, den))
            dve.wait_ge(sem("trig"), 1)
            link(tt(t1, mag, cosr, ALU.mult))
            link(tt(t2, mag, sinr, ALU.mult))
            link(dve.tensor_scalar(t1, t1, -1.0, None, ALU.add))
            link(tt(fre, t1, lr, ALU.mult))
            link(tt(kk, t2, li, ALU.mult))
            link(tt(fre, fre, kk, ALU.add))
            link(tt(fre, fre, den, ALU.mult))
            link(tt(fim, t2, lr, ALU.mult))
            link(tt(kk, t1, li, ALU.mult))
            link(tt(fim, fim, kk, ALU.subtract))
            mark(tt(fim, fim, den, ALU.mult), "lane_rows")

            dve.wait_ge(sem("turned_taken"), T_LANE)
            c4 = cs.rearrange("p (j r t) -> p j r t", r=2, t=CH)
            link(dve.memset(c4[:, :, 0, 0:1], 1.0))
            link(dve.memset(c4[:, :, 1, 0:1], 0.0))
            link(dve.tensor_copy(lam["ere"], lam["cos"]))
            link(dve.tensor_copy(lam["eim"], lam["sin"]))
            n = 1
            while n < CH:
                a, b = (tmp_cs[:, 2048 * i:2048 * i + 32 * n].rearrange("p (j t) -> p j t", t=n) for i in range(2))
                er, ei = (bc(lam[k].unsqueeze(2), [P, ST, n]) for k in ("ere", "eim"))
                pr, pi = c4[:, :, 0, 0:n], c4[:, :, 1, 0:n]
                link(tt(a, pr, er, ALU.mult))
                link(tt(b, pi, ei, ALU.mult))
                link(tt(c4[:, :, 0, n:2 * n], a, b, ALU.subtract))
                link(tt(a, pr, ei, ALU.mult))
                link(tt(b, pi, er, ALU.mult))
                link(tt(c4[:, :, 1, n:2 * n], a, b, ALU.add))
                link(tt(lam["sq"], lam["ere"], lam["ere"], ALU.mult))
                link(tt(lam["sq2"], lam["eim"], lam["eim"], ALU.mult))
                link(tt(lam["eim"], lam["ere"], lam["eim"], ALU.mult))
                link(dve.tensor_scalar(lam["eim"], lam["eim"], 2.0, None, ALU.mult))
                link(tt(lam["ere"], lam["sq"], lam["sq2"], ALU.subtract))
                n *= 2
            mark(dve.memset(cc, 0.0), "tables")

            for i in range(8):
                dve.wait_ge(sem("taken_act"), taken(f"up{i}")[1])
                u = hup[:, 1024 * i:1024 * i + 1024]
                mark(tt(u, u, u, ALU.mult), "ff_ready")

            dve.wait_ge(sem("turned_taken"), T_C)
            cr, ci = (tmp_cs[:, 1024 * i:1024 * i + 1024].rearrange("p (j c) -> p j c", c=32) for i in range(2))
            ta, tb = (tmp_cs[:, 2048 + 1024 * i:3072 + 1024 * i].rearrange("p (j c) -> p j c", c=32) for i in range(2))
            fr, fi = (bc(lam[k].unsqueeze(2), [P, ST, 32]) for k in ("fre", "fim"))
            for i in range(2):
                link(tt(ta, cr, (fr, fi)[i], ALU.mult))
                link(tt(tb, ci, (fi, fr)[i], ALU.mult))
                cv = cc[:, 1024 * i:1024 * i + 1024].rearrange("p (j c) -> p j c", c=32)
                for a in range(2):
                    q = slice(64 * a, 64 * a + 64)
                    w = slice(16 * a, 16 * a + 16)
                    if i == 0:
                        ins = tt(cv[q, :, w], ta[q, :, w], tb[q, :, w], ALU.subtract)
                    else:
                        ins = dve.scalar_tensor_tensor(cv[q, :, w], ta[q, :, w], -1.0, tb[q, :, w], ALU.mult, ALU.subtract)
                    mark(ins, "c_ready")

            for i in range(2):
                residual(f"down{i}", i)
            rms_rows(lambda t: xres[:, t, :], lambda t: xn3[:, DM * t:DM * t + DM], 0, 280, "x", 6)

            def z_silu(z):
                dve.wait_ge(sem("taken_act"), taken(z)[1])
                x = za if z == "za" else zs[:, 1024 * int(z[2]):1024 * int(z[2]) + 1024]
                mark(tt(x, x, raw, ALU.mult), "z_silu")

            def dqk(n):
                g = n % 3
                name, gn = (f"dq{g}", "q_norm_w_2") if n < 3 else (f"dk{g}", "k_norm_w_2")
                dve.wait_ge(sem("taken_act"), taken(name)[1])
                r16 = raw.rearrange("p (g c) -> p g c", c=DD)
                link(dve.tensor_reduce(st[:, 192:208], raw2.rearrange("p (g c) -> p g c", c=DD), AX.X, ALU.add))
                var(st[:, 192:208], st[:, 192:208], DD, "dqk")
                newton(192, 16, "dqk")
                link(tt(r16, r16, bc(st[:, 208:224].unsqueeze(2), [P, 16, DD]), ALU.mult))
                link(tt(r16, r16, bc(gain[gn][:, DD * g:DD * g + DD].unsqueeze(1), [P, 16, DD]), ALU.mult))
                r4 = raw.rearrange("p (t h c) -> p t h c", t=TT, c=DD)
                y1, y2 = r4[:, :, :, 0:8], r4[:, :, :, 8:16]
                cb, sb_ = (bc(rope[:, k, :, 32:40].unsqueeze(2), [P, TT, DH, 8]) for k in range(2))
                tm = [raw2[:, 128 * i:128 * i + 128].rearrange("p (t h c) -> p t h c", t=TT, c=8) for i in range(4)]
                link(tt(tm[0], y1, cb, ALU.mult))
                link(tt(tm[1], y2, sb_, ALU.mult))
                link(tt(tm[2], y2, cb, ALU.mult))
                link(tt(tm[3], y1, sb_, ALU.mult))
                link(tt(y1, tm[0], tm[1], ALU.subtract))
                mark(tt(y2, tm[2], tm[3], ALU.add), "dqk_rows")

            for j in range(ST + 2):
                if j < ST:
                    p = scored()
                    w4 = p[:, :].rearrange("p (c t) -> p c t", t=CH)
                    tab = c4[:, j]
                    m1, m2 = wrot[:, 0:512], wrot[:, 512:1024]
                    link(tt(m1.rearrange("p (c t) -> p c t", t=CH), w4, bc(tab[:, 0:1, :], [P, 4, CH]), ALU.mult))
                    taken_score(tt(m2.rearrange("p (c t) -> p c t", t=CH), w4, bc(tab[:, 1:2, :], [P, 4, CH]), ALU.mult))
                    link(tt(m1[:, 0:256], m1[:, 0:256], m2[:, 256:512], ALU.add))
                    link(tt(m1[:, 256:512], m1[:, 256:512], m2[:, 0:256], ALU.subtract))
                    g = gst[:, 512 * (j % 2):512 * (j % 2) + 512]
                    mg = bc(lam["mag"][:, j:j + 1], [P, CH])
                    if j >= 2:
                        dve.wait_ge(sem("h_ready"), 2 * (j - 1))
                    link(dve.tensor_tensor_scan(g[:, 0:CH], mg, m1[:, 0:CH], 0.0, ALU.mult, ALU.add))
                    link(dve.tensor_tensor_scan(g[:, 256:256 + CH], mg, m1[:, 256:256 + CH], 0.0, ALU.mult, ALU.add))
                    gr, gi = g[:, CH - 1:CH], g[:, 256 + CH - 1:256 + CH]
                    er, ei = lam["ere"][:, j:j + 1], lam["eim"][:, j:j + 1]
                    link(tt(carry[:, 0:1], gi, ei, ALU.mult))
                    link(tt(carry[:, 1:2], gr, ei, ALU.mult))
                    link(dve.scalar_tensor_tensor(carry[:, 2:3], gr, er, carry[:, 0:1], ALU.mult, ALU.subtract))
                    link(dve.scalar_tensor_tensor(carry[:, 3:4], gi, er, carry[:, 1:2], ALU.mult, ALU.add))
                    link(dve.tensor_tensor_scan(g[:, CH:256], mg, m1[:, CH:256], carry[:, 2:3], ALU.mult, ALU.add))
                    mark(dve.tensor_tensor_scan(g[:, 256 + CH:512], mg, m1[:, 256 + CH:512], carry[:, 3:4], ALU.mult, ALU.add), "g_ready")
                if j >= 2:
                    i = j - 2
                    p = scored()
                    q = slice(32 * (i % 4), 32 * (i % 4) + 32)
                    u = uT[q, SEQ * (i // 4):SEQ * (i // 4) + SEQ]
                    taken_score(dve.scalar_tensor_tensor(u, u, col("d_skip_2", i // 4)[q, :], p[q, 0:SEQ], ALU.mult, ALU.add))
                if j in (16, 20, 24):
                    z_silu(("zs0", "zs1", "za")[(j - 16) // 4])
                if j == 29:
                    dqk(0)
            dqk(1)
            for i in range(2):
                y, z = uT[:, 1024 * i:1024 * i + 1024], gz[:, 1024 * i:1024 * i + 1024]
                link(tt(z, y, y, ALU.mult))
                link(dve.tensor_scalar(z, z, 0.044715, 1.0, ALU.mult, ALU.add))
                mark(tt(z, z, y, ALU.mult), "gelu_z")
            dqk(2)
            for i in range(2):
                dve.wait_ge(sem("gelu_sig"), i + 1)
                y, z = uT[:, 1024 * i:1024 * i + 1024], gz[:, 1024 * i:1024 * i + 1024]
                mark(tt(y, y, z, ALU.mult), "gelu_ready")
                link(tt(z, y, zs[:, 1024 * i:1024 * i + 1024], ALU.mult))
            for n in (3, 4, 5):
                dqk(n)

            ya3 = ya.rearrange("p (t c) -> p t c", c=DW)
            for h in range(DH + 2):
                if h < DH:
                    s = dsoft[:, 1152 * (h % 2):1152 * (h % 2) + 1152]
                    c = 340 + 2 * (h % 4)
                    p = scored()
                    taken_score(scores(s, h, ((p[:, :], s[:, 384:896], masks[:, 1:3, :].rearrange("p g s -> p (g s)"), 132),), DD ** -0.5, None))
                    p = scored()
                    taken_score(scores(s, h, ((p[:, 0:256], s[:, 896:1152], masks[:, 3, :], 133),), DD ** -0.5, None))
                    p = scored()
                    taken_score(scores(s, h, ((p[:, 0:384].rearrange("p (g s) -> p g s", s=128), s[:, 0:384].rearrange("p (g s) -> p g s", s=128),
                                               masks[:, 1:4, 128:256], c),), DD ** -0.5, None))
                    link(tt(st[:, c + 1:c + 2], st[:, 132:133], st[:, 133:134], ALU.max))
                    minus(h, "dil")
                if h >= 2:
                    attend("dil", h - 2, lambda t: ya3[:, t, DD * (h - 2):DD * (h - 1)])
                if h == 9:
                    dve.wait_ge(sem("taken_act"), taken("glu0")[1])
                    mark(tt(yssT[:, 0:1024], sig_glu[:, 0:1024], gz[:, 0:1024], ALU.mult), "yss")
            mark(tt(ya, ya, za, ALU.mult), "ya_rows")
            dve.wait_ge(sem("taken_act"), taken("glu1")[1])
            mark(tt(yssT[:, 1024:2048], sig_glu[:, 1024:2048], gz[:, 1024:2048], ALU.mult), "yss")
            m3 = m_tok.rearrange("p (t c) -> p t c", c=DM)
            r3 = rsig.rearrange("p (t c) -> p t c", c=DM)
            s3 = asig.rearrange("p (t c) -> p t c", c=DM)
            for i in range(2):
                p = arrived(f"so{i}")
                for t in range(TT):
                    ins = tt(m3[:, t, 512 * i:512 * i + 512], p[:, 512 * t:512 * t + 512], r3[:, t, 512 * i:512 * i + 512], ALU.mult)
                    if t == 0:
                        link(ins)
                mark(ins, "taken_dve")
            for i in range(2):
                p = arrived(f"ao{i}")
                for t in range(TT):
                    a = s3[:, t, 512 * i:512 * i + 512]
                    ins = tt(a, p[:, 512 * t:512 * t + 512], a, ALU.mult)
                    if t == 0:
                        link(ins)
                mark(ins, "taken_dve")
                mark(tt(m3[:, :, 512 * i:512 * i + 512], m3[:, :, 512 * i:512 * i + 512], s3[:, :, 512 * i:512 * i + 512], ALU.add), "m_sum")
            for i in range(2):
                residual(f"wp{i}", i)

        @block.tensor
        def _(pe):
            n_unit = {"turned": 0, "score": 0}
            turned_at = {}

            def unit(kind):
                n = n_unit[kind]
                n_unit[kind] += 1
                if n >= 2:
                    pe.wait_ge(sem(kind + "_taken"), n - 1)
                return bank[kind][n % 2]

            def turn(name, blocks):
                b = unit("turned")
                a = 0
                for x in blocks:
                    rows = x.shape[0]
                    ins = pe.transpose(b[0:x.shape[1], a:a + rows], x, ident[0:rows, 0:rows])
                    a += rows
                ins.then_inc(sem("turned_ready"), 1)
                turned_at[name] = n_unit["turned"]

            def is_turned(name):
                pe.wait_ge(sem("turned_taken"), turned_at[name])

            def matmuls(name):
                j = JOB[name]
                _, o, w, r0, rows, c0, cols = JOBS[j]
                p = pair[OUTS.index(o) % 2]
                if w is None:
                    return [(p[:, SEQ * h:SEQ * h + SEQ], wgate[0:GR, P * h:P * h + P], aT[0:GR, :], True, True) for h in range(GH)]
                nk = rows // P
                ws = ring[:, STREAMED.index(j) % RING, 0:nk * cols].rearrange("p (k n) -> p k n", n=cols)
                base, total = 0, nk
                if o.startswith("kv"):
                    act_ = lambda k: ckvT[:, SEQ * k:SEQ * k + SEQ]
                elif o in ("mk", "mv0", "mv1"):
                    act_ = lambda k: memT[:, SEQ * k:SEQ * k + SEQ]
                elif o.startswith("down"):
                    base, total = KD * int(name[-1]), FF // P
                    act_ = lambda k: hup[:, SEQ * (base + k):SEQ * (base + k) + SEQ]
                elif o.startswith("glu"):
                    act_ = lambda k: uT[:, SEQ * k:SEQ * k + SEQ]
                elif o.startswith("so"):
                    act_ = lambda k: yssT[:, SEQ * k:SEQ * k + SEQ]
                elif o.startswith("ao"):
                    act_ = lambda k: yaT[:, SEQ * k:SEQ * k + SEQ]
                else:
                    act_ = lambda k: hT[:, k, :]
                if o in CHANNEL_MAJOR:
                    m = min(cols, P)
                    return [(p[0:m, SEQ * c:SEQ * c + SEQ], ws[:, k, m * c:m * c + m], act_(k), k == 0, k == nk - 1)
                            for c in range(cols // m) for k in range(nk)]
                return [(p[:, 512 * t:512 * t + cols], act_(k)[:, P * t:P * t + P], ws[:, k, :], base + k == 0, base + k == total - 1)
                        for t in range(TT) for k in range(nk)]

            def part(name, q, of=4):
                j = JOB[name]
                o = JOBS[j][1]
                if q == 0:
                    if JOBS[j][2]:
                        n = STREAMED.index(j)
                        pe.wait_ge(sem(f"weights{n % RING}"), 16 * (n // RING + 1))
                    i = OUTS.index(o)
                    if i >= 2 and (j == 0 or JOBS[j - 1][1] != o):
                        by, v = taken(OUTS[i - 2])
                        pe.wait_ge(sem("taken_" + by), v)
                mm = matmuls(name)
                n = len(mm)
                for o_, s, m, a, b in mm[n * q // of:n * (q + 1) // of]:
                    ins = pe.matmul(o_, s, m, start=a, stop=b, skip_group_check=JOBS[j][1].startswith("down"))
                if q == of - 1:
                    ins.then_inc(sem("job_done"), 1)

            def job(name):
                part(name, 0, 1)

            def fill(names, i, n):
                for q in range(n * i, n * i + n):
                    if q < 4 * len(names):
                        part(names[q // 4], q % 4)

            def ktiles(x, w=DM):
                v = x.rearrange("p (t c) -> p t c", c=w)
                return [v[:, t, P * k:P * k + P] for k in range(w // P) for t in range(TT)]

            pe.wait_ge(sem("ident_in"), 16)
            pe.wait_ge(sem("rows_in"), 16 * len(COLS))
            turn("cols", [prow[:, :]])
            pe.wait_ge(sem("x_rows"), 2)
            for g in range(4):
                turn("x", ktiles(xn1)[4 * g:4 * g + 4])
            is_turned("x")
            job("ckv")
            job("gq")
            pe.wait_ge(sem("mem_rows"), 2)
            for g in range(4):
                turn("mem", ktiles(mem_tok)[4 * g:4 * g + 4])
            job("gk")
            job("ga")
            pe.wait_ge(sem("ckv_rows"), 2)
            ck = ckv.rearrange("p (t c) -> p t c", c=RANK + ROPE)
            turn("ckv", [ck[:, t, P * k:P * k + P] for k in range(2) for t in range(TT)])
            pe.wait_ge(sem("kpe_rows"), 2)
            turn("kpe", [kpe[:, P * t:P * t + P] for t in range(TT)])
            pe.wait_ge(sem("taken_act"), taken("ga")[1])
            pe.wait_ge(sem("consts_in"), 16 * (8 + len(GAINS)))
            job("gg")
            for i in range(3):
                job(f"q{i}")
            is_turned("ckv")
            for i in range(4):
                job(f"kv{i}")
            q16 = q_tok.rearrange("p (t h c) -> p t h c", t=TT, c=QW)
            pe.wait_ge(sem("q_rows"), 1)
            for g in range(4):
                turn("qn", [q16[:, t, h, 0:NOPE] for h in (2 * g, 2 * g + 1) for t in range(TT)])
            pe.wait_ge(sem("qpe_rows"), 1)
            for g in range(2):
                turn("qp", ktiles(qpe, MH * ROPE)[4 * g:4 * g + 4])
            k16 = kv_tok.rearrange("p (t h c) -> p t h c", t=TT, c=NOPE + DV)
            part("gv0", 0)
            part("gv0", 1)
            pe.wait_ge(sem("k_rows"), 1)
            for g in range(4):
                turn("kn", [k16[:, t, h, 0:NOPE] for h in (2 * g, 2 * g + 1) for t in range(TT)])
            is_turned("kn")

            for h in range(MH + 2):
                if h == 0:
                    part("gv0", 2)
                    part("gv0", 3)
                else:
                    fill(["gv1", "gr0", "gr1", "mq", "mk"], h - 1, 2)
                if h < MH:
                    b = unit("score")
                    r = slice(64 * (h % 2), 64 * (h % 2) + 64)
                    for t in range(TT):
                        w = P * (t + 1)
                        o = b[:, P * t:P * t + w]
                        pe.matmul(o, qnT[:, SEQ * h + P * t:SEQ * h + P * t + P], knT[:, SEQ * h:SEQ * h + w], start=True, stop=False)
                        ins = pe.matmul(o, qpT[r, SEQ * (h // 2) + P * t:SEQ * (h // 2) + P * t + P], kpeT[r, 0:w], start=False, stop=True)
                    ins.then_inc(sem("score_ready"), 1)
                if 1 <= h <= MH:
                    pe.wait_ge(sem("mla_exp"), h)
                    s = soft[:, 512 * ((h - 1) % 2):512 * ((h - 1) % 2) + 384]
                    turn(f"mla{h - 1}", [s[:, 0:128], s[:, 128:256], s[:, 256:384]])
                if h >= 2:
                    i = h - 2
                    is_turned(f"mla{i}")
                    b = unit("score")
                    s = softT[:, 512 * (i % 2):512 * (i % 2) + 384]
                    v = lambda t: k16[:, t, i, NOPE:NOPE + DV]
                    pe.matmul(b[:, 0:128], s[:, 0:128], v(0), start=True, stop=True)
                    pe.matmul(b[:, 128:256], s[:, 128:256], v(0), start=True, stop=False)
                    pe.matmul(b[:, 128:256], s[:, 256:384], v(1), start=False, stop=True).then_inc(sem("score_ready"), 1)
            part("mk", 2)
            part("mk", 3)
            job("mv0")
            pe.wait_ge(sem("m_rows"), 2)
            turn("qm", ktiles(mq_tok, 256))
            turn("km", ktiles(mk_tok, 256))
            is_turned("km")

            vm3 = vm.rearrange("p (t c) -> p t c", c=DM)
            vg3 = vg.rearrange("p (t c) -> p t c", c=DM)
            for i in range(9):
                fill(["mv1", "gate0", "gate1", "gate4", "gate5"], i, 2)
                if i < EH:
                    b = unit("score")
                    r = slice(64 * (i % 2), 64 * (i % 2) + 64)
                    for t in range(TT):
                        ins = pe.matmul(b[:, SEQ * t:SEQ * t + SEQ], qmT[r, SEQ * (i // 2) + P * t:SEQ * (i // 2) + P * t + P],
                                        kmT[r, SEQ * (i // 2):SEQ * (i // 2) + SEQ], start=True, stop=True)
                    ins.then_inc(sem("score_ready"), 1)
                if 1 <= i <= EH:
                    pe.wait_ge(sem("mem_exp"), i)
                    s = soft[:, 512 * ((i - 1) % 2):512 * ((i - 1) % 2) + 512]
                    turn(f"mem{i - 1}", [s[:, P * k:P * k + P] for k in range(4)])
                if 2 <= i < EH + 2:
                    h = i - 2
                    is_turned(f"mem{h}")
                    pe.wait_ge(sem("taken_act"), taken("mv1")[1])
                    b = unit("score")
                    s = softT[:, 512 * (h % 2):512 * (h % 2) + 512]
                    for t in range(TT):
                        for k in range(2):
                            ins = pe.matmul(b[:, SEQ * t:SEQ * t + SEQ], s[:, 256 * t + P * k:256 * t + P * k + P],
                                            vm3[:, k, EV * h:EV * h + EV], start=k == 0, stop=k == 1)
                    ins.then_inc(sem("score_ready"), 1)
                if i < 8:
                    pe.wait_ge(sem("level_ready"), i + 1)
                ks, qs = (kgT, qgT) if i == 8 else (kdec, qdec)
                if i == 7:
                    b = unit("score")
                    for h in range(GH):
                        ins = pe.matmul(b[:, P * h:P * h + P], ks[:, SEQ * h:SEQ * h + P], qs[:, SEQ * h + P:SEQ * h + 2 * P], start=True, stop=True)
                    ins.then_inc(sem("score_ready"), 1)
                else:
                    for u in range(2):
                        b = unit("score")
                        for k in range(4):
                            a = P * (4 * u + k)
                            ins = pe.matmul(b[:, P * k:P * k + P], ks[:, a:a + P], qs[:, a:a + P], start=True, stop=True)
                        ins.then_inc(sem("score_ready"), 1)
            pe.wait_ge(sem("amat"), 2)
            for n in range(4):
                b = unit("score")
                t = n // 2
                for k in range(2):
                    h = 2 * (n % 2) + k
                    o = b[:, GV * k:GV * k + GV]
                    ins = pe.matmul(o, amat[:, P * (2 * h + t):P * (2 * h + t) + P], vg3[:, t, GV * h:GV * h + GV], start=True, stop=t == 0)
                    if t:
                        ins = pe.matmul(o, across[:, P * h:P * h + P], vg3[:, 0, GV * h:GV * h + GV], start=False, stop=True)
                ins.then_inc(sem("score_ready"), 1)
            part("gate5", 2)
            part("gate5", 3)
            job("gate2")
            job("gate3")
            pe.wait_ge(sem("y_rows"), 2)
            for g in range(4):
                turn("y", ktiles(o_mla)[4 * g:4 * g + 4])
            is_turned("y")
            job("wo0")
            job("wo1")

            pe.wait_ge(sem("x_rows"), 4)
            for g in range(4):
                turn("x", ktiles(xn2)[4 * g:4 * g + 4])
            is_turned("x")
            R = srow[0:ST, :].rearrange("p (k n) -> p k n", n=128)
            for i in range(8):
                job(f"up{i}")
                if i == 2:
                    pe.wait_ge(sem("lane_rows"), 1)
                    turn("lane", [R[:, k, :] for k in (4, 5, 3, 7, 8)])
                    assert n_unit["turned"] == T_LANE, n_unit
                if i == 4:
                    pe.wait_ge(sem("bexp_ready"), 4)
                    for k in range(4):
                        turn("b", [bexp[:, 512 * k + P * m:512 * k + P * m + P] for m in range(4)])
            for h in range(2):
                for k in range(4):
                    if h == 0:
                        pe.wait_ge(sem("ff_ready"), 2 * k + 2)
                    job(f"down{h}{k}")
                    if h == 0 and k == 0:
                        for m in range(4):
                            turn("c", [cnat[:, 512 * m + P * a:512 * m + P * a + P] for a in range(4)])
                        assert n_unit["turned"] == T_C, n_unit

            pe.wait_ge(sem("x_rows"), 6)
            for g in range(4):
                turn("x", ktiles(xn3)[4 * g:4 * g + 4])
            is_turned("x")
            job("us0")
            job("us1")
            pe.wait_ge(sem("taken_act"), taken("us1")[1])
            pe.wait_ge(sem("c_ready"), 4)
            for j in range(ST + 2):
                if j < ST:
                    fill(["dv0", "dv1", "dv2", "zs0", "zs1", "za", "dq0", "dq1"], j, 1)
                    b = unit("score")
                    r = slice(32 * (j % 4), 32 * (j % 4) + 32)
                    for i in range(2):
                        ins = pe.matmul(b[:, SEQ * i:SEQ * i + SEQ], bt[r, 1024 * i + P * (j // 4):1024 * i + P * (j // 4) + P],
                                        uT[r, SEQ * (j // 4):SEQ * (j // 4) + SEQ], start=True, stop=True)
                    ins.then_inc(sem("score_ready"), 1)
                if j >= 2:
                    i = j - 2
                    b = unit("score")
                    pe.wait_ge(sem("h_ready"), 2 * i + 2)
                    h = hst[:, 512 * (i % 3):512 * (i % 3) + 512]
                    r = slice(32 * (i % 4), 32 * (i % 4) + 32)
                    pe.matmul(b[r, 0:SEQ], cc[:, 32 * i:32 * i + 32], h[:, 0:256], start=True, stop=False)
                    pe.matmul(b[r, 0:SEQ], cc[:, 1024 + 32 * i:1024 + 32 * i + 32], h[:, 256:512], start=False, stop=True).then_inc(sem("score_ready"), 1)

            def turn_dqk(n):
                pe.wait_ge(sem("dqk_rows"), n + 1)
                for k in range(2):
                    turn(f"dqk{n}", ktiles(raw, DW)[4 * k:4 * k + 4])

            turn_dqk(0)
            job("dq2")
            turn_dqk(1)
            for n in range(3):
                job(f"dk{n}")
                turn_dqk(n + 2)
            job("rs0")
            turn_dqk(5)
            is_turned("dqk5")
            vd4 = vd.rearrange("p (g t c) -> p g t c", g=NDIL, t=TT)
            for h in range(DH + 2):
                if h == 6:
                    pe.wait_ge(sem("gelu_ready"), 2)
                fill(["rs1", "ra0", "ra1", "glu0", "glu1"], h, 2)
                if h < DH:
                    r = slice(64 * (h % 2), 64 * (h % 2) + 64)
                    q = lambda g, t: qdT[r, 1024 * g + SEQ * (h // 2) + P * t:1024 * g + SEQ * (h // 2) + P * t + P]
                    k = lambda g, w: kdT[r, 1024 * g + SEQ * (h // 2):1024 * g + SEQ * (h // 2) + w]
                    b = unit("score")
                    for g in range(2):
                        ins = pe.matmul(b[:, 256 * g:256 * g + 256], q(g, 1), k(g, 256), start=True, stop=True)
                    ins.then_inc(sem("score_ready"), 1)
                    b = unit("score")
                    pe.matmul(b[:, 0:256], q(2, 1), k(2, 256), start=True, stop=True).then_inc(sem("score_ready"), 1)
                    b = unit("score")
                    for g in range(NDIL):
                        ins = pe.matmul(b[:, P * g:P * g + P], q(g, 0), k(g, 128), start=True, stop=True)
                    ins.then_inc(sem("score_ready"), 1)
                if 1 <= h <= DH:
                    pe.wait_ge(sem("dil_exp"), h)
                    s = dsoft[:, 1152 * ((h - 1) % 2):1152 * ((h - 1) % 2) + 1152]
                    for g in range(NDIL):
                        a = 384 + 256 * g
                        turn(f"dil{h - 1}", [s[:, P * g:P * g + P], s[:, a:a + P], s[:, a + P:a + 2 * P]])
                if h >= 2:
                    i = h - 2
                    is_turned(f"dil{i}")
                    b = unit("score")
                    s = dsoftT[:, 1152 * (i % 2):1152 * (i % 2) + 1152]
                    v = lambda g, t: vd4[:, g, t, DD * i:DD * i + DD]
                    for g in range(NDIL):
                        pe.matmul(b[:, 0:DD], s[:, 384 * g:384 * g + P], v(g, 0), start=g == 0, stop=g == NDIL - 1)
                    for g in range(NDIL):
                        for k in range(2):
                            ins = pe.matmul(b[:, DD:2 * DD], s[:, 384 * g + P * (k + 1):384 * g + P * (k + 2)], v(g, k),
                                            start=g == 0 and k == 0, stop=g == NDIL - 1 and k == 1)
                    ins.then_inc(sem("score_ready"), 1)
            pe.wait_ge(sem("ya_rows"), 1)
            for k in range(2):
                turn("ya", ktiles(ya, DW)[4 * k:4 * k + 4])
            pe.wait_ge(sem("yss"), 2)
            job("so0")
            job("so1")
            is_turned("ya")
            job("ao0")
            job("ao1")
            pe.wait_ge(sem("m_sum"), 2)
            for g in range(4):
                turn("m", ktiles(m_tok)[4 * g:4 * g + 4])
            is_turned("m")
            job("wp0")
            job("wp1")


_INS = ["x", "mem", "positions", "g_mix", "w_in", "b_gate", "g_ckv", "w_ukv", "g_q_nope", "g_k_nope", "g_q_rope",
        "g_k_rope", "w_gla_gate", "b_gla_gate", "g_gla_out", "g_mem", "w_mem_kv", "g_q_mem", "g_k_mem", "w_o", "g_ffn",
        "w_up", "w_down", "positions_2", "norm_w_2", "w_in_2", "lam_re_2", "lam_im_2", "log_dt_2", "b_re_2", "b_im_2",
        "c_re_2", "c_im_2", "d_skip_2", "w_glu_2", "q_norm_w_2", "k_norm_w_2", "w_ssm_out_2", "w_attn_out_2", "w_o_2"]


def constants():
    p, k = np.arange(P)[:, None], np.arange(SEQ)[None, :]
    back = P + p - k
    masks = [np.where(back >= 0, 0.0, NEG)]
    for window, dil in ((128, 1), (512, 4), (2048, 16)):
        masks.append(np.where((back >= 0) & (back <= window) & (back % dil == 0), 0.0, NEG))
    j, i = np.arange(P)[:, None], np.arange(P)[None, :]
    levels = [((j // (2 * s) == i // (2 * s)) & (j % (2 * s) < s) & (i % (2 * s) >= s)) for s in LEVELS]
    levels.append(i == j)
    one = np.float32(1)
    inv1 = one / (np.float32(10000.0) ** (np.arange(0, ROPE, 2, dtype=np.float32) / np.float32(ROPE)))
    inv2 = np.float32(500000.0) ** (-np.arange(0, RD, 2, dtype=np.float32) / np.float32(RD))
    inv = np.concatenate([inv1, inv2]).astype(np.float32)
    return {
        "c_ident": np.eye(P, dtype=np.float32),
        "c_masks": np.stack(masks, 1).astype(np.float32),
        "c_levels": np.stack(levels, 1).astype(np.float32),
        "c_inv": np.ascontiguousarray(np.broadcast_to(inv, (P, inv.size))),
    }


def kernel(**inputs):
    import numpy as _np
    import concourse.bacc as _bacc
    from concourse import mybir as _mybir
    from concourse.bass_utils import run_bass_kernel_spmd as _run

    nc = _bacc.Bacc("TRN2", target_bir_lowering=False, num_devices=1)
    arrays, aps = {}, {}
    for name in _INS:
        arrays[f"in_{name}"] = _np.ascontiguousarray(inputs[name])
    for name, a in constants().items():
        arrays[f"in_{name}"] = a
    for name, a in arrays.items():
        aps[name[3:]] = nc.dram_tensor(name, a.shape, _mybir.dt.from_np(a.dtype), kind="ExternalInput").ap()
    out = nc.dram_tensor("out", (1, SEQ, DM), F32, kind="ExternalOutput").ap()
    build(nc, aps, out)
    r = _run(nc, [arrays], core_ids=[0])
    return r.results[0]["out"]
```

```python
from contextlib import ExitStack

import concourse.bass as bass
from concourse import mybir
import numpy as np

F32 = mybir.dt.float32
I32 = mybir.dt.int32
ACT = mybir.ActivationFunctionType
ALU = mybir.AluOpType
AX = mybir.AxisListType

P = 128
SEQ = 256
TT = SEQ // P
DM = 1024
KD = DM // P
EPS = 1e-6

MH, NOPE, ROPE, DV = 8, 128, 64, 128
QW = NOPE + ROPE
RANK = 256
GH, GK, GV, GR = 4, 128, 256, 16
EH, EQ, EV = 4, 64, 256
FF = 4 * DM
C_Q = 0
C_CKV = MH * QW
C_GQ = C_CKV + RANK + ROPE
C_GK = C_GQ + GH * GK
C_GV = C_GK + GH * GK
C_GA = C_GV + GH * GV
C_GR = C_GA + GR
C_MQ = C_GR + GH * GV
C_GATE = C_MQ + EH * EQ

SG, SP_, SN = 64, 16, 64
ST = SG // 2
CH = 128
NDIL, DH, DD = 3, 8, 64
DW = DH * DD
RD = DD // 4
C_US = 0
C_ZS = DM
C_DQ = 2 * DM
C_DK = C_DQ + NDIL * DW
C_DVV = C_DK + NDIL * DW
C_ZA = C_DVV + NDIL * DW
C_RS = C_ZA + DW
C_RA = C_RS + DM

RING = 3
NEG = -1e30
ROUND = 12582912.0
TWO_PI_A = 6.28125
TWO_PI_B = 0.0019350051879882812
TWO_PI_C = 3.019916e-07
PI_IN = 3.1415925

COLS = {}
for _name, _n in (("g_mix", 8), ("g_mem", 8), ("g_ffn", 8), ("norm_w_2", 8), ("g_ckv", 2), ("g_q_nope", 1),
                  ("g_k_nope", 1), ("b_gla_gate", 4), ("d_skip_2", 8)):
    COLS[_name] = (sum(n for _, n in COLS.values()), _n)
NCOLS = sum(n for _, n in COLS.values())

GAINS = (("g_q_rope", 64), ("g_k_rope", 64), ("g_q_mem", 64), ("g_k_mem", 64), ("g_gla_out", 256),
         ("q_norm_w_2", 192), ("k_norm_w_2", 192))
LEVELS = (64, 32, 16, 8, 4, 2, 1)
T_LANE = 44
T_C = T_LANE + 8


def jobs_table():
    j = [("ckv", "w_in", C_CKV, RANK + ROPE), ("gq", "w_in", C_GQ, 512), ("gk", "w_in", C_GK, 512),
         ("ga", "w_in", C_GA, GR), ("gg", None, 0, 0)]
    j += [(f"q{i}", "w_in", C_Q + 512 * i, 512) for i in range(3)]
    j += [(f"kv{i}", "w_ukv", 512 * i, 512) for i in range(4)]
    j += [(f"gv{i}", "w_in", C_GV + 512 * i, 512) for i in range(2)]
    j += [(f"gr{i}", "w_in", C_GR + 512 * i, 512) for i in range(2)]
    j += [("mq", "w_in", C_MQ, 256), ("mk", "w_mem_kv", 0, 256)]
    j += [(f"mv{i}", "w_mem_kv", 256 + 512 * i, 512) for i in range(2)]
    j += [(f"gate{i}", "w_in", C_GATE + 512 * i, 512) for i in (0, 1, 4, 5, 2, 3)]
    j += [(f"wo{i}", "w_o", 512 * i, 512) for i in range(2)]
    out = [(n, n, w, 0, RANK if w == "w_ukv" else DM, c, m) for n, w, c, m in j]
    out += [(f"up{i}", f"up{i}", "w_up", 0, DM, 512 * i, 512) for i in range(8)]
    out += [(f"down{h}{k}", f"down{h}", "w_down", DM * k, DM, 512 * h, 512) for k in range(4) for h in range(2)]
    j = [(f"us{i}", "w_in_2", C_US + 512 * i, 512) for i in range(2)]
    j += [(f"dv{g}", "w_in_2", C_DVV + DW * g, DW) for g in range(NDIL)]
    j += [(f"zs{i}", "w_in_2", C_ZS + 512 * i, 512) for i in range(2)]
    j += [("za", "w_in_2", C_ZA, DW)]
    j += [(f"dq{g}", "w_in_2", C_DQ + DW * g, DW) for g in range(NDIL)]
    j += [(f"dk{g}", "w_in_2", C_DK + DW * g, DW) for g in range(NDIL)]
    j += [(f"rs{i}", "w_in_2", C_RS + 512 * i, 512) for i in range(2)]
    j += [(f"ra{i}", "w_in_2", C_RA + 512 * i, 512) for i in range(2)]
    j += [(f"glu{i}", "w_glu_2", 512 * i, 512) for i in range(2)]
    j += [(f"ao{i}", "w_attn_out_2", 512 * i, 512) for i in range(2)]
    j += [(f"so{i}", "w_ssm_out_2", 512 * i, 512) for i in range(2)]
    j += [(f"wp{i}", "w_o_2", 512 * i, 512) for i in range(2)]
    out += [(n, n, w, 0, DW if w == "w_attn_out_2" else DM, c, m) for n, w, c, m in j]
    return out


JOBS = jobs_table()
JOB = {job[0]: n for n, job in enumerate(JOBS)}
OUTS = list(dict.fromkeys(job[1] for job in JOBS))
LAST_JOB = {job[1]: job[0] for job in JOBS}
FIRST_JOB = {job[1]: job[0] for job in reversed(JOBS)}
BY_TOKENS = (("gate2", "gate3"), ("wo0", "wo1"), ("up0", "up1"), ("down03", "down13"), ("us0", "us1"), ("so0", "so1"),
             ("wp0", "wp1"))
HALVES = []
for _job in JOBS:
    _pair = next((x for x in BY_TOKENS if _job[0] in x), None)
    if _pair is None:
        HALVES += [(_job[0], 0), (_job[0], 1)]
    elif _job[0] == _pair[0]:
        HALVES += [(_n, _t) for _t in range(2) for _n in _pair]
BY_DVE = {"gg", "wo0", "wo1", "down0", "down1", "so0", "so1", "ao0", "ao1", "wp0", "wp1"} | {f"gate{i}" for i in range(6)}
SPLIT_TOKENS = ("up0", "up1", "us0", "us1")
CHANNEL_MAJOR = {"gq", "gk", "ga", "us0", "us1", "zs0", "zs1", "glu0", "glu1"} | {f"up{i}" for i in range(8)}
STREAMED = [n for n, job in enumerate(JOBS) if job[2]]
GATES = (0, 1, 4, 5, 2, 3)


def done(name, half):
    return HALVES.index((name, half)) + 1


def taken(name):
    own = {"wo0": ("residual", 3), "wo1": ("residual", 4), "down0": ("residual", 7), "down1": ("residual", 8),
           "gate2": ("gate_in", 3), "gate3": ("gate_in", 4)}
    if name in own:
        return own[name]
    by_dve = name in BY_DVE
    return ("taken_dve" if by_dve else "taken_act",
            sum(o not in own and (o in BY_DVE) == by_dve for o in OUTS[:OUTS.index(name) + 1]))


def build(nc, d, out):
    with ExitStack() as ctx:
        def sb(name, shape, dt=F32):
            return ctx.enter_context(nc.sbuf_tensor(name, shape, dt))

        sems = {}

        def sem(name):
            if name not in sems:
                sems[name] = ctx.enter_context(nc.semaphore(name))
            return sems[name]

        ident = sb("ident", [P, P])
        masks = sb("masks", [P, 1 + NDIL, SEQ])
        pcol = sb("pcol", [P, NCOLS])
        prow = sb("prow", [NCOLS, P])
        inv = sb("inv", [P, 40])
        ring = sb("ring", [P, RING, KD * 512])
        hT = sb("hT", [P, KD, SEQ])
        xres = sb("xres", [P, TT, DM])
        st = sb("stats", [P, 400])
        gains = sb("gains", [P, sum(w for _, w in GAINS)])
        rope = sb("rope", [P, 2, TT, 40])
        posi = sb("posi", [P, 2 * TT], I32)
        posf = sb("posf", [P, 2 * TT])
        carry = sb("carry", [P, 4])
        AR = 33700
        arena = sb("arena", [P, AR])

        gain, at = {}, 0
        for name, w in GAINS:
            gain[name] = gains[:, at:at + w]
            at += w

        def col(name, i=0, n=1):
            a = COLS[name][0] + i
            return pcol[:, a:a + n]

        class Place:
            def __init__(self, at=0):
                self.at = at

            def __call__(self, n):
                a = self.at
                self.at += n
                assert self.at <= AR, self.at
                return arena[:, a:a + n]

        a1 = Place()
        mem_tok = a1(2048); o_mla = mem_tok
        memT = a1(2048)
        q_tok = a1(3072)
        vg, mq_tok, mk_tok = q_tok[:, 0:2048], q_tok[:, 2048:2560], q_tok[:, 2560:3072]
        kv_tok = a1(4096)
        vm, gate_buf = kv_tok[:, 0:2048], kv_tok[:, 2048:4096]
        qnT = a1(2048); o_gla = qnT
        qpT = a1(1024)
        kmT, qmT = qpT[:, 0:512], qpT[:, 512:1024]
        knT = a1(2048); o_mem = knT
        kpeT = a1(256)
        kpe = a1(256)
        ckv = a1(640)
        ckvT = a1(512)
        qgT, kgT, bT, dec = a1(1024), a1(1024), a1(1024), a1(1024)
        qdec, kdec = a1(1024), a1(1024)
        amat = a1(1024); qpe = amat
        across = a1(512)
        r_gla = a1(2048); xn1 = r_gla
        soft = a1(1024)
        softT = a1(1024)
        aT = a1(256)
        wgate = a1(512)
        junk = a1(1024)

        levels = a1(192)
        adiag = a1(256)
        bgate = a1(1024)

        a2 = Place()
        cs = a2(ST * 2 * CH)
        bt = a2(2048)
        cc = a2(2048)
        lane = a2(288)
        p2 = a2.at
        hup = a2(8192)
        xn2 = a2(2048)
        bnat = a2(1024)
        bexp = a2(2048)
        cnat = a2(2048)
        srow = a2(1536)
        tmp_cs = a2(4096)

        a3 = Place(p2)
        uT = a3(2048)
        zs = a3(2048); xn3 = zs
        za = a3(1024)
        vd = a3(3072)
        at_qk = a3.at
        qdT = a3(3072)
        kdT = a3(3072)
        hst = arena[:, at_qk:at_qk + 8 * 512]
        at_work = a3.at
        raw = a3(1024)
        raw2 = a3(1024)
        wrot = a3(1024)
        gst = a3(1024)
        hrot = a3(1024)
        a4 = Place()
        dsoft = a4(2304)
        dsoftT = a4(2304)
        ya = a4(1024)
        gz = a4(2048)
        sig_glu = a4(2048); yssT = sig_glu
        yaT = a4(1024)
        assert a4.at <= p2
        a5 = Place(at_work)
        m_tok, rsig, asig = a5(2048), a5(2048), a5(2048)

        lam = {}
        for i, name in enumerate(("cos", "sin", "mag", "fre", "fim", "ere", "eim", "sq", "sq2")):
            lam[name] = lane[:, 32 * i:32 * i + 32]

        pair = [ctx.enter_context(nc.psum_tensor(f"pair{i}", [P, 1024], F32)) for i in range(2)]
        bank = {k: [ctx.enter_context(nc.psum_tensor(f"{k}{i}", [P, 512], F32)) for i in range(2)]
                for k in ("turned", "score")}

        block = ctx.enter_context(nc.Block())
        small = {}

        @block.sync
        def _(sp):
            for t in range(TT):
                sp.dma_start(xres[:, t, :], d["x"][0, P * t:P * t + P, :]).then_inc(sem(f"x_in{t}"), 16)
            for n, j in enumerate(STREAMED):
                name, _, w, r0, rows, c0, cols = JOBS[j]
                slot = n % RING
                if n >= RING:
                    sp.wait_ge(sem("half_done"), done(JOBS[STREAMED[n - RING]][0], 1))
                dst = ring[:, slot, 0:rows // P * cols].rearrange("p (k n) -> p k n", n=cols)
                src = d[w][0, r0:r0 + rows, c0:c0 + cols].rearrange("(k p) n -> p k n", p=P)
                sp.dma_start(dst, src).then_inc(sem(f"weights{slot}"), 16)
            for t in range(TT):
                for i in range(2):
                    sp.wait_ge(sem("result"), 2 * t + i + 1)
                    sp.dma_start(out[0, P * t:P * t + P, 512 * i:512 * i + 512],
                                 xres[:, t, 512 * i:512 * i + 512]).then_inc(sem("stored"), 16)
            sp.wait_ge(sem("stored"), 64)

        @block.gpsimd
        def _(pool):
            count = [0]

            def link(ins):
                count[0] += 1
                ins.then_inc(sem("pool_step"), 1)
                pool.wait_ge(sem("pool_step"), count[0])

            pool.dma_start(ident[:, :], d["c_ident"]).then_inc(sem("ident_in"), 16)
            for name, (a, n) in COLS.items():
                pool.dma_start(prow[a:a + n, :], d[name].rearrange("o (a b) -> (o a) b", b=P)).then_inc(sem("rows_in"), 16)
            pool.dma_start(masks[:, :, :], d["c_masks"]).then_inc(sem("consts_in"), 16)
            pool.dma_start(levels.rearrange("p (l n) -> p l n", n=32), d["c_levels"]).then_inc(sem("consts_in"), 16)
            pool.dma_start(inv[:, :], d["c_inv"]).then_inc(sem("consts_in"), 16)
            for i, name in enumerate(("positions", "positions_2")):
                for t in range(TT):
                    pool.dma_start(posi[:, TT * i + t:TT * i + t + 1],
                                   d[name][:, P * t:P * t + P].rearrange("o (p a) -> (o p) a", a=1)).then_inc(sem("consts_in"), 16)
            pool.dma_start(wgate[0:GR, :], d["w_gla_gate"][0]).then_inc(sem("consts_in"), 16)
            for name, w in GAINS:
                src = d[name].rearrange("o a b -> o (a b)") if len(d[name].shape) == 3 else d[name]
                pool.dma_start(gain[name], src.to_broadcast([P, w])).then_inc(sem("consts_in"), 16)
            for n, i in enumerate(GATES):
                if n >= 2:
                    pool.wait_ge(sem("taken_dve"), taken(f"gate{GATES[n - 2]}")[1])
                pool.dma_start(bgate[:, 512 * (n % 2):512 * (n % 2) + 512],
                               d["b_gate"][:, 512 * i:512 * i + 512].to_broadcast([P, 512])).then_inc(sem(f"bgate{n % 2}"), 16)

            pool.wait_ge(sem("residual"), taken("wo1")[1])
            link(pool.memset(bexp, 0.0))
            for i, name in enumerate(("b_re_2", "b_im_2")):
                pool.dma_start(bnat[:, 512 * i:512 * i + 512].rearrange("p (j c) -> p j c", c=SP_),
                               d[name][0].rearrange("(j a) n c -> (a n) j c", a=2)).then_inc(sem("ssm_in"), 16)
            for i, name in enumerate(("c_re_2", "c_im_2")):
                for half in range(2):
                    pool.dma_start(cnat[:, 1024 * i:1024 * i + 1024].rearrange("p (j h n) -> p j h n", h=2, n=SN)[:, :, half, :],
                                   d[name][0].rearrange("(j g) c n -> (g c) j n", g=8)).then_inc(sem("ssm_in"), 16)
            pool.dma_start(srow[0:ST, 0:128], d["lam_re_2"][0].rearrange("(j a) n -> j (a n)", a=2)).then_inc(sem("ssm_in"), 16)
            pool.dma_start(srow[0:ST, 128:256], d["lam_im_2"][0].rearrange("(j a) n -> j (a n)", a=2)).then_inc(sem("ssm_in"), 16)
            pool.dma_start(srow[0:ST, 256:258], d["log_dt_2"][0:1, :].rearrange("o (j a) -> (o j) a", a=2)).then_inc(sem("ssm_in"), 16)
            pool.wait_ge(sem("ssm_in"), 16 * 9)
            for i in range(2):
                for a in range(2):
                    last = pool.tensor_copy(
                        bexp[64 * a:64 * a + 64, 1024 * i:1024 * i + 1024].rearrange("p (j h c) -> p j h c", h=2, c=SP_)[:, :, a, :],
                        bnat[64 * a:64 * a + 64, 512 * i:512 * i + 512].rearrange("p (j c) -> p j c", c=SP_))
                    last.then_inc(sem("bexp_ready"), 1)

            for j in range(ST):
                pool.wait_ge(sem("g_ready"), j + 1)
                g = gst[:, 512 * (j % 2):512 * (j % 2) + 512]
                gv = g.rearrange("p (c t) -> p c t", t=CH)
                tab = cs.rearrange("p (j r t) -> p j r t", r=2, t=CH)[:, j]
                n1, n2 = hrot[:, 0:512], hrot[:, 512:1024]
                h = hst[:, 512 * (j % 8):512 * (j % 8) + 512]
                pool.tensor_tensor(n1.rearrange("p (c t) -> p c t", t=CH), gv,
                                   tab[:, 0:1, :].to_broadcast([P, 4, CH]), ALU.mult).then_inc(sem("pool_step"), 1)
                pool.tensor_tensor(n2.rearrange("p (c t) -> p c t", t=CH), gv,
                                   tab[:, 1:2, :].to_broadcast([P, 4, CH]), ALU.mult).then_inc(sem("pool_step"), 1)
                count[0] += 2
                pool.wait_ge(sem("pool_step"), count[0])
                pool.tensor_tensor(h[:, 0:256], n1[:, 0:256], n2[:, 256:512], ALU.subtract).then_inc(sem("h_ready"), 1)
                pool.tensor_tensor(h[:, 256:512], n1[:, 256:512], n2[:, 0:256], ALU.add).then_inc(sem("h_ready"), 1)
                pool.wait_ge(sem("h_ready"), 2 * j + 2)

        @block.scalar
        def _(act):
            n_out, n_turn, count = [0], [0], [0]

            def link(ins):
                count[0] += 1
                ins.then_inc(sem("act_step"), 1)
                act.wait_ge(sem("act_step"), count[0])

            def arrived(name, half=1):
                act.wait_ge(sem("half_done"), done(LAST_JOB[name], half))
                return pair[OUTS.index(name) % 2]

            def take(name, dst, func=ACT.Copy, scale=1.0, cols=512):
                for t in range(TT):
                    p = arrived(name, 1 if name in SPLIT_TOKENS else t)
                    ins = act.activation(dst(t), p[:, 512 * t:512 * t + cols], func, scale=scale)
                ins.then_inc(sem("taken_act"), 1)

            def turned(dst, n, scale=None, rows=P):
                i = n_turn[0]
                n_turn[0] += 1
                act.wait_ge(sem("turned_ready"), i + 1)
                src = bank["turned"][i % 2][0:rows, 0:n]
                if scale is None:
                    act.activation(dst, src, ACT.Copy).then_inc(sem("turned_taken"), 1)
                else:
                    w = n // len(scale)
                    for k, s in enumerate(scale):
                        ins = act.activation(dst[:, w * k:w * k + w], src[:, w * k:w * k + w], ACT.Copy, scale=s)
                    ins.then_inc(sem("turned_taken"), 1)

            def root(lo, n, name):
                act.wait_ge(sem(name + "_var"), root.seen.setdefault(name, 0) + 1)
                root.seen[name] += 1
                link(act.activation(st[:, lo + n:lo + 2 * n], st[:, lo:lo + n], ACT.Ln))
                act.activation(st[:, lo + n:lo + 2 * n], st[:, lo + n:lo + 2 * n], ACT.Exp, scale=-0.5).then_inc(sem(name + "_guess"), 1)
            root.seen = {}

            act.dma_start(mem_tok.rearrange("p (t c) -> p t c", c=DM), d["mem"][0].rearrange("(t p) c -> p t c", p=P)).then_inc(sem("mem_in"), 16)

            def row_norm(t, src, lo, name, sink):
                act.activation(sink, src, ACT.Square, accum_out=st[:, 280 + lo // 2 + t:281 + lo // 2 + t]).then_inc(sem(name + "_ss"), 1)
                root(lo + 2 * t, 1, name)

            def turned_rows(t, dst, gain_name=None):
                for g in range(2):
                    i = n_turn[0]
                    n_turn[0] += 1
                    act.wait_ge(sem("turned_ready"), i + 1)
                    src = bank["turned"][i % 2][:, :].rearrange("p (k n) -> p k n", n=P)
                    if gain_name is None:
                        ins = act.activation(dst[:, 4 * g:4 * g + 4, P * t:P * t + P], src, ACT.Copy)
                    else:
                        for k in range(4):
                            ins = act.activation(dst[:, 4 * g + k, P * t:P * t + P], src[:, k, :], ACT.Copy,
                                                 scale=col(gain_name, 4 * g + k))
                    ins.then_inc(sem("turned_taken"), 1)

            memT3 = memT.rearrange("p (k n) -> p k n", n=SEQ)
            for t in range(TT):
                act.wait_ge(sem(f"x_in{t}"), 16)
                row_norm(t, xres[:, t, :], 0, "x", junk)
                if t == 0:
                    turned(pcol[:, :], NCOLS)
                    act.wait_ge(sem("turned_taken"), 1)
                turned_rows(t, hT, "g_mix")
            act.wait_ge(sem("mem_in"), 16)
            for t in range(TT):
                row_norm(t, mem_tok[:, DM * t:DM * t + DM], 4, "mem", junk)
            act.wait_ge(sem("angle"), 1)
            link(act.activation(rope[:, 1, :, :], rope[:, 1, :, :], ACT.Sin))
            act.activation(rope[:, 0, :, :], rope[:, 0, :, :], ACT.Sin).then_inc(sem("rope_ready"), 1)
            ck = ckv.rearrange("p (t c) -> p t c", c=RANK + ROPE)
            take("ckv", lambda t: ck[:, t, :], cols=RANK + ROPE)
            for t in range(TT):
                turned_rows(t, memT3, "g_mem")
            take("gq", lambda t: qgT[:, 512 * t:512 * t + 512], scale=GK ** -0.5)
            take("gk", lambda t: kgT[:, 512 * t:512 * t + 512])
            p = arrived("ga")
            act.activation(aT[0:GR, :], p[0:GR, 0:SEQ], ACT.Copy).then_inc(sem("taken_act"), 1)
            root(8, 4, "ckv")
            turned(ckvT, 512, [col("g_ckv", 0), col("g_ckv", 1)])
            turned(kpeT, 256)
            act.wait_ge(sem("taken_dve"), taken("gg")[1])
            link(act.activation(dec, bT, ACT.Abs))
            link(act.activation(dec, dec, ACT.Exp, scale=-1.0))
            act.activation(dec, dec, ACT.Ln, bias=1.0).then_inc(sem("gate_ln"), 1)
            q3 = q_tok.rearrange("p (t c) -> p t c", c=MH * QW)
            for i in range(3):
                take(f"q{i}", lambda t: q3[:, t, 512 * i:512 * i + 512])
            k3 = kv_tok.rearrange("p (t c) -> p t c", c=MH * (NOPE + DV))
            for i in range(4):
                take(f"kv{i}", lambda t: k3[:, t, 512 * i:512 * i + 512])
            root(16, 32, "q")
            for g in range(4):
                turned(qnT[:, 512 * g:512 * g + 512], 512, [col("g_q_nope")])
            for g in range(2):
                turned(qpT[:, 512 * g:512 * g + 512], 512)
            root(80, 16, "k")
            for g in range(4):
                turned(knT[:, 512 * g:512 * g + 512], 512, [col("g_k_nope")])

            vg3 = vg.rearrange("p (t c) -> p t c", c=DM)
            rg3 = r_gla.rearrange("p (t c) -> p t c", c=DM)

            def exps(tag, n, parts):
                act.wait_ge(sem(tag + "_scores"), n + 1)
                for k, (a, w, t) in enumerate(parts):
                    s = (soft if tag != "dil" else dsoft)
                    half = (512 if tag != "dil" else 1152) * (n % 2)
                    ins = act.activation(s[:, half + a:half + a + w], s[:, half + a:half + a + w], ACT.Exp,
                                         bias=st[:, 340 + 2 * (n % 4) + t:341 + 2 * (n % 4) + t],
                                         accum_out=st[:, 350 + 2 * (n % 4) + t:351 + 2 * (n % 4) + t])
                ins.then_inc(sem(tag + "_exp"), 1)

            take("gv0", lambda t: vg3[:, t, 0:512])
            mq3 = mq_tok.rearrange("p (t c) -> p t c", c=EH * EQ)
            mk3 = mk_tok.rearrange("p (t c) -> p t c", c=EH * EQ)
            for h in range(MH + 2):
                if h == 1:
                    take("gv1", lambda t: vg3[:, t, 512:1024])
                if h in (3, 5):
                    i = (h - 3) // 2
                    take(f"gr{i}", lambda t: rg3[:, t, 512 * i:512 * i + 512])
                if h == 7:
                    take("mq", lambda t: mq3[:, t, :], cols=256)
                if h == 9:
                    take("mk", lambda t: mk3[:, t, :], cols=256)
                if 1 <= h <= MH:
                    turned(softT[:, 512 * ((h - 1) % 2):512 * ((h - 1) % 2) + 384], 384)
                if h < MH:
                    exps("mla", h, ((0, 128, 0), (128, 256, 1)))
            root(144, 16, "m")
            for t in range(TT):
                if t:
                    act.wait_ge(sem("silu_done"), t)
                act.activation(junk, rg3[:, t, :], ACT.Sigmoid).then_inc(sem("silu_sig"), 1)
            turned(qmT, 512)
            turned(kmT, 512)
            vm3 = vm.rearrange("p (t c) -> p t c", c=DM)
            take("mv0", lambda t: vm3[:, t, 0:512])

            def gate_sigmoid(n, half=None):
                g = gate_buf[:, 1024 * (n % 2):1024 * (n % 2) + 1024]
                if half is not None:
                    act.wait_ge(sem("gate_in"), 2 * half + n - 3)
                    g = g[:, 512 * half:512 * half + 512]
                else:
                    act.wait_ge(sem("taken_dve"), taken(f"gate{GATES[n]}")[1])
                act.activation(g, g, ACT.Sigmoid).then_inc(sem("gate_sig"), 1)

            def level_exp(lv):
                act.wait_ge(sem("level_diff"), lv + 1)
                act.activation(dec, dec, ACT.Exp, scale=1.0 / 16.0).then_inc(sem("level_exp"), 1)

            for i in range(9):
                if i < 8:
                    level_exp(i)
                if i == 2:
                    take("mv1", lambda t: vm3[:, t, 512:1024])
                if 1 <= i <= EH:
                    turned(softT[:, 512 * ((i - 1) % 2):512 * ((i - 1) % 2) + 512], 512)
                if i < EH:
                    exps("mem", i, ((0, 256, 0), (256, 256, 1)))
                if i in (4, 6, 8):
                    gate_sigmoid((i - 4) // 2)
            gate_sigmoid(3)
            root(176, 8, "og")
            for t in range(TT):
                gate_sigmoid(4, t)
                gate_sigmoid(5, t)
                turned_rows(t, hT)

            for t in range(TT):
                act.wait_ge(sem("residual"), 2 * t + 2)
                row_norm(t, xres[:, t, :], 0, "x", hup[:, 0:1024])
                turned_rows(t, hT, "g_ffn")
            R = srow[0:ST, :].rearrange("p (k n) -> p k n", n=128)
            for i in range(8):
                take(f"up{i}", lambda t: hup[:, 1024 * i + 512 * t:1024 * i + 512 * t + 512], func=ACT.Relu)
                if i == 0:
                    act.wait_ge(sem("ssm_in"), 16 * 9)
                    act.activation(srow[0:ST, 258:260], srow[0:ST, 256:258], ACT.Exp).then_inc(sem("dt_ready"), 1)
                    act.wait_ge(sem("theta"), 1)
                    link(act.activation(R[:, 3, :], R[:, 3, :], ACT.Exp))
                    link(act.activation(R[:, 5, :], R[:, 5, :], ACT.Sin))
                    act.activation(R[:, 4, :], R[:, 4, :], ACT.Sin).then_inc(sem("trig"), 1)
                if i == 2:
                    turned(lane[:, 0:160], 160)
                if i == 4:
                    for k in range(4):
                        turned(bt[:, 512 * k:512 * k + 512], 512)
            act.wait_ge(sem("tables"), 1)
            for k in range(4):
                turned(tmp_cs[:, 512 * k:512 * k + 512], 512)

            for t in range(TT):
                act.wait_ge(sem("residual"), 2 * TT + 2 * t + 2)
                row_norm(t, xres[:, t, :], 0, "x", raw)
                turned_rows(t, hT, "norm_w_2")
            for i in range(2):
                take(f"us{i}", lambda t: uT[:, 1024 * i + 512 * t:1024 * i + 512 * t + 512])
            vd4 = vd.rearrange("p (g t c) -> p g t c", g=NDIL, t=TT)
            for g in range(NDIL):
                take(f"dv{g}", lambda t: vd4[:, g, t, :])
            for i in range(2):
                if i == 1:
                    act.wait_ge(sem("z_silu"), 1)
                p = arrived(f"zs{i}")
                for t in range(2):
                    act.activation(zs[:, 1024 * i + 512 * t:1024 * i + 512 * t + 512], p[:, 512 * t:512 * t + 512], ACT.Copy)
                for t in range(2):
                    ins = act.activation(raw[:, 512 * t:512 * t + 512], p[:, 512 * t:512 * t + 512], ACT.Sigmoid)
                ins.then_inc(sem("taken_act"), 1)
            act.wait_ge(sem("z_silu"), 2)
            p = arrived("za")
            za3 = za.rearrange("p (t c) -> p t c", c=DW)
            for t in range(2):
                act.activation(za3[:, t, :], p[:, 512 * t:512 * t + 512], ACT.Copy)
            for t in range(2):
                ins = act.activation(raw[:, 512 * t:512 * t + 512], p[:, 512 * t:512 * t + 512], ACT.Sigmoid)
            ins.then_inc(sem("taken_act"), 1)
            for n in range(6):
                name = f"dq{n}" if n < 3 else f"dk{n - 3}"
                act.wait_ge(sem("z_silu"), 3)
                if n:
                    for _k in range(2):
                        turned((qdT if n - 1 < 3 else kdT)[:, 1024 * ((n - 1) % 3) + 512 * _k:1024 * ((n - 1) % 3) + 512 * _k + 512], 512)
                p = arrived(name)
                for t in range(2):
                    act.activation(raw[:, 512 * t:512 * t + 512], p[:, 512 * t:512 * t + 512], ACT.Copy)
                for t in range(2):
                    ins = act.activation(raw2[:, 512 * t:512 * t + 512], p[:, 512 * t:512 * t + 512], ACT.Square)
                ins.then_inc(sem("taken_act"), 1)
                root(192, 16, "dqk")
                if n == 2:
                    for i in range(2):
                        act.wait_ge(sem("gelu_z"), i + 1)
                        act.activation(gz[:, 1024 * i:1024 * i + 1024], gz[:, 1024 * i:1024 * i + 1024], ACT.Sigmoid,
                                       scale=1.5957691216057308).then_inc(sem("gelu_sig"), 1)
            take("rs0", lambda t: rsig[:, DM * t:DM * t + 512], func=ACT.Sigmoid)
            for k in range(2):
                turned(kdT[:, 2048 + 512 * k:2048 + 512 * k + 512], 512)
            for h in range(DH + 2):
                if h == 2:
                    take("rs1", lambda t: rsig[:, DM * t + 512:DM * t + 1024], func=ACT.Sigmoid)
                if h in (4, 6):
                    i = (h - 4) // 2
                    take(f"ra{i}", lambda t: asig[:, DM * t + 512 * i:DM * t + 512 * i + 512], func=ACT.Sigmoid)
                if h == 8:
                    take("glu0", lambda t: sig_glu[:, 512 * t:512 * t + 512], func=ACT.Sigmoid)
                if 1 <= h <= DH:
                    for g in range(NDIL):
                        b = 1152 * ((h - 1) % 2) + 384 * g
                        turned(dsoftT[:, b:b + 384], 384)
                if h < DH:
                    exps("dil", h, ((0, 384, 0), (384, 768, 1)))
            for k in range(2):
                turned(yaT[:, 512 * k:512 * k + 512], 512)
            take("glu1", lambda t: sig_glu[:, 1024 + 512 * t:1024 + 512 * t + 512], func=ACT.Sigmoid)
            for t in range(TT):
                turned_rows(t, hT)

        @block.vector
        def _(dve):
            count, n_score, own = [0], [0], {}

            def link(ins):
                count[0] += 1
                ins.then_inc(sem("dve_step"), 1)
                dve.wait_ge(sem("dve_step"), count[0])

            def mark(ins, name):
                own[name] = own.get(name, 0) + 1
                ins.then_inc(sem(name), 1)
                dve.wait_ge(sem(name), own[name])

            def arrived(name, half=1):
                dve.wait_ge(sem("half_done"), done(LAST_JOB[name], half))
                return pair[OUTS.index(name) % 2]

            def scored():
                i = n_score[0]
                n_score[0] += 1
                dve.wait_ge(sem("score_ready"), i + 1)
                return bank["score"][i % 2]

            def tt(o, a, b, op):
                return dve.tensor_tensor(o, a, b, op)

            def bc(x, shape):
                return x.to_broadcast(shape)

            def newton(lo, n, name):
                own[name + "_g"] = own.get(name + "_g", 0) + 1
                dve.wait_ge(sem(name + "_guess"), own[name + "_g"])
                v, y, a = st[:, lo:lo + n], st[:, lo + n:lo + 2 * n], st[:, 300:300 + n]
                link(tt(a, y, y, ALU.mult))
                link(tt(a, a, v, ALU.mult))
                link(dve.tensor_scalar(a, a, -0.5, 1.5, ALU.mult, ALU.add))
                link(tt(y, y, a, ALU.mult))

            def var(dst, src, n, name=None):
                ins = dve.tensor_scalar(dst, src, 1.0 / n, EPS, ALU.mult, ALU.add)
                if name:
                    mark(ins, name + "_var")
                else:
                    link(ins)

            def row_norm(t, src, dst, lo, name):
                own[name + "_s"] = own.get(name + "_s", 0) + 1
                dve.wait_ge(sem(name + "_ss"), own[name + "_s"])
                a = lo + 2 * t
                var(st[:, a:a + 1], st[:, 280 + lo // 2 + t:281 + lo // 2 + t], DM, name)
                newton(a, 1, name)
                mark(dve.tensor_scalar(dst, src, st[:, a + 1:a + 2], None, ALU.mult), name + "_rows")

            def reduce_angle(x, k, rows):
                link(dve.tensor_scalar(k, x, 1.0 / (2 * np.pi), ROUND, ALU.mult, ALU.add))
                link(dve.tensor_scalar(k, k, -ROUND, None, ALU.add))
                for part in (TWO_PI_A, TWO_PI_B, TWO_PI_C):
                    link(dve.scalar_tensor_tensor(x, k, -part, x, ALU.mult, ALU.add))
                link(dve.tensor_scalar(x, x, PI_IN, -PI_IN, ALU.min, ALU.max))
                link(dve.tensor_scalar(k, x, -1.0, None, ALU.mult))
                link(tt(k, k, x, ALU.min))
                return dve.tensor_scalar(k, k, np.pi / 2, None, ALU.add)

            link(dve.memset(st[:, 399:400], 1.0))
            for t in range(TT):
                row_norm(t, xres[:, t, :], xn1[:, DM * t:DM * t + DM], 0, "x")
            dve.wait_ge(sem("consts_in"), 16 * (8 + len(GAINS)))
            link(dve.tensor_copy(posf[:, :], posi[:, :]))
            ang, turns = rope[:, 1, :, :], rope[:, 0, :, :]
            for t in range(TT):
                link(dve.tensor_scalar(ang[:, t, 0:32], inv[:, 0:32], posf[:, t:t + 1], None, ALU.mult))
                link(dve.tensor_scalar(ang[:, t, 32:40], inv[:, 32:40], posf[:, TT + t:TT + t + 1], None, ALU.mult))
            mark(reduce_angle(ang, turns, P), "angle")
            for t in range(TT):
                row_norm(t, mem_tok[:, DM * t:DM * t + DM], mem_tok[:, DM * t:DM * t + DM], 4, "mem")

            dve.wait_ge(sem("taken_act"), taken("ckv")[1])
            ck = ckv.rearrange("p (t c) -> p t c", c=RANK + ROPE)
            for t in range(TT):
                link(tt(qdec[:, 0:320], ck[:, t, :], ck[:, t, :], ALU.mult))
                link(dve.tensor_reduce(st[:, 284 + t:285 + t], qdec[:, 0:RANK], AX.X, ALU.add))
                link(dve.tensor_reduce(st[:, 286 + t:287 + t], qdec[:, RANK:RANK + ROPE], AX.X, ALU.add))
            var(st[:, 8:10], st[:, 284:286], RANK)
            var(st[:, 10:12], st[:, 286:288], ROPE, "ckv")
            newton(8, 4, "ckv")
            for t in range(TT):
                mark(dve.tensor_scalar(ck[:, t, 0:RANK], ck[:, t, 0:RANK], st[:, 12 + t:13 + t], None, ALU.mult), "ckv_rows")
                link(dve.tensor_scalar(ck[:, t, RANK:RANK + ROPE], ck[:, t, RANK:RANK + ROPE], st[:, 14 + t:15 + t], None, ALU.mult))
            kr = ck[:, :, RANK:RANK + ROPE]
            link(tt(kr, kr, bc(gain["g_k_rope"].unsqueeze(1), [P, TT, ROPE]), ALU.mult))
            dve.wait_ge(sem("rope_ready"), 1)
            kp = kpe.rearrange("p (t c) -> p t c", c=2 * ROPE)
            cos_a, sin_a = rope[:, 0, :, 0:32], rope[:, 1, :, 0:32]
            tmp = [kdec[:, 64 * i:64 * i + 64].rearrange("p (t c) -> p t c", c=32) for i in range(4)]
            x1, x2 = kr[:, :, 0:32], kr[:, :, 32:64]
            link(tt(tmp[0], x1, cos_a, ALU.mult))
            link(tt(tmp[1], x2, sin_a, ALU.mult))
            link(tt(tmp[2], x1, sin_a, ALU.mult))
            link(tt(tmp[3], x2, cos_a, ALU.mult))
            for i in range(2):
                link(tt(kp[:, :, 64 * i:64 * i + 32], tmp[0], tmp[1], ALU.subtract))
                mark(tt(kp[:, :, 64 * i + 32:64 * i + 64], tmp[2], tmp[3], ALU.add), "kpe_rows")

            p = arrived("gg")
            b4 = bT.rearrange("p (h s) -> p h s", s=SEQ)
            for i in range(2):
                ins = tt(b4[:, 2 * i:2 * i + 2, :], p[:, 512 * i:512 * i + 512].rearrange("p (h s) -> p h s", s=SEQ),
                         bc(col("b_gla_gate", 2 * i, 2).unsqueeze(2), [P, 2, SEQ]), ALU.add)
            mark(ins, "taken_dve")
            dve.wait_ge(sem("gate_ln"), 1)
            link(dve.scalar_tensor_tensor(dec, bT, 0.0, dec, ALU.min, ALU.subtract))
            for i in range(2 * GH):
                link(dve.tensor_tensor_scan(bT[:, P * i:P * i + P], bc(st[:, 399:400], [P, P]), dec[:, P * i:P * i + P],
                                            0.0, ALU.mult, ALU.add))

            dve.wait_ge(sem("taken_act"), taken("q2")[1])
            for t in range(TT):
                qt = q_tok[:, MH * QW * t:MH * QW * (t + 1)]
                link(tt(knT[:, 0:1536], qt, qt, ALU.mult))
                s3 = knT[:, 0:1536].rearrange("p (h c) -> p h c", c=QW)
                link(dve.tensor_reduce(st[:, 16 + 8 * t:24 + 8 * t], s3[:, :, 0:NOPE], AX.X, ALU.add))
                link(dve.tensor_reduce(st[:, 32 + 8 * t:40 + 8 * t], s3[:, :, NOPE:QW], AX.X, ALU.add))
            var(st[:, 16:32], st[:, 16:32], NOPE)
            var(st[:, 32:48], st[:, 32:48], ROPE, "q")
            newton(16, 32, "q")
            q16 = q_tok.rearrange("p (g c) -> p g c", c=QW)
            mark(tt(q16[:, :, 0:NOPE], q16[:, :, 0:NOPE], bc(st[:, 48:64].unsqueeze(2), [P, 16, NOPE]), ALU.mult), "q_rows")
            link(tt(q16[:, :, NOPE:QW], q16[:, :, NOPE:QW], bc(st[:, 64:80].unsqueeze(2), [P, 16, ROPE]), ALU.mult))
            link(tt(q16[:, :, NOPE:QW], q16[:, :, NOPE:QW], bc(gain["g_q_rope"].unsqueeze(1), [P, 16, ROPE]), ALU.mult))
            q4 = q_tok.rearrange("p (t h c) -> p t h c", t=TT, c=QW)
            x1, x2 = q4[:, :, :, NOPE:NOPE + 32], q4[:, :, :, NOPE + 32:QW]
            cosb = bc(cos_a.unsqueeze(2), [P, TT, MH, 32])
            sinb = bc(sin_a.unsqueeze(2), [P, TT, MH, 32])
            tmp = [(qdec, kdec)[i // 2][:, 512 * (i % 2):512 * (i % 2) + 512].rearrange("p (t h c) -> p t h c", t=TT, c=32)
                   for i in range(4)]
            link(tt(tmp[0], x1, cosb, ALU.mult))
            link(tt(tmp[1], x2, sinb, ALU.mult))
            link(tt(tmp[2], x1, sinb, ALU.mult))
            link(tt(tmp[3], x2, cosb, ALU.mult))
            qp4 = qpe.rearrange("p (t h c) -> p t h c", t=TT, c=ROPE)
            link(tt(qp4[:, :, :, 0:32], tmp[0], tmp[1], ALU.subtract))
            mark(tt(qp4[:, :, :, 32:64], tmp[2], tmp[3], ALU.add), "qpe_rows")

            dve.wait_ge(sem("taken_act"), taken("kv3")[1])
            k16 = kv_tok.rearrange("p (g c) -> p g c", c=NOPE + DV)
            kn = k16[:, :, 0:NOPE]
            link(tt(knT.rearrange("p (g c) -> p g c", c=NOPE), kn, kn, ALU.mult))
            link(dve.tensor_reduce(st[:, 80:96], knT.rearrange("p (g c) -> p g c", c=NOPE), AX.X, ALU.add))
            var(st[:, 80:96], st[:, 80:96], NOPE, "k")
            newton(80, 16, "k")
            mark(tt(kn, kn, bc(st[:, 96:112].unsqueeze(2), [P, 16, NOPE]), ALU.mult), "k_rows")

            def scores(buf, n, parts, scale, name):
                for src, dst, mask, a in parts:
                    ins = dve.tensor_tensor_reduce(dst, src, mask, scale, -3e38, ALU.add, ALU.max, st[:, a:a + 1])
                return ins

            def minus(n, name):
                c = 340 + 2 * (n % 4)
                mark(dve.tensor_scalar(st[:, c:c + 2], st[:, c:c + 2], -1.0, None, ALU.mult), name + "_scores")

            def taken_score(ins):
                mark(ins, "score_taken")

            def attend(name, n, dst):
                p = scored()
                dve.wait_ge(sem(name + "_exp"), n + 1)
                c = 350 + 2 * (n % 4)
                link(dve.reciprocal(st[:, 360 + 2 * (n % 4):362 + 2 * (n % 4)], st[:, c:c + 2]))
                for t in range(TT):
                    o = dst(t)
                    w = o.shape[-1]
                    ins = dve.tensor_scalar(o, p[:, w * t:w * t + w], st[:, 360 + 2 * (n % 4) + t:361 + 2 * (n % 4) + t], None, ALU.mult)
                    if t == 0:
                        link(ins)
                mark(ins, "score_taken")

            om3 = o_mla.rearrange("p (t c) -> p t c", c=DM)
            for h in range(MH + 2):
                if h < MH:
                    p = scored()
                    s = soft[:, 512 * (h % 2):512 * (h % 2) + 512]
                    c = 340 + 2 * (h % 4)
                    link(scores(s, h, ((p[:, 0:128], s[:, 0:128], masks[:, 0, 128:256], c),), QW ** -0.5, None))
                    taken_score(scores(s, h, ((p[:, 128:384], s[:, 128:384], masks[:, 0, :], c + 1),), QW ** -0.5, None))
                    minus(h, "mla")
                if h >= 2:
                    attend("mla", h - 2, lambda t: om3[:, t, DV * (h - 2):DV * (h - 1)])

            dve.wait_ge(sem("taken_act"), taken("mk")[1])
            for i, (x, g) in enumerate(((mq_tok, "g_q_mem"), (mk_tok, "g_k_mem"))):
                x8 = x.rearrange("p (g c) -> p g c", c=EQ)
                q8 = qdec[:, 0:512].rearrange("p (g c) -> p g c", c=EQ)
                link(tt(q8, x8, x8, ALU.mult))
                link(dve.tensor_reduce(st[:, 144 + 8 * i:152 + 8 * i], q8, AX.X, ALU.add))
            var(st[:, 144:160], st[:, 144:160], EQ, "m")
            newton(144, 16, "m")
            for i, (x, g) in enumerate(((mq_tok, "g_q_mem"), (mk_tok, "g_k_mem"))):
                x8 = x.rearrange("p (g c) -> p g c", c=EQ)
                link(tt(x8, x8, bc(st[:, 160 + 8 * i:168 + 8 * i].unsqueeze(2), [P, 8, EQ]), ALU.mult))
                mark(tt(x8, x8, bc(gain[g].unsqueeze(1), [P, 8, EQ]), ALU.mult), "m_rows")

            rg3 = r_gla.rearrange("p (t c) -> p t c", c=DM)
            for t in range(TT):
                dve.wait_ge(sem("silu_sig"), t + 1)
                mark(tt(rg3[:, t, :], rg3[:, t, :], junk, ALU.mult), "silu_done")
                g4 = rg3[:, t, :].rearrange("p (h c) -> p h c", c=GV)
                link(tt(g4, g4, bc(gain["g_gla_out"].unsqueeze(1), [P, GH, GV]), ALU.mult))

            def level_diff(i):
                if i < len(LEVELS):
                    s = LEVELS[i]
                    b, dd = (x.rearrange("p (b u s) -> p b u s", u=2, s=s) for x in (bT, dec))
                    nb = 1024 // (2 * s)
                    ref = bc(b[:, :, 0, s - 1:s], [P, nb, s])
                    link(tt(dd[:, :, 0, :], ref, b[:, :, 0, :], ALU.subtract))
                    mark(tt(dd[:, :, 1, :], b[:, :, 1, :], ref, ALU.subtract), "level_diff")
                else:
                    b, dd = (x.rearrange("p (h t s) -> p h t s", t=TT, s=P) for x in (bT, dec))
                    link(tt(dd[:, :, 0, :], bc(b[:, :, 0, P - 1:P], [P, GH, P]), b[:, :, 0, :], ALU.subtract))
                    mark(dve.tensor_copy(dd[:, :, 1, :], b[:, :, 1, :]), "level_diff")

            om_mem = o_mem.rearrange("p (t c) -> p t c", c=DM)
            og3 = o_gla.rearrange("p (t c) -> p t c", c=DM)

            def gate_add(n, t):
                p = arrived(f"gate{GATES[n]}", t)
                dve.wait_ge(sem(f"bgate{n % 2}"), 16 * (n // 2 + 1))
                g = gate_buf[:, 1024 * (n % 2) + 512 * t:1024 * (n % 2) + 512 * t + 512]
                return tt(g, p[:, 512 * t:512 * t + 512], bgate[:, 512 * (n % 2):512 * (n % 2) + 512], ALU.add)

            def gate_take(n):
                link(gate_add(n, 0))
                mark(gate_add(n, 1), "taken_dve")

            def gate_apply(n, need):
                dve.wait_ge(sem("gate_sig"), need)
                i = GATES[n]
                o = (om3, og3, om_mem)[i // 2][:, :, 512 * (i % 2):512 * (i % 2) + 512]
                g = gate_buf[:, 1024 * (n % 2):1024 * (n % 2) + 1024].rearrange("p (t c) -> p t c", c=512)
                link(tt(o, o, g, ALU.mult))

            lv3 = levels.rearrange("p (l n) -> p l n", n=32)
            am3 = amat.rearrange("p (b n) -> p b n", n=P)
            ad3 = adiag.rearrange("p (b n) -> p b n", n=32)
            link(dve.memset(amat, 0.0))
            level_diff(0)
            for i in range(9):
                if i < 8:
                    dve.wait_ge(sem("level_exp"), i + 1)
                    link(tt(qdec, qgT, dec, ALU.mult))
                    mark(tt(kdec, kgT, dec, ALU.mult), "level_ready")
                    if i + 1 < 8:
                        level_diff(i + 1)
                if i < EH:
                    p = scored()
                    s = soft[:, 512 * (i % 2):512 * (i % 2) + 512]
                    c = 340 + 2 * (i % 4)
                    zero = bc(masks[:, 0, 0:1], [P, 256])
                    link(scores(s, i, ((p[:, 0:256], s[:, 0:256], zero, c),), EQ ** -0.5, None))
                    taken_score(scores(s, i, ((p[:, 256:512], s[:, 256:512], zero, c + 1),), EQ ** -0.5, None))
                    minus(i, "mem")
                if 2 <= i < EH + 2:
                    attend("mem", i - 2, lambda t: om_mem[:, t, EV * (i - 2):EV * (i - 1)])
                p = scored()
                if i == 7:
                    taken_score(dve.tensor_copy(across, p[:, :]))
                elif i == 0:
                    taken_score(dve.tensor_copy(am3[0:64, :, 64:128], p[0:64, :].rearrange("p (b n) -> p b n", n=64)))
                elif i == 1:
                    src = p[:, 0:256].rearrange("p (b n) -> p b n", n=32)
                    link(dve.tensor_copy(am3[0:32, :, 32:64], src[0:32]))
                    taken_score(dve.tensor_copy(am3[64:96, :, 96:128], src[64:96]))
                else:
                    k = i - 2 if i < 7 else 5
                    mask = bc(lv3[:, k:k + 1, :], [P, 8, 32])
                    src = p[:, 0:256].rearrange("p (b n) -> p b n", n=32)
                    if i == 2:
                        taken_score(tt(ad3, src, mask, ALU.mult))
                    else:
                        w = wgate[:, 0:256]
                        taken_score(tt(w.rearrange("p (b n) -> p b n", n=32), src, mask, ALU.mult))
                        link(tt(adiag, adiag, w, ALU.add))
                if i in (3, 5, 7, 8):
                    gate_take((i - 2) // 2)
                if i in (5, 7):
                    gate_apply((i - 5) // 2, (i - 5) // 2 + 1)
            for k in range(4):
                q = slice(32 * k, 32 * k + 32)
                mark(dve.tensor_copy(am3[q, :, q], ad3[q]), "amat")
            for n in range(4):
                p = scored()
                taken_score(dve.tensor_copy(og3[:, n // 2, 512 * (n % 2):512 * (n % 2) + 512], p[:, :]))
            for t in range(TT):
                link(tt(junk, og3[:, t, :], og3[:, t, :], ALU.mult))
                link(dve.tensor_reduce(st[:, 176 + 4 * t:180 + 4 * t], junk.rearrange("p (h c) -> p h c", c=GV), AX.X, ALU.add))
            var(st[:, 176:184], st[:, 176:184], GV, "og")
            newton(176, 8, "og")
            o8 = o_gla.rearrange("p (g c) -> p g c", c=GV)
            link(tt(o8, o8, bc(st[:, 184:192].unsqueeze(2), [P, 8, GV]), ALU.mult))
            link(tt(o_gla, o_gla, r_gla, ALU.mult))
            gate_apply(2, 3)
            gate_apply(3, 4)
            link(tt(o_mla, o_mla, o_mem, ALU.add))
            for t in range(TT):
                for n in (4, 5):
                    ins = gate_add(n, t)
                    mark(ins, "gate_in")
                for n in (4, 5):
                    c = 512 * (GATES[n] % 2)
                    g = gate_buf[:, 1024 * (n % 2) + 512 * t:1024 * (n % 2) + 512 * t + 512]
                    dve.wait_ge(sem("gate_sig"), 4 + 2 * t + n - 3)
                    link(tt(og3[:, t, c:c + 512], og3[:, t, c:c + 512], g, ALU.mult))
                    ins = tt(om3[:, t, c:c + 512], om3[:, t, c:c + 512], og3[:, t, c:c + 512], ALU.add)
                    mark(ins, "y_rows")

            def residual(name, i, t):
                p = arrived(name, t)
                x = xres[:, t, 512 * i:512 * i + 512]
                return tt(x, p[:, 512 * t:512 * t + 512], x, ALU.add)

            def residual_norm(names, dst):
                for t in range(TT):
                    for i in range(2):
                        mark(residual(names[i], i, t), "residual")
                    row_norm(t, xres[:, t, :], dst[:, DM * t:DM * t + DM], 0, "x")

            residual_norm(("wo0", "wo1"), xn2)

            R = srow[0:ST, :].rearrange("p (k n) -> p k n", n=128)
            lr, li, mag, cosr, sinr, kk, fre, fim, den, t1, t2 = (R[:, i, :] for i in (0, 1, 3, 4, 5, 6, 7, 8, 9, 10, 11))
            dve.wait_ge(sem("ssm_in"), 16 * 9)
            dve.wait_ge(sem("dt_ready"), 1)
            dtb = bc(srow[0:ST, 258:260].unsqueeze(2), [ST, 2, SN])
            h2 = lambda x: x.rearrange("p (a n) -> p a n", n=SN)
            link(tt(h2(mag), h2(lr), dtb, ALU.mult))
            link(tt(h2(sinr), h2(li), dtb, ALU.mult))
            mark(reduce_angle(sinr, cosr, ST), "theta")
            link(tt(t1, lr, lr, ALU.mult))
            link(tt(den, li, li, ALU.mult))
            link(tt(den, den, t1, ALU.add))
            link(dve.reciprocal(den, den))
            dve.wait_ge(sem("trig"), 1)
            link(tt(t1, mag, cosr, ALU.mult))
            link(tt(t2, mag, sinr, ALU.mult))
            link(dve.tensor_scalar(t1, t1, -1.0, None, ALU.add))
            link(tt(fre, t1, lr, ALU.mult))
            link(tt(kk, t2, li, ALU.mult))
            link(tt(fre, fre, kk, ALU.add))
            link(tt(fre, fre, den, ALU.mult))
            link(tt(fim, t2, lr, ALU.mult))
            link(tt(kk, t1, li, ALU.mult))
            link(tt(fim, fim, kk, ALU.subtract))
            mark(tt(fim, fim, den, ALU.mult), "lane_rows")

            dve.wait_ge(sem("turned_taken"), T_LANE)
            c4 = cs.rearrange("p (j r t) -> p j r t", r=2, t=CH)
            link(dve.memset(c4[:, :, 0, 0:1], 1.0))
            link(dve.memset(c4[:, :, 1, 0:1], 0.0))
            link(dve.tensor_copy(lam["ere"], lam["cos"]))
            link(dve.tensor_copy(lam["eim"], lam["sin"]))
            n = 1
            while n < CH:
                a, b = (tmp_cs[:, 2048 * i:2048 * i + 32 * n].rearrange("p (j t) -> p j t", t=n) for i in range(2))
                er, ei = (bc(lam[k].unsqueeze(2), [P, ST, n]) for k in ("ere", "eim"))
                pr, pi = c4[:, :, 0, 0:n], c4[:, :, 1, 0:n]
                link(tt(a, pr, er, ALU.mult))
                link(tt(b, pi, ei, ALU.mult))
                link(tt(c4[:, :, 0, n:2 * n], a, b, ALU.subtract))
                link(tt(a, pr, ei, ALU.mult))
                link(tt(b, pi, er, ALU.mult))
                link(tt(c4[:, :, 1, n:2 * n], a, b, ALU.add))
                link(tt(lam["sq"], lam["ere"], lam["ere"], ALU.mult))
                link(tt(lam["sq2"], lam["eim"], lam["eim"], ALU.mult))
                link(tt(lam["eim"], lam["ere"], lam["eim"], ALU.mult))
                link(dve.tensor_scalar(lam["eim"], lam["eim"], 2.0, None, ALU.mult))
                link(tt(lam["ere"], lam["sq"], lam["sq2"], ALU.subtract))
                n *= 2
            mark(dve.memset(cc, 0.0), "tables")

            for i in range(8):
                dve.wait_ge(sem("taken_act"), taken(f"up{i}")[1])
                u = hup[:, 1024 * i:1024 * i + 1024]
                mark(tt(u, u, u, ALU.mult), "ff_ready")

            dve.wait_ge(sem("turned_taken"), T_C)
            cr, ci = (tmp_cs[:, 1024 * i:1024 * i + 1024].rearrange("p (j c) -> p j c", c=32) for i in range(2))
            ta, tb = (tmp_cs[:, 2048 + 1024 * i:3072 + 1024 * i].rearrange("p (j c) -> p j c", c=32) for i in range(2))
            fr, fi = (bc(lam[k].unsqueeze(2), [P, ST, 32]) for k in ("fre", "fim"))
            for i in range(2):
                link(tt(ta, cr, (fr, fi)[i], ALU.mult))
                link(tt(tb, ci, (fi, fr)[i], ALU.mult))
                cv = cc[:, 1024 * i:1024 * i + 1024].rearrange("p (j c) -> p j c", c=32)
                for a in range(2):
                    q = slice(64 * a, 64 * a + 64)
                    w = slice(16 * a, 16 * a + 16)
                    if i == 0:
                        ins = tt(cv[q, :, w], ta[q, :, w], tb[q, :, w], ALU.subtract)
                    else:
                        ins = dve.scalar_tensor_tensor(cv[q, :, w], ta[q, :, w], -1.0, tb[q, :, w], ALU.mult, ALU.subtract)
                    mark(ins, "c_ready")

            residual_norm(("down0", "down1"), xn3)

            def z_silu(z):
                dve.wait_ge(sem("taken_act"), taken(z)[1])
                x = za if z == "za" else zs[:, 1024 * int(z[2]):1024 * int(z[2]) + 1024]
                mark(tt(x, x, raw, ALU.mult), "z_silu")

            def dqk(n):
                g = n % 3
                name, gn = (f"dq{g}", "q_norm_w_2") if n < 3 else (f"dk{g}", "k_norm_w_2")
                dve.wait_ge(sem("taken_act"), taken(name)[1])
                r16 = raw.rearrange("p (g c) -> p g c", c=DD)
                link(dve.tensor_reduce(st[:, 192:208], raw2.rearrange("p (g c) -> p g c", c=DD), AX.X, ALU.add))
                var(st[:, 192:208], st[:, 192:208], DD, "dqk")
                newton(192, 16, "dqk")
                link(tt(r16, r16, bc(st[:, 208:224].unsqueeze(2), [P, 16, DD]), ALU.mult))
                link(tt(r16, r16, bc(gain[gn][:, DD * g:DD * g + DD].unsqueeze(1), [P, 16, DD]), ALU.mult))
                r4 = raw.rearrange("p (t h c) -> p t h c", t=TT, c=DD)
                y1, y2 = r4[:, :, :, 0:8], r4[:, :, :, 8:16]
                cb, sb_ = (bc(rope[:, k, :, 32:40].unsqueeze(2), [P, TT, DH, 8]) for k in range(2))
                tm = [raw2[:, 128 * i:128 * i + 128].rearrange("p (t h c) -> p t h c", t=TT, c=8) for i in range(4)]
                link(tt(tm[0], y1, cb, ALU.mult))
                link(tt(tm[1], y2, sb_, ALU.mult))
                link(tt(tm[2], y2, cb, ALU.mult))
                link(tt(tm[3], y1, sb_, ALU.mult))
                link(tt(y1, tm[0], tm[1], ALU.subtract))
                mark(tt(y2, tm[2], tm[3], ALU.add), "dqk_rows")

            def ssm_out(i):
                u = uT[:, SEQ * i:SEQ * i + SEQ]
                p = scored()
                taken_score(dve.scalar_tensor_tensor(u, u, col("d_skip_2", i), p[:, 0:SEQ], ALU.mult, ALU.add))

            for j in range(ST):
                if True:
                    p = scored()
                    w4 = p[:, :].rearrange("p (c t) -> p c t", t=CH)
                    tab = c4[:, j]
                    m1, m2 = wrot[:, 0:512], wrot[:, 512:1024]
                    link(tt(m1.rearrange("p (c t) -> p c t", t=CH), w4, bc(tab[:, 0:1, :], [P, 4, CH]), ALU.mult))
                    taken_score(tt(m2.rearrange("p (c t) -> p c t", t=CH), w4, bc(tab[:, 1:2, :], [P, 4, CH]), ALU.mult))
                    link(tt(m1[:, 0:256], m1[:, 0:256], m2[:, 256:512], ALU.add))
                    link(tt(m1[:, 256:512], m1[:, 256:512], m2[:, 0:256], ALU.subtract))
                    g = gst[:, 512 * (j % 2):512 * (j % 2) + 512]
                    mg = bc(lam["mag"][:, j:j + 1], [P, CH])
                    if j >= 2:
                        dve.wait_ge(sem("h_ready"), 2 * (j - 1))
                    link(dve.tensor_tensor_scan(g[:, 0:CH], mg, m1[:, 0:CH], 0.0, ALU.mult, ALU.add))
                    link(dve.tensor_tensor_scan(g[:, 256:256 + CH], mg, m1[:, 256:256 + CH], 0.0, ALU.mult, ALU.add))
                    gr, gi = g[:, CH - 1:CH], g[:, 256 + CH - 1:256 + CH]
                    er, ei = lam["ere"][:, j:j + 1], lam["eim"][:, j:j + 1]
                    link(tt(carry[:, 0:1], gi, ei, ALU.mult))
                    link(tt(carry[:, 1:2], gr, ei, ALU.mult))
                    link(dve.scalar_tensor_tensor(carry[:, 2:3], gr, er, carry[:, 0:1], ALU.mult, ALU.subtract))
                    link(dve.scalar_tensor_tensor(carry[:, 3:4], gi, er, carry[:, 1:2], ALU.mult, ALU.add))
                    link(dve.tensor_tensor_scan(g[:, CH:256], mg, m1[:, CH:256], carry[:, 2:3], ALU.mult, ALU.add))
                    mark(dve.tensor_tensor_scan(g[:, 256 + CH:512], mg, m1[:, 256 + CH:512], carry[:, 3:4], ALU.mult, ALU.add), "g_ready")
                if j % 4 == 3 and j >= 7:
                    ssm_out(j // 4 - 1)
                if j in (16, 20, 24):
                    z_silu(("zs0", "zs1", "za")[(j - 16) // 4])
                if j == 29:
                    dqk(0)
            dqk(1)
            ssm_out(7)
            for i in range(2):
                y, z = uT[:, 1024 * i:1024 * i + 1024], gz[:, 1024 * i:1024 * i + 1024]
                link(tt(z, y, y, ALU.mult))
                link(dve.tensor_scalar(z, z, 0.044715, 1.0, ALU.mult, ALU.add))
                mark(tt(z, z, y, ALU.mult), "gelu_z")
            dqk(2)
            for i in range(2):
                dve.wait_ge(sem("gelu_sig"), i + 1)
                y, z = uT[:, 1024 * i:1024 * i + 1024], gz[:, 1024 * i:1024 * i + 1024]
                mark(tt(y, y, z, ALU.mult), "gelu_ready")
                link(tt(z, y, zs[:, 1024 * i:1024 * i + 1024], ALU.mult))
            for n in (3, 4, 5):
                dqk(n)

            ya3 = ya.rearrange("p (t c) -> p t c", c=DW)
            for h in range(DH + 2):
                if h < DH:
                    s = dsoft[:, 1152 * (h % 2):1152 * (h % 2) + 1152]
                    c = 340 + 2 * (h % 4)
                    p = scored()
                    taken_score(scores(s, h, ((p[:, :], s[:, 384:896], masks[:, 1:3, :].rearrange("p g s -> p (g s)"), 132),), DD ** -0.5, None))
                    p = scored()
                    taken_score(scores(s, h, ((p[:, 0:256], s[:, 896:1152], masks[:, 3, :], 133),), DD ** -0.5, None))
                    p = scored()
                    taken_score(scores(s, h, ((p[:, 0:384].rearrange("p (g s) -> p g s", s=128), s[:, 0:384].rearrange("p (g s) -> p g s", s=128),
                                               masks[:, 1:4, 128:256], c),), DD ** -0.5, None))
                    link(tt(st[:, c + 1:c + 2], st[:, 132:133], st[:, 133:134], ALU.max))
                    minus(h, "dil")
                if h >= 2:
                    attend("dil", h - 2, lambda t: ya3[:, t, DD * (h - 2):DD * (h - 1)])
            mark(tt(ya, ya, za, ALU.mult), "ya_rows")
            dve.wait_ge(sem("taken_act"), taken("glu0")[1])
            mark(tt(yssT[:, 0:1024], sig_glu[:, 0:1024], gz[:, 0:1024], ALU.mult), "yss")
            dve.wait_ge(sem("taken_act"), taken("glu1")[1])
            mark(tt(yssT[:, 1024:2048], sig_glu[:, 1024:2048], gz[:, 1024:2048], ALU.mult), "yss")
            m3 = m_tok.rearrange("p (t c) -> p t c", c=DM)
            r3 = rsig.rearrange("p (t c) -> p t c", c=DM)
            s3 = asig.rearrange("p (t c) -> p t c", c=DM)
            for i in range(2):
                for t in range(TT):
                    p = arrived(f"ao{i}", t)
                    ins = tt(m3[:, t, 512 * i:512 * i + 512], p[:, 512 * t:512 * t + 512], s3[:, t, 512 * i:512 * i + 512], ALU.mult)
                    if t == 0:
                        link(ins)
                mark(ins, "taken_dve")
            for t in range(TT):
                for i in range(2):
                    p = arrived(f"so{i}", t)
                    r = r3[:, t, 512 * i:512 * i + 512]
                    ins = tt(r, p[:, 512 * t:512 * t + 512], r, ALU.mult)
                    mark(ins, "taken_dve") if t else link(ins)
                    m = m3[:, t, 512 * i:512 * i + 512]
                    mark(tt(m, m, r, ALU.add), "m_sum")
            for t in range(TT):
                for i in range(2):
                    mark(residual(f"wp{i}", i, t), "result")

        @block.tensor
        def _(pe):
            n_unit = {"turned": 0, "score": 0}
            turned_at = {}

            def unit(kind):
                n = n_unit[kind]
                n_unit[kind] += 1
                if n >= 2:
                    pe.wait_ge(sem(kind + "_taken"), n - 1)
                return bank[kind][n % 2]

            def turn(name, blocks):
                b = unit("turned")
                a = 0
                for x in blocks:
                    rows = x.shape[0]
                    ins = pe.transpose(b[0:x.shape[1], a:a + rows], x, ident[0:rows, 0:rows])
                    a += rows
                ins.then_inc(sem("turned_ready"), 1)
                turned_at[name] = n_unit["turned"]

            def is_turned(name):
                pe.wait_ge(sem("turned_taken"), turned_at[name])

            def matmuls(name, half):
                j = JOB[name]
                _, o, w, r0, rows, c0, cols = JOBS[j]
                p = pair[OUTS.index(o) % 2]
                if w is None:
                    return [(p[:, SEQ * h:SEQ * h + SEQ], wgate[0:GR, P * h:P * h + P], aT[0:GR, :], True, True)
                            for h in (2 * half, 2 * half + 1)]
                nk = rows // P
                ws = ring[:, STREAMED.index(j) % RING, 0:nk * cols].rearrange("p (k n) -> p k n", n=cols)
                base, total = 0, nk
                if o.startswith("kv"):
                    act_ = lambda k: ckvT[:, SEQ * k:SEQ * k + SEQ]
                elif o in ("mk", "mv0", "mv1"):
                    act_ = lambda k: memT[:, SEQ * k:SEQ * k + SEQ]
                elif o.startswith("down"):
                    base, total = KD * int(name[-1]), FF // P
                    act_ = lambda k: hup[:, SEQ * (base + k):SEQ * (base + k) + SEQ]
                elif o.startswith("glu"):
                    act_ = lambda k: uT[:, SEQ * k:SEQ * k + SEQ]
                elif o.startswith("so"):
                    act_ = lambda k: yssT[:, SEQ * k:SEQ * k + SEQ]
                elif o.startswith("ao"):
                    act_ = lambda k: yaT[:, SEQ * k:SEQ * k + SEQ]
                else:
                    act_ = lambda k: hT[:, k, :]
                if o in SPLIT_TOKENS:
                    return [(p[:, SEQ * c + P * half:SEQ * c + P * half + P], ws[:, k, P * c:P * c + P],
                             act_(k)[:, P * half:P * half + P], k == 0, k == nk - 1) for c in range(4) for k in range(nk)]
                if cols < P:
                    return [(p[0:cols, 0:SEQ], ws[:, k, :], act_(k), k == 0, k == nk - 1)
                            for k in range(nk // 2 * half, nk // 2 * (half + 1))]
                if o in CHANNEL_MAJOR:
                    return [(p[:, SEQ * c:SEQ * c + SEQ], ws[:, k, P * c:P * c + P], act_(k), k == 0, k == nk - 1)
                            for c in (2 * half, 2 * half + 1) for k in range(nk)]
                return [(p[:, 512 * half:512 * half + cols], act_(k)[:, P * half:P * half + P], ws[:, k, :], base + k == 0,
                         base + k == total - 1) for k in range(nk)]

            finished = [0]

            def half_job(name, half, sub=None):
                j = JOB[name]
                o = JOBS[j][1]
                if half == 0 and sub != 1:
                    if JOBS[j][2]:
                        n = STREAMED.index(j)
                        pe.wait_ge(sem(f"weights{n % RING}"), 16 * (n // RING + 1))
                    i = OUTS.index(o)
                    if i >= 2 and FIRST_JOB[o] == name:
                        by, v = taken(OUTS[i - 2])
                        pe.wait_ge(sem(by), v)
                mm = matmuls(name, half)
                n = len(mm)
                lo, hi = (0, n) if sub is None else (n * sub // 2, n * (sub + 1) // 2)
                for o_, s, m, a, b in mm[lo:hi]:
                    ins = pe.matmul(o_, s, m, start=a, stop=b, skip_group_check=o.startswith("down"))
                if sub != 0:
                    assert HALVES[finished[0]] == (name, half), (HALVES[finished[0]], name, half)
                    finished[0] += 1
                    ins.then_inc(sem("half_done"), 1)

            def part(name, q):
                half_job(name, q // 2, q % 2)

            def job(name):
                half_job(name, 0)
                half_job(name, 1)

            def fill(names, i, n):
                for q in range(n * i, n * i + n):
                    if q < 4 * len(names):
                        part(names[q // 4], q % 4)

            def turn_rows(name, x, t):
                for g in range(2):
                    turn(name, [x[:, DM * t + P * k:DM * t + P * k + P] for k in range(4 * g, 4 * g + 4)])

            def ktiles(x, w=DM):
                v = x.rearrange("p (t c) -> p t c", c=w)
                return [v[:, t, P * k:P * k + P] for k in range(w // P) for t in range(TT)]

            pe.wait_ge(sem("ident_in"), 16)
            pe.wait_ge(sem("rows_in"), 16 * len(COLS))
            turn("cols", [prow[:, :]])
            pe.wait_ge(sem("x_rows"), 1)
            turn_rows("x", xn1, 0)
            is_turned("x")
            half_job("ckv", 0)
            pe.wait_ge(sem("x_rows"), 2)
            turn_rows("x", xn1, 1)
            is_turned("x")
            half_job("ckv", 1)
            half_job("gq", 0)
            pe.wait_ge(sem("mem_rows"), 1)
            turn_rows("mem", mem_tok, 0)
            half_job("gq", 1)
            pe.wait_ge(sem("mem_rows"), 2)
            turn_rows("mem", mem_tok, 1)
            job("gk")
            job("ga")
            pe.wait_ge(sem("ckv_rows"), 2)
            ck = ckv.rearrange("p (t c) -> p t c", c=RANK + ROPE)
            turn("ckv", [ck[:, t, P * k:P * k + P] for k in range(2) for t in range(TT)])
            pe.wait_ge(sem("kpe_rows"), 2)
            turn("kpe", [kpe[:, P * t:P * t + P] for t in range(TT)])
            pe.wait_ge(sem("taken_act"), taken("ga")[1])
            pe.wait_ge(sem("consts_in"), 16 * (8 + len(GAINS)))
            job("gg")
            for i in range(3):
                job(f"q{i}")
            is_turned("ckv")
            for i in range(4):
                job(f"kv{i}")
            job("gv0")
            q16 = q_tok.rearrange("p (t h c) -> p t h c", t=TT, c=QW)
            pe.wait_ge(sem("q_rows"), 1)
            for g in range(4):
                turn("qn", [q16[:, t, h, 0:NOPE] for h in (2 * g, 2 * g + 1) for t in range(TT)])
            pe.wait_ge(sem("qpe_rows"), 1)
            for g in range(2):
                turn("qp", ktiles(qpe, MH * ROPE)[4 * g:4 * g + 4])
            k16 = kv_tok.rearrange("p (t h c) -> p t h c", t=TT, c=NOPE + DV)
            half_job("gv1", 0)
            pe.wait_ge(sem("k_rows"), 1)
            for g in range(4):
                turn("kn", [k16[:, t, h, 0:NOPE] for h in (2 * g, 2 * g + 1) for t in range(TT)])
            is_turned("kn")

            for h in range(MH + 2):
                if h == 0:
                    half_job("gv1", 1)
                else:
                    fill(["gr0", "gr1", "mq", "mk", "mv0"], h - 1, 2)
                if h < MH:
                    b = unit("score")
                    r = slice(64 * (h % 2), 64 * (h % 2) + 64)
                    for t in range(TT):
                        w = P * (t + 1)
                        o = b[:, P * t:P * t + w]
                        pe.matmul(o, qnT[:, SEQ * h + P * t:SEQ * h + P * t + P], knT[:, SEQ * h:SEQ * h + w], start=True, stop=False)
                        ins = pe.matmul(o, qpT[r, SEQ * (h // 2) + P * t:SEQ * (h // 2) + P * t + P], kpeT[r, 0:w], start=False, stop=True)
                    ins.then_inc(sem("score_ready"), 1)
                if 1 <= h <= MH:
                    pe.wait_ge(sem("mla_exp"), h)
                    s = soft[:, 512 * ((h - 1) % 2):512 * ((h - 1) % 2) + 384]
                    turn(f"mla{h - 1}", [s[:, 0:128], s[:, 128:256], s[:, 256:384]])
                if h >= 2:
                    i = h - 2
                    is_turned(f"mla{i}")
                    b = unit("score")
                    s = softT[:, 512 * (i % 2):512 * (i % 2) + 384]
                    v = lambda t: k16[:, t, i, NOPE:NOPE + DV]
                    pe.matmul(b[:, 0:128], s[:, 0:128], v(0), start=True, stop=True)
                    pe.matmul(b[:, 128:256], s[:, 128:256], v(0), start=True, stop=False)
                    pe.matmul(b[:, 128:256], s[:, 256:384], v(1), start=False, stop=True).then_inc(sem("score_ready"), 1)
            half_job("mv0", 1)
            half_job("mv1", 0)
            pe.wait_ge(sem("m_rows"), 2)
            turn("qm", ktiles(mq_tok, 256))
            turn("km", ktiles(mk_tok, 256))
            is_turned("km")

            vm3 = vm.rearrange("p (t c) -> p t c", c=DM)
            vg3 = vg.rearrange("p (t c) -> p t c", c=DM)
            for i in range(9):
                fill(["mv1", "gate0", "gate1", "gate4", "gate5"], i + 1, 2)
                if i < EH:
                    b = unit("score")
                    r = slice(64 * (i % 2), 64 * (i % 2) + 64)
                    for t in range(TT):
                        ins = pe.matmul(b[:, SEQ * t:SEQ * t + SEQ], qmT[r, SEQ * (i // 2) + P * t:SEQ * (i // 2) + P * t + P],
                                        kmT[r, SEQ * (i // 2):SEQ * (i // 2) + SEQ], start=True, stop=True)
                    ins.then_inc(sem("score_ready"), 1)
                if 1 <= i <= EH:
                    pe.wait_ge(sem("mem_exp"), i)
                    s = soft[:, 512 * ((i - 1) % 2):512 * ((i - 1) % 2) + 512]
                    turn(f"mem{i - 1}", [s[:, P * k:P * k + P] for k in range(4)])
                if 2 <= i < EH + 2:
                    h = i - 2
                    is_turned(f"mem{h}")
                    pe.wait_ge(sem("taken_act"), taken("mv1")[1])
                    b = unit("score")
                    s = softT[:, 512 * (h % 2):512 * (h % 2) + 512]
                    for t in range(TT):
                        for k in range(2):
                            ins = pe.matmul(b[:, SEQ * t:SEQ * t + SEQ], s[:, 256 * t + P * k:256 * t + P * k + P],
                                            vm3[:, k, EV * h:EV * h + EV], start=k == 0, stop=k == 1)
                    ins.then_inc(sem("score_ready"), 1)
                if i < 8:
                    pe.wait_ge(sem("level_ready"), i + 1)
                ks, qs = (kgT, qgT) if i == 8 else (kdec, qdec)
                b = unit("score")
                if i == 7:
                    for h in range(GH):
                        ins = pe.matmul(b[:, P * h:P * h + P], ks[:, SEQ * h:SEQ * h + P], qs[:, SEQ * h + P:SEQ * h + 2 * P], start=True, stop=True)
                else:
                    w, blocks = ((64, ((0, 0, 64),)), (32, ((0, 0, 32), (64, 64, 96))))[i] if i < 2 else \
                        (32, tuple((32 * k, 32 * k, 32 * k) for k in range(4)))
                    for x in range(GH * TT):
                        for lane0, k0, q0 in blocks:
                            ins = pe.matmul(b[lane0:lane0 + w, w * x:w * x + w], ks[:, P * x + k0:P * x + k0 + w],
                                            qs[:, P * x + q0:P * x + q0 + w], start=True, stop=True)
                ins.then_inc(sem("score_ready"), 1)
            pe.wait_ge(sem("amat"), 4)
            for n in range(4):
                b = unit("score")
                t = n // 2
                for k in range(2):
                    h = 2 * (n % 2) + k
                    o = b[:, GV * k:GV * k + GV]
                    ins = pe.matmul(o, amat[:, P * (2 * h + t):P * (2 * h + t) + P], vg3[:, t, GV * h:GV * h + GV], start=True, stop=t == 0)
                    if t:
                        ins = pe.matmul(o, across[:, P * h:P * h + P], vg3[:, 0, GV * h:GV * h + GV], start=False, stop=True)
                ins.then_inc(sem("score_ready"), 1)
            half_job("gate2", 0)
            half_job("gate3", 0)
            half_job("gate2", 1)
            half_job("gate3", 1, 0)
            pe.wait_ge(sem("y_rows"), 2)
            turn_rows("y", o_mla, 0)
            half_job("gate3", 1, 1)
            is_turned("y")
            half_job("wo0", 0)
            half_job("wo1", 0, 0)
            pe.wait_ge(sem("y_rows"), 4)
            turn_rows("y", o_mla, 1)
            half_job("wo1", 0, 1)
            is_turned("y")
            half_job("wo0", 1)
            half_job("wo1", 1, 0)
            pe.wait_ge(sem("x_rows"), 3)
            turn_rows("x", xn2, 0)
            half_job("wo1", 1, 1)
            is_turned("x")

            half_job("up0", 0)
            pe.wait_ge(sem("x_rows"), 4)
            turn_rows("x", xn2, 1)
            half_job("up1", 0)
            is_turned("x")
            half_job("up0", 1)
            half_job("up1", 1)
            R = srow[0:ST, :].rearrange("p (k n) -> p k n", n=128)
            for i in range(2, 8):
                job(f"up{i}")
                if i == 2:
                    pe.wait_ge(sem("lane_rows"), 1)
                    turn("lane", [R[:, k, :] for k in (4, 5, 3, 7, 8)])
                    assert n_unit["turned"] == T_LANE, n_unit
                if i == 4:
                    pe.wait_ge(sem("bexp_ready"), 4)
                    for k in range(4):
                        turn("b", [bexp[:, 512 * k + P * m:512 * k + P * m + P] for m in range(4)])
            for k in range(3):
                pe.wait_ge(sem("ff_ready"), 2 * k + 2)
                job(f"down0{k}")
                if k == 0:
                    for m in range(4):
                        turn("c", [cnat[:, 512 * m + P * a:512 * m + P * a + P] for a in range(4)])
                    assert n_unit["turned"] == T_C, n_unit
                job(f"down1{k}")
            pe.wait_ge(sem("ff_ready"), 8)
            half_job("down03", 0)
            half_job("down13", 0)
            half_job("down03", 1)
            half_job("down13", 1, 0)

            pe.wait_ge(sem("x_rows"), 5)
            turn_rows("x", xn3, 0)
            half_job("down13", 1, 1)
            is_turned("x")
            half_job("us0", 0)
            pe.wait_ge(sem("x_rows"), 6)
            turn_rows("x", xn3, 1)
            half_job("us1", 0)
            is_turned("x")
            half_job("us0", 1)
            half_job("us1", 1)

            def states(k):
                b = unit("score")
                pe.wait_ge(sem("h_ready"), 2 * (4 * k + 4))
                for i in range(2):
                    for j in range(4 * k, 4 * k + 4):
                        a = 512 * (j % 8) + 256 * i
                        ins = pe.matmul(b[32 * (j % 4):32 * (j % 4) + 32, 0:SEQ], cc[:, 1024 * i + 32 * j:1024 * i + 32 * j + 32],
                                        hst[:, a:a + 256], start=i == 0, stop=i == 1)
                ins.then_inc(sem("score_ready"), 1)

            for j in range(ST):
                fill(["dv0", "dv1", "dv2", "zs0", "zs1", "za", "dq0", "dq1"], j, 1)
                if j == 0:
                    pe.wait_ge(sem("taken_act"), taken("us1")[1])
                    pe.wait_ge(sem("c_ready"), 4)
                if j % 2:
                    two = [unit("score") for _ in range(2)]
                    for i in range(2):
                        for m, b in zip((j - 1, j), two):
                            r = slice(32 * (m % 4), 32 * (m % 4) + 32)
                            ins = pe.matmul(b[:, SEQ * i:SEQ * i + SEQ], bt[r, 1024 * i + P * (m // 4):1024 * i + P * (m // 4) + P],
                                            uT[r, SEQ * (m // 4):SEQ * (m // 4) + SEQ], start=True, stop=True)
                            if i:
                                ins.then_inc(sem("score_ready"), 1)
                if j % 4 == 3 and j >= 7:
                    states(j // 4 - 1)

            def turn_dqk(n):
                pe.wait_ge(sem("dqk_rows"), n + 1)
                for k in range(2):
                    turn(f"dqk{n}", ktiles(raw, DW)[4 * k:4 * k + 4])

            turn_dqk(0)
            job("dq2")
            states(7)
            turn_dqk(1)
            for n in range(3):
                job(f"dk{n}")
                turn_dqk(n + 2)
            job("rs0")
            turn_dqk(5)
            is_turned("dqk5")
            vd4 = vd.rearrange("p (g t c) -> p g t c", g=NDIL, t=TT)
            for h in range(DH + 2):
                if h == 6:
                    pe.wait_ge(sem("gelu_ready"), 2)
                fillers = ["rs1", "ra0", "ra1", "glu0", "glu1"]
                last = h == DH + 1
                s = dsoft[:, 1152 * ((h - 1) % 2):1152 * ((h - 1) % 2) + 1152]
                tiles = lambda g: [s[:, a:a + P] for a in (P * g, 384 + 256 * g, 512 + 256 * g)]
                if h < DH:
                    r = slice(64 * (h % 2), 64 * (h % 2) + 64)
                    q = lambda g, t: qdT[r, 1024 * g + SEQ * (h // 2) + P * t:1024 * g + SEQ * (h // 2) + P * t + P]
                    k = lambda g, w: kdT[r, 1024 * g + SEQ * (h // 2):1024 * g + SEQ * (h // 2) + w]
                    b = unit("score")
                    for g in range(2):
                        ins = pe.matmul(b[:, 256 * g:256 * g + 256], q(g, 1), k(g, 256), start=True, stop=True)
                    ins.then_inc(sem("score_ready"), 1)
                    b = unit("score")
                    pe.matmul(b[:, 0:256], q(2, 1), k(2, 256), start=True, stop=True).then_inc(sem("score_ready"), 1)
                if not last:
                    fill(fillers, 2 * h, 1)
                if 1 <= h <= DH:
                    pe.wait_ge(sem("dil_exp"), h)
                    for g in range(2):
                        turn(f"dil{h - 1}", tiles(g))
                if h < DH:
                    b = unit("score")
                    for g in range(NDIL):
                        ins = pe.matmul(b[:, P * g:P * g + P], q(g, 0), k(g, 128), start=True, stop=True)
                    ins.then_inc(sem("score_ready"), 1)
                fill(fillers, 2 * h + (not last), 1)
                if 1 <= h <= DH:
                    turn(f"dil{h - 1}", tiles(2))
                if h >= 2:
                    i = h - 2
                    is_turned(f"dil{i}")
                    b = unit("score")
                    s = dsoftT[:, 1152 * (i % 2):1152 * (i % 2) + 1152]
                    v = lambda g, t: vd4[:, g, t, DD * i:DD * i + DD]
                    for g in range(NDIL):
                        pe.matmul(b[:, 0:DD], s[:, 384 * g:384 * g + P], v(g, 0), start=g == 0, stop=g == NDIL - 1)
                    for g in range(NDIL):
                        for k in range(2):
                            ins = pe.matmul(b[:, DD:2 * DD], s[:, 384 * g + P * (k + 1):384 * g + P * (k + 2)], v(g, k),
                                            start=g == 0 and k == 0, stop=g == NDIL - 1 and k == 1)
                    ins.then_inc(sem("score_ready"), 1)
            part("glu1", 3)
            pe.wait_ge(sem("ya_rows"), 1)
            for k in range(2):
                turn("ya", ktiles(ya, DW)[4 * k:4 * k + 4])
            is_turned("ya")
            job("ao0")
            job("ao1")
            pe.wait_ge(sem("yss"), 2)
            half_job("so0", 0)
            half_job("so1", 0)
            half_job("so0", 1)
            half_job("so1", 1, 0)
            pe.wait_ge(sem("m_sum"), 2)
            turn_rows("m", m_tok, 0)
            half_job("so1", 1, 1)
            is_turned("m")
            half_job("wp0", 0)
            pe.wait_ge(sem("m_sum"), 4)
            turn_rows("m", m_tok, 1)
            half_job("wp1", 0)
            is_turned("m")
            half_job("wp0", 1)
            half_job("wp1", 1)


_INS = ["x", "mem", "positions", "g_mix", "w_in", "b_gate", "g_ckv", "w_ukv", "g_q_nope", "g_k_nope", "g_q_rope",
        "g_k_rope", "w_gla_gate", "b_gla_gate", "g_gla_out", "g_mem", "w_mem_kv", "g_q_mem", "g_k_mem", "w_o", "g_ffn",
        "w_up", "w_down", "positions_2", "norm_w_2", "w_in_2", "lam_re_2", "lam_im_2", "log_dt_2", "b_re_2", "b_im_2",
        "c_re_2", "c_im_2", "d_skip_2", "w_glu_2", "q_norm_w_2", "k_norm_w_2", "w_ssm_out_2", "w_attn_out_2", "w_o_2"]


def constants():
    p, k = np.arange(P)[:, None], np.arange(SEQ)[None, :]
    back = P + p - k
    masks = [np.where(back >= 0, 0.0, NEG)]
    for window, dil in ((128, 1), (512, 4), (2048, 16)):
        masks.append(np.where((back >= 0) & (back <= window) & (back % dil == 0), 0.0, NEG))
    j, i = np.arange(P)[:, None] % 32, np.arange(32)[None, :]
    levels = [((j // (2 * s) == i // (2 * s)) & (j % (2 * s) < s) & (i % (2 * s) >= s)) for s in LEVELS if s < 32]
    levels.append(i == j)
    one = np.float32(1)
    inv1 = one / (np.float32(10000.0) ** (np.arange(0, ROPE, 2, dtype=np.float32) / np.float32(ROPE)))
    inv2 = np.float32(500000.0) ** (-np.arange(0, RD, 2, dtype=np.float32) / np.float32(RD))
    inv = np.concatenate([inv1, inv2]).astype(np.float32)
    return {
        "c_ident": np.eye(P, dtype=np.float32),
        "c_masks": np.stack(masks, 1).astype(np.float32),
        "c_levels": np.stack(levels, 1).astype(np.float32),
        "c_inv": np.ascontiguousarray(np.broadcast_to(inv, (P, inv.size))),
    }


def kernel(**inputs):
    import numpy as _np
    import concourse.bacc as _bacc
    from concourse import mybir as _mybir
    from concourse.bass_utils import run_bass_kernel_spmd as _run

    nc = _bacc.Bacc("TRN2", target_bir_lowering=False, num_devices=1)
    arrays, aps = {}, {}
    for name in _INS:
        arrays[f"in_{name}"] = _np.ascontiguousarray(inputs[name])
    for name, a in constants().items():
        arrays[f"in_{name}"] = a
    for name, a in arrays.items():
        aps[name[3:]] = nc.dram_tensor(name, a.shape, _mybir.dt.from_np(a.dtype), kind="ExternalInput").ap()
    out = nc.dram_tensor("out", (1, SEQ, DM), F32, kind="ExternalOutput").ap()
    build(nc, aps, out)
    r = _run(nc, [arrays], core_ids=[0])
    return r.results[0]["out"]
```

```python
from contextlib import ExitStack

import concourse.bass as bass
from concourse import mybir
import numpy as np

F32 = mybir.dt.float32
I32 = mybir.dt.int32
ACT = mybir.ActivationFunctionType
ALU = mybir.AluOpType
AX = mybir.AxisListType

P = 128
SEQ = 256
TT = SEQ // P
DM = 1024
KD = DM // P
EPS = 1e-6

MH, NOPE, ROPE, DV = 8, 128, 64, 128
QW = NOPE + ROPE
RANK = 256
GH, GK, GV, GR = 4, 128, 256, 16
EH, EQ, EV = 4, 64, 256
FF = 4 * DM
C_Q = 0
C_CKV = MH * QW
C_GQ = C_CKV + RANK + ROPE
C_GK = C_GQ + GH * GK
C_GV = C_GK + GH * GK
C_GA = C_GV + GH * GV
C_GR = C_GA + GR
C_MQ = C_GR + GH * GV
C_GATE = C_MQ + EH * EQ

SG, SP_, SN = 64, 16, 64
ST = SG // 2
CH = 128
NDIL, DH, DD = 3, 8, 64
DW = DH * DD
RD = DD // 4
C_US = 0
C_ZS = DM
C_DQ = 2 * DM
C_DK = C_DQ + NDIL * DW
C_DVV = C_DK + NDIL * DW
C_ZA = C_DVV + NDIL * DW
C_RS = C_ZA + DW
C_RA = C_RS + DM

RING = 3
NEG = -1e30
ROUND = 12582912.0
TWO_PI_A = 6.28125
TWO_PI_B = 0.0019350051879882812
TWO_PI_C = 3.019916e-07
PI_IN = 3.1415925
ROOT_BITS = float(0x5f3759df)

COLS = {}
for _name, _n in (("g_mix", 8), ("g_mem", 8), ("g_ffn", 8), ("norm_w_2", 8), ("g_ckv", 2), ("g_q_nope", 1),
                  ("g_k_nope", 1), ("b_gla_gate", 4), ("d_skip_2", 8)):
    COLS[_name] = (sum(n for _, n in COLS.values()), _n)
NCOLS = sum(n for _, n in COLS.values())

GAINS = (("g_q_rope", 64), ("g_k_rope", 64), ("g_q_mem", 64), ("g_k_mem", 64), ("g_gla_out", 256),
         ("q_norm_w_2", 192), ("k_norm_w_2", 192))
LEVELS = (64, 32, 16, 8, 4, 2, 1)
T_LANE = 44
T_C = T_LANE + 8


def jobs_table():
    j = [("ckv", "w_in", C_CKV, RANK + ROPE), ("gq", "w_in", C_GQ, 512), ("gk", "w_in", C_GK, 512),
         ("ga", "w_in", C_GA, GR), ("q0", "w_in", C_Q, 512), ("gg", None, 0, 0)]
    j += [(f"q{i}", "w_in", C_Q + 512 * i, 512) for i in (1, 2)]
    j += [(f"kv{i}", "w_ukv", 512 * i, 512) for i in range(4)]
    j += [(f"gv{i}", "w_in", C_GV + 512 * i, 512) for i in range(2)]
    j += [(f"gr{i}", "w_in", C_GR + 512 * i, 512) for i in range(2)]
    j += [("mq", "w_in", C_MQ, 256), ("mk", "w_mem_kv", 0, 256)]
    j += [(f"mv{i}", "w_mem_kv", 256 + 512 * i, 512) for i in range(2)]
    j += [(f"gate{i}", "w_in", C_GATE + 512 * i, 512) for i in (0, 1, 4, 5, 2, 3)]
    j += [(f"wo{i}", "w_o", 512 * i, 512) for i in range(2)]
    out = [(n, n, w, 0, RANK if w == "w_ukv" else DM, c, m) for n, w, c, m in j]
    out += [(f"up{i}", f"up{i}", "w_up", 0, DM, 512 * i, 512) for i in range(8)]
    out += [(f"down{h}{k}", f"down{h}", "w_down", DM * k, DM, 512 * h, 512) for k in range(4) for h in range(2)]
    j = [(f"us{i}", "w_in_2", C_US + 512 * i, 512) for i in range(2)]
    j += [(f"dv{g}", "w_in_2", C_DVV + DW * g, DW) for g in range(NDIL)]
    j += [(f"zs{i}", "w_in_2", C_ZS + 512 * i, 512) for i in range(2)]
    j += [("za", "w_in_2", C_ZA, DW)]
    j += [(f"dq{g}", "w_in_2", C_DQ + DW * g, DW) for g in range(NDIL)]
    j += [(f"dk{g}", "w_in_2", C_DK + DW * g, DW) for g in range(NDIL)]
    j += [(f"rs{i}", "w_in_2", C_RS + 512 * i, 512) for i in range(2)]
    j += [(f"ra{i}", "w_in_2", C_RA + 512 * i, 512) for i in range(2)]
    j += [(f"glu{i}", "w_glu_2", 512 * i, 512) for i in range(2)]
    j += [(f"ao{i}", "w_attn_out_2", 512 * i, 512) for i in range(2)]
    j += [(f"so{i}", "w_ssm_out_2", 512 * i, 512) for i in range(2)]
    j += [(f"wp{i}", "w_o_2", 512 * i, 512) for i in range(2)]
    out += [(n, n, w, 0, DW if w == "w_attn_out_2" else DM, c, m) for n, w, c, m in j]
    return out


JOBS = jobs_table()
JOB = {job[0]: n for n, job in enumerate(JOBS)}
OUTS = list(dict.fromkeys(job[1] for job in JOBS))
LAST_JOB = {job[1]: job[0] for job in JOBS}
FIRST_JOB = {job[1]: job[0] for job in reversed(JOBS)}
BY_TOKENS = (("gate2", "gate3"), ("wo0", "wo1"), ("up0", "up1"), ("down03", "down13"), ("us0", "us1"), ("so0", "so1"),
             ("wp0", "wp1"))
HALVES = []
for _job in JOBS:
    _pair = next((x for x in BY_TOKENS if _job[0] in x), None)
    if _pair is None:
        HALVES += [(_job[0], 0), (_job[0], 1)]
    elif _job[0] == _pair[0]:
        HALVES += [(_n, _t) for _t in range(2) for _n in _pair]
BY_DVE = {"gg", "wo0", "wo1", "down0", "down1", "so0", "so1", "ao0", "ao1", "wp0", "wp1"} | {f"gate{i}" for i in range(6)}
SPLIT_TOKENS = ("up0", "up1", "us0", "us1")
CHANNEL_MAJOR = {"gq", "gk", "ga", "us0", "us1", "zs0", "zs1", "za", "glu0", "glu1"} | {f"up{i}" for i in range(8)}
STREAMED = [n for n, job in enumerate(JOBS) if job[2]]
GATES = (0, 1, 4, 5, 2, 3)


SEMAPHORES = {
    "x_in0": "first tile of x", "x_in1": "second tile of x", "mem_in": "the memory", "ident_in": "the identity",
    "rows_in": "parameters that become columns", "consts_in": "masks, gains, positions and the gate's weight",
    "bgate0": "bias of the even gates", "bgate1": "bias of the odd gates", "ssm_in": "state space parameters",
    "weights0": "weights in slot 0", "weights1": "weights in slot 1", "weights2": "weights in slot 2",
    "stored": "tiles of the result in DRAM",
    "half_done": "TensorE: halves of jobs", "taken_act": "ScalarE: outputs out of PSUM", "taken_dve": "outputs out of PSUM",
    "turned_ready": "TensorE: groups of transposes", "turned_taken": "ScalarE: groups of transposes out of PSUM",
    "score_ready": "TensorE: banks of scores, values or states", "score_taken": "those banks out of PSUM",
    "act_step": "ScalarE's own", "dve_step": "VectorE's own", "pool_step": "GpSimd's own",
    "one_ready": "the column of ones", "x_ss": "squares of a tile of x", "mem_ss": "squares of a tile of the memory",
    "x_rows": "normalised tiles of x", "mem_rows": "normalised tiles of the memory", "ckv_rows": "tiles of the latent",
    "kpe_rows": "rotated key, twice", "q_rows": "queries without rotation", "qpe_rows": "rotated queries",
    "k_rows": "keys without rotation", "m_rows": "memory attention's queries, then keys",
    "dqk_rows": "one group's queries or keys of the dilated attention",
    "angle": "reduced rotary angles", "rope_ready": "ScalarE: cosines and sines",
    "mla_scores": "heads", "mla_exp": "heads", "mem_scores": "heads", "mem_exp": "heads", "dil_scores": "heads",
    "dil_exp": "heads", "dil_norm": "heads whose probabilities are divided by their sum",
    "gate_ln": "ScalarE: ln(1 + exp(-|x|)) of the forget gates", "silu_sig": "ScalarE: sigmoids of a tile's output gates",
    "silu_done": "a tile's output gates times their sigmoids", "level_diff": "exponents of a level",
    "level_exp": "ScalarE: decays of a level", "level_ready": "decayed queries and keys of a level",
    "amat": "lanes of the products within a tile",
    "gate_in": "a tile of one of the last two gates, biased", "gate_sig": "ScalarE: sigmoids of a gate, or of its tile",
    "y_rows": "a tile's half of the gated sum", "residual": "a tile's half of x with a branch's output added",
    "ff_ready": "squared rows of the feed-forward",
    "bexp_ready": "GpSimd: B spread over its group's channels", "dt_ready": "ScalarE: exp(log dt)",
    "theta": "angle and log of the modulus", "trig": "ScalarE: cosine, sine and modulus", "lane_rows": "lane parameters",
    "tables": "rotation tables, and C zeroed", "c_ready": "quarters of C times f", "g_ready": "scanned tiles",
    "h_ready": "GpSimd: halves of a tile of states", "z_silu": "gates times their sigmoids",
    "gelu_z": "argument of the gelu's sigmoid", "gelu_sig": "ScalarE: that sigmoid", "gelu_ready": "halves of the gelu",
    "yss": "halves of the gated state space output",
    "m_sum": "a tile's half of the gated sum", "result": "a tile's half of the result",
}


def done(name, half):
    return HALVES.index((name, half)) + 1


def taken(name):
    own = {"wo0": ("residual", 3), "wo1": ("residual", 4), "down0": ("residual", 7), "down1": ("residual", 8),
           "gate2": ("gate_in", 3), "gate3": ("gate_in", 4)}
    if name in own:
        return own[name]
    by_dve = name in BY_DVE
    return ("taken_dve" if by_dve else "taken_act",
            sum(o not in own and (o in BY_DVE) == by_dve for o in OUTS[:OUTS.index(name) + 1]))


def build(nc, d, out):
    with ExitStack() as ctx:
        def sb(name, shape, dt=F32):
            return ctx.enter_context(nc.sbuf_tensor(name, shape, dt))

        sems = {name: ctx.enter_context(nc.semaphore(name)) for name in SEMAPHORES}

        def sem(name):
            return sems[name]

        ident = sb("ident", [P, P])
        masks = sb("masks", [P, 1 + NDIL, SEQ])
        pcol = sb("pcol", [P, NCOLS])
        prow = sb("prow", [NCOLS, P])
        inv = sb("inv", [P, 40])
        ring = sb("ring", [P, RING, KD * 512])
        hT = sb("hT", [P, KD, SEQ])
        xres = sb("xres", [P, TT, DM])
        st = sb("stats", [P, 400])
        gains = sb("gains", [P, sum(w for _, w in GAINS)])
        rope = sb("rope", [P, 2, TT, 40])
        posi = sb("posi", [P, 2 * TT], I32)
        posf = sb("posf", [P, 2 * TT])
        carry = sb("carry", [P, 4])
        AR = 33700
        arena = sb("arena", [P, AR])

        gain, at = {}, 0
        for name, w in GAINS:
            gain[name] = gains[:, at:at + w]
            at += w

        def col(name, i=0, n=1):
            a = COLS[name][0] + i
            return pcol[:, a:a + n]

        class Place:
            def __init__(self, at=0):
                self.at = at

            def __call__(self, n):
                a = self.at
                self.at += n
                assert self.at <= AR, self.at
                return arena[:, a:a + n]

        a1 = Place()
        mem_tok = a1(2048); o_mla = mem_tok
        memT = a1(2048)
        q_tok = a1(3072)
        vg, mq_tok, mk_tok = q_tok[:, 0:2048], q_tok[:, 2048:2560], q_tok[:, 2560:3072]
        kv_tok = a1(4096)
        vm, gate_buf = kv_tok[:, 0:2048], kv_tok[:, 2048:4096]
        qnT = a1(2048); o_gla = qnT
        qpT = a1(1024)
        kmT, qmT = qpT[:, 0:512], qpT[:, 512:1024]
        knT = a1(2048); o_mem = knT
        kpeT = a1(256)
        kpe = a1(256)
        ckv = a1(640)
        ckvT = a1(512)
        qgT, kgT, bT, dec = a1(1024), a1(1024), a1(1024), a1(1024)
        qdec, kdec = a1(1024), a1(1024)
        amat = a1(1024); qpe = amat
        across = a1(512)
        r_gla = a1(2048); xn1 = r_gla
        soft = a1(1024)
        softT = a1(1024)
        aT = a1(256)
        wgate = a1(512)
        junk = a1(1024)
        levels = a1(192)
        adiag = a1(256)
        bgate = a1(1024)

        a2 = Place()
        cs = a2(ST * 2 * CH)
        bt = a2(2048)
        cc = a2(2048)
        lane = a2(288)
        ff_at = a2.at
        hup = a2(8192)
        xn2 = a2(2048)
        bnat = a2(1024)
        bexp = a2(2048)
        cnat = a2(2048)
        srow = a2(1536)
        tmp_cs = a2(4096)

        a3 = Place(ff_at)
        uT = a3(2048)
        zs = a3(2048); xn3 = zs
        za = a3(1024)
        vd = a3(3072)
        at_qk = a3.at
        qdT = a3(3072)
        kdT = a3(3072)
        hst = arena[:, at_qk:at_qk + 8 * 512]
        at_work = a3.at
        raw = a3(1024)
        raw2 = a3(1024)
        wrot = a3(1024)
        gst = a3(1024)
        hrot = a3(1024)
        a4 = Place()
        dsoft = a4(2304)
        dsoftT = a4(2304)
        gz = a4(2048)
        sig_glu = a4(2048); yssT = sig_glu
        yaT = a4(1024)
        assert a4.at <= ff_at
        a5 = Place(at_work)
        m_tok, rsig, asig = a5(2048), a5(2048), a5(2048)

        lam = {}
        for i, name in enumerate(("cos", "sin", "mag", "fre", "fim", "ere", "eim", "sq", "sq2")):
            lam[name] = lane[:, 32 * i:32 * i + 32]

        pair = [ctx.enter_context(nc.psum_tensor(f"pair{i}", [P, 1024], F32)) for i in range(2)]
        bank = {k: [ctx.enter_context(nc.psum_tensor(f"{k}{i}", [P, 512], F32)) for i in range(2)]
                for k in ("turned", "score")}

        block = ctx.enter_context(nc.Block())

        @block.sync
        def _(sp):
            def rows_of(names):
                for name in names:
                    a, n = COLS[name]
                    sp.dma_start(prow[a:a + n, :], d[name].rearrange("o (a b) -> (o a) b", b=P)).then_inc(sem("rows_in"), 16)

            sp.dma_start(xres[:, 0, :], d["x"][0, 0:P, :]).then_inc(sem("x_in0"), 16)
            sp.dma_start(xres[:, 1, :], d["x"][0, P:2 * P, :]).then_inc(sem("x_in1"), 16)
            rows_of(list(COLS)[4:])
            for n, j in enumerate(STREAMED):
                name, _, w, r0, rows, c0, cols = JOBS[j]
                slot = n % RING
                if n == 2:
                    sp.dma_start(mem_tok.rearrange("p (t c) -> p t c", c=DM),
                                 d["mem"][0].rearrange("(t p) c -> p t c", p=P)).then_inc(sem("mem_in"), 16)
                if n >= RING:
                    sp.wait_ge(sem("half_done"), done(JOBS[STREAMED[n - RING]][0], 1))
                dst = ring[:, slot, 0:rows // P * cols].rearrange("p (k n) -> p k n", n=cols)
                src = d[w][0, r0:r0 + rows, c0:c0 + cols].rearrange("(k p) n -> p k n", p=P)
                sp.dma_start(dst, src).then_inc(sem(f"weights{slot}"), 16)
            for t in range(TT):
                for i in range(2):
                    sp.wait_ge(sem("result"), 2 * t + i + 1)
                    sp.dma_start(out[0, P * t:P * t + P, 512 * i:512 * i + 512],
                                 xres[:, t, 512 * i:512 * i + 512]).then_inc(sem("stored"), 16)
            sp.wait_ge(sem("stored"), 64)

        @block.gpsimd
        def _(pool):
            count = [0]

            def link(ins):
                count[0] += 1
                ins.then_inc(sem("pool_step"), 1)
                pool.wait_ge(sem("pool_step"), count[0])

            pool.dma_start(masks[:, :, :], d["c_masks"]).then_inc(sem("consts_in"), 16)
            pool.dma_start(levels.rearrange("p (l n) -> p l n", n=32), d["c_levels"]).then_inc(sem("consts_in"), 16)
            pool.dma_start(inv[:, :], d["c_inv"]).then_inc(sem("consts_in"), 16)
            for i, name in enumerate(("positions", "positions_2")):
                for t in range(TT):
                    pool.dma_start(posi[:, TT * i + t:TT * i + t + 1],
                                   d[name][:, P * t:P * t + P].rearrange("o (p a) -> (o p) a", a=1)).then_inc(sem("consts_in"), 16)
            pool.dma_start(wgate[0:GR, :], d["w_gla_gate"][0]).then_inc(sem("consts_in"), 16)
            for name, w in GAINS:
                src = d[name].rearrange("o a b -> o (a b)") if len(d[name].shape) == 3 else d[name]
                pool.dma_start(gain[name], src.to_broadcast([P, w])).then_inc(sem("consts_in"), 16)
            for n, i in enumerate(GATES):
                if n >= 2:
                    pool.wait_ge(sem("taken_dve"), taken(f"gate{GATES[n - 2]}")[1])
                pool.dma_start(bgate[:, 512 * (n % 2):512 * (n % 2) + 512],
                               d["b_gate"][:, 512 * i:512 * i + 512].to_broadcast([P, 512])).then_inc(sem(f"bgate{n % 2}"), 16)

            pool.wait_ge(sem("residual"), taken("wo1")[1])
            link(pool.memset(bexp, 0.0))
            for i, name in enumerate(("b_re_2", "b_im_2")):
                pool.dma_start(bnat[:, 512 * i:512 * i + 512].rearrange("p (j c) -> p j c", c=SP_),
                               d[name][0].rearrange("(j a) n c -> (a n) j c", a=2)).then_inc(sem("ssm_in"), 16)
            for i, name in enumerate(("c_re_2", "c_im_2")):
                for half in range(2):
                    pool.dma_start(cnat[:, 1024 * i:1024 * i + 1024].rearrange("p (j h n) -> p j h n", h=2, n=SN)[:, :, half, :],
                                   d[name][0].rearrange("(j g) c n -> (g c) j n", g=8)).then_inc(sem("ssm_in"), 16)
            pool.dma_start(srow[0:ST, 0:128], d["lam_re_2"][0].rearrange("(j a) n -> j (a n)", a=2)).then_inc(sem("ssm_in"), 16)
            pool.dma_start(srow[0:ST, 128:256], d["lam_im_2"][0].rearrange("(j a) n -> j (a n)", a=2)).then_inc(sem("ssm_in"), 16)
            pool.dma_start(srow[0:ST, 256:258], d["log_dt_2"][0:1, :].rearrange("o (j a) -> (o j) a", a=2)).then_inc(sem("ssm_in"), 16)
            pool.wait_ge(sem("ssm_in"), 16 * 9)
            for i in range(2):
                for a in range(2):
                    last = pool.tensor_copy(
                        bexp[64 * a:64 * a + 64, 1024 * i:1024 * i + 1024].rearrange("p (j h c) -> p j h c", h=2, c=SP_)[:, :, a, :],
                        bnat[64 * a:64 * a + 64, 512 * i:512 * i + 512].rearrange("p (j c) -> p j c", c=SP_))
                    last.then_inc(sem("bexp_ready"), 1)

            for j in range(ST):
                pool.wait_ge(sem("g_ready"), j + 1)
                g = gst[:, 512 * (j % 2):512 * (j % 2) + 512]
                gv = g.rearrange("p (c t) -> p c t", t=CH)
                tab = cs.rearrange("p (j r t) -> p j r t", r=2, t=CH)[:, j]
                n1, n2 = hrot[:, 0:512], hrot[:, 512:1024]
                h = hst[:, 512 * (j % 8):512 * (j % 8) + 512]
                pool.tensor_tensor(n1.rearrange("p (c t) -> p c t", t=CH), gv,
                                   tab[:, 0:1, :].to_broadcast([P, 4, CH]), ALU.mult).then_inc(sem("pool_step"), 1)
                pool.tensor_tensor(n2.rearrange("p (c t) -> p c t", t=CH), gv,
                                   tab[:, 1:2, :].to_broadcast([P, 4, CH]), ALU.mult).then_inc(sem("pool_step"), 1)
                count[0] += 2
                pool.wait_ge(sem("pool_step"), count[0])
                pool.tensor_tensor(h[:, 0:256], n1[:, 0:256], n2[:, 256:512], ALU.subtract).then_inc(sem("h_ready"), 1)
                pool.tensor_tensor(h[:, 256:512], n1[:, 256:512], n2[:, 0:256], ALU.add).then_inc(sem("h_ready"), 1)
                pool.wait_ge(sem("h_ready"), 2 * j + 2)

        @block.scalar
        def _(act):
            n_turn, count, squared = [0], [0], {}

            def link(ins):
                count[0] += 1
                ins.then_inc(sem("act_step"), 1)
                act.wait_ge(sem("act_step"), count[0])

            def arrived(name, half=1):
                act.wait_ge(sem("half_done"), done(LAST_JOB[name], half))
                return pair[OUTS.index(name) % 2]

            def take(name, dst, func=ACT.Copy, scale=1.0, cols=512):
                for t in range(TT):
                    p = arrived(name, 1 if name in SPLIT_TOKENS else t)
                    ins = act.activation(dst(t), p[:, 512 * t:512 * t + cols], func, scale=scale)
                ins.then_inc(sem("taken_act"), 1)

            def turned(dst, n, scale=None, rows=P):
                i = n_turn[0]
                n_turn[0] += 1
                act.wait_ge(sem("turned_ready"), i + 1)
                src = bank["turned"][i % 2][0:rows, 0:n]
                if scale is None:
                    act.activation(dst, src, ACT.Copy).then_inc(sem("turned_taken"), 1)
                else:
                    w = n // len(scale)
                    for k, s in enumerate(scale):
                        ins = act.activation(dst[:, w * k:w * k + w], src[:, w * k:w * k + w], ACT.Copy, scale=s)
                    ins.then_inc(sem("turned_taken"), 1)

            act.dma_start(ident[:, :], d["c_ident"]).then_inc(sem("ident_in"), 16)
            for name in list(COLS)[:4]:
                a, n = COLS[name]
                act.dma_start(prow[a:a + n, :], d[name].rearrange("o (a b) -> (o a) b", b=P)).then_inc(sem("rows_in"), 16)

            def row_norm(t, src, lo, name, sink):
                act.activation(sink, src, ACT.Square, accum_out=st[:, 280 + lo // 2 + t:281 + lo // 2 + t]).then_inc(sem(name + "_ss"), 1)
                squared[name] = squared.get(name, 0) + 1
                act.wait_ge(sem(name + "_ss"), squared[name])

            def turned_rows(t, dst, gain_name=None):
                for g in range(2):
                    i = n_turn[0]
                    n_turn[0] += 1
                    act.wait_ge(sem("turned_ready"), i + 1)
                    src = bank["turned"][i % 2][:, :].rearrange("p (k n) -> p k n", n=P)
                    if gain_name is None:
                        ins = act.activation(dst[:, 4 * g:4 * g + 4, P * t:P * t + P], src, ACT.Copy)
                    else:
                        for k in range(4):
                            ins = act.activation(dst[:, 4 * g + k, P * t:P * t + P], src[:, k, :], ACT.Copy,
                                                 scale=col(gain_name, 4 * g + k))
                    ins.then_inc(sem("turned_taken"), 1)

            memT3 = memT.rearrange("p (k n) -> p k n", n=SEQ)
            act.wait_ge(sem("one_ready"), 1)
            act.activation(st[:, 398:399], st[:, 399:400], ACT.Square)
            for t in range(TT):
                act.wait_ge(sem(f"x_in{t}"), 16)
                row_norm(t, xres[:, t, :], 0, "x", junk)
            turned(pcol[:, :], NCOLS)
            act.wait_ge(sem("turned_taken"), 1)
            for t in range(TT):
                turned_rows(t, hT, "g_mix")
            act.wait_ge(sem("mem_in"), 16)
            for t in range(TT):
                row_norm(t, mem_tok[:, DM * t:DM * t + DM], 4, "mem", junk)
            act.wait_ge(sem("angle"), 1)
            link(act.activation(rope[:, 1, :, :], rope[:, 1, :, :], ACT.Sin))
            act.activation(rope[:, 0, :, :], rope[:, 0, :, :], ACT.Sin).then_inc(sem("rope_ready"), 1)
            ck = ckv.rearrange("p (t c) -> p t c", c=RANK + ROPE)
            take("ckv", lambda t: ck[:, t, :], cols=RANK + ROPE)
            for t in range(TT):
                turned_rows(t, memT3, "g_mem")
            take("gq", lambda t: qgT[:, 512 * t:512 * t + 512], scale=GK ** -0.5)
            take("gk", lambda t: kgT[:, 512 * t:512 * t + 512])
            p = arrived("ga")
            act.activation(aT[0:GR, :], p[0:GR, 0:SEQ], ACT.Copy).then_inc(sem("taken_act"), 1)
            q3 = q_tok.rearrange("p (t c) -> p t c", c=MH * QW)
            take("q0", lambda t: q3[:, t, 0:512])
            turned(ckvT, 512, [col("g_ckv", 0), col("g_ckv", 1)])
            turned(kpeT, 256)
            act.wait_ge(sem("taken_dve"), taken("gg")[1])
            link(act.activation(dec, bT, ACT.Abs))
            link(act.activation(dec, dec, ACT.Exp, scale=-1.0))
            act.activation(dec, dec, ACT.Ln, bias=1.0).then_inc(sem("gate_ln"), 1)
            for i in (1, 2):
                take(f"q{i}", lambda t: q3[:, t, 512 * i:512 * i + 512])
            k3 = kv_tok.rearrange("p (t c) -> p t c", c=MH * (NOPE + DV))
            for i in range(4):
                take(f"kv{i}", lambda t: k3[:, t, 512 * i:512 * i + 512])
            for g in range(4):
                turned(qnT[:, 512 * g:512 * g + 512], 512, [col("g_q_nope")])
            for g in range(2):
                turned(qpT[:, 512 * g:512 * g + 512], 512)
            for g in range(4):
                turned(knT[:, 512 * g:512 * g + 512], 512, [col("g_k_nope")])

            vg3 = vg.rearrange("p (t c) -> p t c", c=DM)
            rg3 = r_gla.rearrange("p (t c) -> p t c", c=DM)

            def exps(tag, n, parts):
                act.wait_ge(sem(tag + "_scores"), n + 1)
                for k, (a, w, t) in enumerate(parts):
                    s = (soft if tag != "dil" else dsoft)
                    half = (512 if tag != "dil" else 1152) * (n % 2)
                    ins = act.activation(s[:, half + a:half + a + w], s[:, half + a:half + a + w], ACT.Exp,
                                         bias=st[:, 340 + 2 * (n % 4) + t:341 + 2 * (n % 4) + t],
                                         accum_out=st[:, 350 + 2 * (n % 4) + t:351 + 2 * (n % 4) + t])
                ins.then_inc(sem(tag + "_exp"), 1)

            take("gv0", lambda t: vg3[:, t, 0:512])
            mq3 = mq_tok.rearrange("p (t c) -> p t c", c=EH * EQ)
            mk3 = mk_tok.rearrange("p (t c) -> p t c", c=EH * EQ)
            for h in range(MH + 2):
                if h == 1:
                    take("gv1", lambda t: vg3[:, t, 512:1024])
                if h in (3, 5):
                    i = (h - 3) // 2
                    take(f"gr{i}", lambda t: rg3[:, t, 512 * i:512 * i + 512])
                if h == 7:
                    take("mq", lambda t: mq3[:, t, :], cols=256)
                if h == 9:
                    take("mk", lambda t: mk3[:, t, :], cols=256)
                if 1 <= h <= MH:
                    turned(softT[:, 512 * ((h - 1) % 2):512 * ((h - 1) % 2) + 384], 384)
                if h < MH:
                    exps("mla", h, ((0, 128, 0), (128, 256, 1)))
            for t in range(TT):
                if t:
                    act.wait_ge(sem("silu_done"), t)
                act.activation(junk, rg3[:, t, :], ACT.Sigmoid).then_inc(sem("silu_sig"), 1)
            turned(qmT, 512)
            turned(kmT, 512)
            vm3 = vm.rearrange("p (t c) -> p t c", c=DM)
            take("mv0", lambda t: vm3[:, t, 0:512])

            def gate_sigmoid(n, half=None):
                g = gate_buf[:, 1024 * (n % 2):1024 * (n % 2) + 1024]
                if half is not None:
                    act.wait_ge(sem("gate_in"), 2 * half + n - 3)
                    g = g[:, 512 * half:512 * half + 512]
                else:
                    act.wait_ge(sem("taken_dve"), taken(f"gate{GATES[n]}")[1])
                act.activation(g, g, ACT.Sigmoid).then_inc(sem("gate_sig"), 1)

            def level_exp(lv):
                act.wait_ge(sem("level_diff"), lv + 1)
                act.activation(dec, dec, ACT.Exp, scale=1.0 / 16.0).then_inc(sem("level_exp"), 1)

            for i in range(9):
                if i < 8:
                    level_exp(i)
                if i == 2:
                    take("mv1", lambda t: vm3[:, t, 512:1024])
                if 1 <= i <= EH:
                    turned(softT[:, 512 * ((i - 1) % 2):512 * ((i - 1) % 2) + 512], 512)
                if i < EH:
                    exps("mem", i, ((0, 256, 0), (256, 256, 1)))
                if i in (4, 6, 8):
                    gate_sigmoid((i - 4) // 2)
            gate_sigmoid(3)
            for t in range(TT):
                gate_sigmoid(4, t)
                gate_sigmoid(5, t)
                turned_rows(t, hT)

            for t in range(TT):
                act.wait_ge(sem("residual"), 2 * t + 2)
                row_norm(t, xres[:, t, :], 0, "x", hup[:, 0:1024])
                turned_rows(t, hT, "g_ffn")
            R = srow[0:ST, :].rearrange("p (k n) -> p k n", n=128)
            for i in range(8):
                take(f"up{i}", lambda t: hup[:, 1024 * i + 512 * t:1024 * i + 512 * t + 512], func=ACT.Relu)
                if i == 0:
                    act.wait_ge(sem("ssm_in"), 16 * 9)
                    act.activation(srow[0:ST, 258:260], srow[0:ST, 256:258], ACT.Exp).then_inc(sem("dt_ready"), 1)
                    act.wait_ge(sem("theta"), 1)
                    link(act.activation(R[:, 3, :], R[:, 3, :], ACT.Exp))
                    link(act.activation(R[:, 5, :], R[:, 5, :], ACT.Sin))
                    act.activation(R[:, 4, :], R[:, 4, :], ACT.Sin).then_inc(sem("trig"), 1)
                if i == 2:
                    turned(lane[:, 0:160], 160)
                if i == 4:
                    for k in range(4):
                        turned(bt[:, 512 * k:512 * k + 512], 512)
            act.wait_ge(sem("tables"), 1)
            for k in range(4):
                turned(tmp_cs[:, 512 * k:512 * k + 512], 512)

            for t in range(TT):
                act.wait_ge(sem("residual"), 2 * TT + 2 * t + 2)
                row_norm(t, xres[:, t, :], 0, "x", raw)
                turned_rows(t, hT, "norm_w_2")
            for i in range(2):
                take(f"us{i}", lambda t: uT[:, 1024 * i + 512 * t:1024 * i + 512 * t + 512])
            vd4 = vd.rearrange("p (g t c) -> p g t c", g=NDIL, t=TT)
            for g in range(NDIL):
                take(f"dv{g}", lambda t: vd4[:, g, t, :])
            for i in range(2):
                if i == 1:
                    act.wait_ge(sem("z_silu"), 1)
                p = arrived(f"zs{i}")
                for t in range(2):
                    act.activation(zs[:, 1024 * i + 512 * t:1024 * i + 512 * t + 512], p[:, 512 * t:512 * t + 512], ACT.Copy)
                for t in range(2):
                    ins = act.activation(raw[:, 512 * t:512 * t + 512], p[:, 512 * t:512 * t + 512], ACT.Sigmoid)
                ins.then_inc(sem("taken_act"), 1)
            act.wait_ge(sem("z_silu"), 2)
            p = arrived("za")
            for t in range(2):
                act.activation(za[:, 512 * t:512 * t + 512], p[:, 512 * t:512 * t + 512], ACT.Copy)
            for t in range(2):
                ins = act.activation(raw[:, 512 * t:512 * t + 512], p[:, 512 * t:512 * t + 512], ACT.Sigmoid)
            ins.then_inc(sem("taken_act"), 1)
            for n in range(6):
                name = f"dq{n}" if n < 3 else f"dk{n - 3}"
                act.wait_ge(sem("z_silu"), 3)
                if n:
                    for _k in range(2):
                        turned((qdT if n - 1 < 3 else kdT)[:, 1024 * ((n - 1) % 3) + 512 * _k:1024 * ((n - 1) % 3) + 512 * _k + 512], 512)
                p = arrived(name)
                for t in range(2):
                    act.activation(raw[:, 512 * t:512 * t + 512], p[:, 512 * t:512 * t + 512], ACT.Copy)
                for t in range(2):
                    ins = act.activation(raw2[:, 512 * t:512 * t + 512], p[:, 512 * t:512 * t + 512], ACT.Square)
                ins.then_inc(sem("taken_act"), 1)
                if n == 2:
                    for i in range(2):
                        act.wait_ge(sem("gelu_z"), i + 1)
                        act.activation(gz[:, 1024 * i:1024 * i + 1024], gz[:, 1024 * i:1024 * i + 1024], ACT.Sigmoid,
                                       scale=1.5957691216057308).then_inc(sem("gelu_sig"), 1)
            take("rs0", lambda t: rsig[:, DM * t:DM * t + 512], func=ACT.Sigmoid)
            for k in range(2):
                turned(kdT[:, 2048 + 512 * k:2048 + 512 * k + 512], 512)
            take("rs1", lambda t: rsig[:, DM * t + 512:DM * t + 1024], func=ACT.Sigmoid)
            for s in range(DH // 2):
                if s >= 2:
                    i = s - 2
                    take(f"ra{i}", lambda t: asig[:, DM * t + 512 * i:DM * t + 512 * i + 512], func=ACT.Sigmoid)
                for h in (2 * s, 2 * s + 1):
                    exps("dil", h, ((0, 384, 0), (384, 768, 1)))
                for k in range(2 * NDIL):
                    turned(dsoftT[:, 384 * k:384 * k + 384], 384)
            take("glu0", lambda t: sig_glu[:, 512 * t:512 * t + 512], func=ACT.Sigmoid)
            take("glu1", lambda t: sig_glu[:, 1024 + 512 * t:1024 + 512 * t + 512], func=ACT.Sigmoid)
            for t in range(TT):
                turned_rows(t, hT)

        @block.vector
        def _(dve):
            count, n_score, own = [0], [0], {}

            def link(ins):
                count[0] += 1
                ins.then_inc(sem("dve_step"), 1)
                dve.wait_ge(sem("dve_step"), count[0])

            def step(ins):
                count[0] += 1
                ins.then_inc(sem("dve_step"), 1)

            def mark(ins, name):
                own[name] = own.get(name, 0) + 1
                ins.then_inc(sem(name), 1)
                dve.wait_ge(sem(name), own[name])

            def arrived(name, half=1):
                dve.wait_ge(sem("half_done"), done(LAST_JOB[name], half))
                return pair[OUTS.index(name) % 2]

            def scored():
                i = n_score[0]
                n_score[0] += 1
                dve.wait_ge(sem("score_ready"), i + 1)
                return bank["score"][i % 2]

            def tt(o, a, b, op):
                return dve.tensor_tensor(o, a, b, op)

            def bc(x, shape):
                return x.to_broadcast(shape)

            def inverse_root(lo, n):
                v, y, a = st[:, lo:lo + n], st[:, lo + n:lo + 2 * n], st[:, 300:300 + n]
                link(dve.tensor_scalar(y.bitcast(I32), v.bitcast(I32), -0.5, ROOT_BITS, ALU.mult, ALU.add))
                for _step in range(3):
                    link(tt(a, y, y, ALU.mult))
                    link(dve.scalar_tensor_tensor(a, a, -0.5, v, ALU.mult, ALU.mult))
                    link(dve.scalar_tensor_tensor(y, a, 1.5, y, ALU.add, ALU.mult))

            def mean(dst, src, n):
                link(dve.tensor_scalar(dst, src, 1.0 / n, EPS, ALU.mult, ALU.add))

            def row_norm(t, src, dst, lo, name):
                own[name + "_s"] = own.get(name + "_s", 0) + 1
                dve.wait_ge(sem(name + "_ss"), own[name + "_s"])
                a = lo + 2 * t
                mean(st[:, a:a + 1], st[:, 280 + lo // 2 + t:281 + lo // 2 + t], DM)
                inverse_root(a, 1)
                mark(dve.tensor_scalar(dst, src, st[:, a + 1:a + 2], None, ALU.mult), name + "_rows")

            def reduce_angle(x, k, rows):
                link(dve.tensor_scalar(k, x, 1.0 / (2 * np.pi), ROUND, ALU.mult, ALU.add))
                link(dve.tensor_scalar(k, k, -ROUND, None, ALU.add))
                for part in (TWO_PI_A, TWO_PI_B, TWO_PI_C):
                    link(dve.scalar_tensor_tensor(x, k, -part, x, ALU.mult, ALU.add))
                link(dve.tensor_scalar(x, x, PI_IN, -PI_IN, ALU.min, ALU.max))
                link(dve.tensor_scalar(k, x, -1.0, None, ALU.mult))
                link(tt(k, k, x, ALU.min))
                return dve.tensor_scalar(k, k, np.pi / 2, None, ALU.add)

            mark(dve.memset(st[:, 399:400], 1.0), "one_ready")
            for t in range(TT):
                row_norm(t, xres[:, t, :], xn1[:, DM * t:DM * t + DM], 0, "x")
            for t in range(TT):
                row_norm(t, mem_tok[:, DM * t:DM * t + DM], mem_tok[:, DM * t:DM * t + DM], 4, "mem")
            dve.wait_ge(sem("consts_in"), 16 * (8 + len(GAINS)))
            link(dve.tensor_copy(posf[:, :], posi[:, :]))
            ang, turns = rope[:, 1, :, :], rope[:, 0, :, :]
            for t in range(TT):
                link(dve.tensor_scalar(ang[:, t, 0:32], inv[:, 0:32], posf[:, t:t + 1], None, ALU.mult))
                link(dve.tensor_scalar(ang[:, t, 32:40], inv[:, 32:40], posf[:, TT + t:TT + t + 1], None, ALU.mult))
            mark(reduce_angle(ang, turns, P), "angle")

            dve.wait_ge(sem("taken_act"), taken("ckv")[1])
            ck = ckv.rearrange("p (t c) -> p t c", c=RANK + ROPE)
            for t in range(TT):
                link(tt(qdec[:, 0:320], ck[:, t, :], ck[:, t, :], ALU.mult))
                link(dve.tensor_reduce(st[:, 284 + t:285 + t], qdec[:, 0:RANK], AX.X, ALU.add))
                link(dve.tensor_reduce(st[:, 286 + t:287 + t], qdec[:, RANK:RANK + ROPE], AX.X, ALU.add))
            mean(st[:, 8:10], st[:, 284:286], RANK)
            mean(st[:, 10:12], st[:, 286:288], ROPE)
            inverse_root(8, 4)
            for t in range(TT):
                mark(dve.tensor_scalar(ck[:, t, 0:RANK], ck[:, t, 0:RANK], st[:, 12 + t:13 + t], None, ALU.mult), "ckv_rows")
                link(dve.tensor_scalar(ck[:, t, RANK:RANK + ROPE], ck[:, t, RANK:RANK + ROPE], st[:, 14 + t:15 + t], None, ALU.mult))
            kr = ck[:, :, RANK:RANK + ROPE]
            link(tt(kr, kr, bc(gain["g_k_rope"].unsqueeze(1), [P, TT, ROPE]), ALU.mult))
            dve.wait_ge(sem("rope_ready"), 1)
            kp = kpe.rearrange("p (t c) -> p t c", c=2 * ROPE)
            cos_a, sin_a = rope[:, 0, :, 0:32], rope[:, 1, :, 0:32]
            tmp = [kdec[:, 64 * i:64 * i + 64].rearrange("p (t c) -> p t c", c=32) for i in range(4)]
            x1, x2 = kr[:, :, 0:32], kr[:, :, 32:64]
            step(tt(tmp[0], x1, cos_a, ALU.mult))
            step(tt(tmp[1], x2, sin_a, ALU.mult))
            step(tt(tmp[2], x1, sin_a, ALU.mult))
            link(tt(tmp[3], x2, cos_a, ALU.mult))
            for i in range(2):
                link(tt(kp[:, :, 64 * i:64 * i + 32], tmp[0], tmp[1], ALU.subtract))
                mark(tt(kp[:, :, 64 * i + 32:64 * i + 64], tmp[2], tmp[3], ALU.add), "kpe_rows")

            p = arrived("gg")
            b4 = bT.rearrange("p (h s) -> p h s", s=SEQ)
            for i in range(2):
                ins = tt(b4[:, 2 * i:2 * i + 2, :], p[:, 512 * i:512 * i + 512].rearrange("p (h s) -> p h s", s=SEQ),
                         bc(col("b_gla_gate", 2 * i, 2).unsqueeze(2), [P, 2, SEQ]), ALU.add)
            mark(ins, "taken_dve")
            dve.wait_ge(sem("gate_ln"), 1)
            link(dve.scalar_tensor_tensor(dec, bT, 0.0, dec, ALU.min, ALU.subtract))
            for i in range(2 * GH):
                link(dve.tensor_tensor_scan(bT[:, P * i:P * i + P], bc(st[:, 399:400], [P, P]), dec[:, P * i:P * i + P],
                                            0.0, ALU.mult, ALU.add))

            dve.wait_ge(sem("taken_act"), taken("q2")[1])
            for t in range(TT):
                qt = q_tok[:, MH * QW * t:MH * QW * (t + 1)]
                link(tt(knT[:, 0:1536], qt, qt, ALU.mult))
                s3 = knT[:, 0:1536].rearrange("p (h c) -> p h c", c=QW)
                link(dve.tensor_reduce(st[:, 16 + 8 * t:24 + 8 * t], s3[:, :, 0:NOPE], AX.X, ALU.add))
                link(dve.tensor_reduce(st[:, 32 + 8 * t:40 + 8 * t], s3[:, :, NOPE:QW], AX.X, ALU.add))
            mean(st[:, 16:32], st[:, 16:32], NOPE)
            mean(st[:, 32:48], st[:, 32:48], ROPE)
            inverse_root(16, 32)
            q16 = q_tok.rearrange("p (g c) -> p g c", c=QW)
            mark(tt(q16[:, :, 0:NOPE], q16[:, :, 0:NOPE], bc(st[:, 48:64].unsqueeze(2), [P, 16, NOPE]), ALU.mult), "q_rows")
            link(tt(q16[:, :, NOPE:QW], q16[:, :, NOPE:QW], bc(st[:, 64:80].unsqueeze(2), [P, 16, ROPE]), ALU.mult))
            link(tt(q16[:, :, NOPE:QW], q16[:, :, NOPE:QW], bc(gain["g_q_rope"].unsqueeze(1), [P, 16, ROPE]), ALU.mult))
            q4 = q_tok.rearrange("p (t h c) -> p t h c", t=TT, c=QW)
            x1, x2 = q4[:, :, :, NOPE:NOPE + 32], q4[:, :, :, NOPE + 32:QW]
            cosb = bc(cos_a.unsqueeze(2), [P, TT, MH, 32])
            sinb = bc(sin_a.unsqueeze(2), [P, TT, MH, 32])
            tmp = [(qdec, kdec)[i // 2][:, 512 * (i % 2):512 * (i % 2) + 512].rearrange("p (t h c) -> p t h c", t=TT, c=32)
                   for i in range(4)]
            step(tt(tmp[0], x1, cosb, ALU.mult))
            step(tt(tmp[1], x2, sinb, ALU.mult))
            step(tt(tmp[2], x1, sinb, ALU.mult))
            link(tt(tmp[3], x2, cosb, ALU.mult))
            qp4 = qpe.rearrange("p (t h c) -> p t h c", t=TT, c=ROPE)
            link(tt(qp4[:, :, :, 0:32], tmp[0], tmp[1], ALU.subtract))
            mark(tt(qp4[:, :, :, 32:64], tmp[2], tmp[3], ALU.add), "qpe_rows")

            dve.wait_ge(sem("taken_act"), taken("kv3")[1])
            k16 = kv_tok.rearrange("p (g c) -> p g c", c=NOPE + DV)
            kn = k16[:, :, 0:NOPE]
            link(tt(knT.rearrange("p (g c) -> p g c", c=NOPE), kn, kn, ALU.mult))
            link(dve.tensor_reduce(st[:, 80:96], knT.rearrange("p (g c) -> p g c", c=NOPE), AX.X, ALU.add))
            mean(st[:, 80:96], st[:, 80:96], NOPE)
            inverse_root(80, 16)
            mark(tt(kn, kn, bc(st[:, 96:112].unsqueeze(2), [P, 16, NOPE]), ALU.mult), "k_rows")

            def scores(buf, n, parts, scale, name):
                for src, dst, mask, a in parts:
                    ins = dve.tensor_tensor_reduce(dst, src, mask, scale, -3e38, ALU.add, ALU.max, st[:, a:a + 1])
                return ins

            def minus(n, name):
                c = 340 + 2 * (n % 4)
                mark(dve.tensor_scalar(st[:, c:c + 2], st[:, c:c + 2], -1.0, None, ALU.mult), name + "_scores")

            def taken_score(ins):
                mark(ins, "score_taken")

            def attend(name, n, dst):
                p = scored()
                dve.wait_ge(sem(name + "_exp"), n + 1)
                c = 350 + 2 * (n % 4)
                link(dve.reciprocal(st[:, 360 + 2 * (n % 4):362 + 2 * (n % 4)], st[:, c:c + 2]))
                for t in range(TT):
                    o = dst(t)
                    w = o.shape[-1]
                    ins = dve.tensor_scalar(o, p[:, w * t:w * t + w], st[:, 360 + 2 * (n % 4) + t:361 + 2 * (n % 4) + t], None, ALU.mult)
                    if t == 0:
                        link(ins)
                mark(ins, "score_taken")

            om3 = o_mla.rearrange("p (t c) -> p t c", c=DM)
            for h in range(MH + 2):
                if h < MH:
                    p = scored()
                    s = soft[:, 512 * (h % 2):512 * (h % 2) + 512]
                    c = 340 + 2 * (h % 4)
                    link(scores(s, h, ((p[:, 0:128], s[:, 0:128], masks[:, 0, 128:256], c),), QW ** -0.5, None))
                    taken_score(scores(s, h, ((p[:, 128:384], s[:, 128:384], masks[:, 0, :], c + 1),), QW ** -0.5, None))
                    minus(h, "mla")
                if h >= 2:
                    attend("mla", h - 2, lambda t: om3[:, t, DV * (h - 2):DV * (h - 1)])

            dve.wait_ge(sem("taken_act"), taken("mk")[1])
            for i, (x, g) in enumerate(((mq_tok, "g_q_mem"), (mk_tok, "g_k_mem"))):
                x8 = x.rearrange("p (g c) -> p g c", c=EQ)
                q8 = qdec[:, 0:512].rearrange("p (g c) -> p g c", c=EQ)
                link(tt(q8, x8, x8, ALU.mult))
                link(dve.tensor_reduce(st[:, 144 + 8 * i:152 + 8 * i], q8, AX.X, ALU.add))
            mean(st[:, 144:160], st[:, 144:160], EQ)
            inverse_root(144, 16)
            for i, (x, g) in enumerate(((mq_tok, "g_q_mem"), (mk_tok, "g_k_mem"))):
                x8 = x.rearrange("p (g c) -> p g c", c=EQ)
                link(tt(x8, x8, bc(st[:, 160 + 8 * i:168 + 8 * i].unsqueeze(2), [P, 8, EQ]), ALU.mult))
                mark(tt(x8, x8, bc(gain[g].unsqueeze(1), [P, 8, EQ]), ALU.mult), "m_rows")

            rg3 = r_gla.rearrange("p (t c) -> p t c", c=DM)
            for t in range(TT):
                dve.wait_ge(sem("silu_sig"), t + 1)
                mark(tt(rg3[:, t, :], rg3[:, t, :], junk, ALU.mult), "silu_done")
                g4 = rg3[:, t, :].rearrange("p (h c) -> p h c", c=GV)
                link(tt(g4, g4, bc(gain["g_gla_out"].unsqueeze(1), [P, GH, GV]), ALU.mult))

            def level_diff(i):
                if i < len(LEVELS):
                    s = LEVELS[i]
                    b, dd = (x.rearrange("p (b u s) -> p b u s", u=2, s=s) for x in (bT, dec))
                    nb = 1024 // (2 * s)
                    ref = bc(b[:, :, 0, s - 1:s], [P, nb, s])
                    link(tt(dd[:, :, 0, :], ref, b[:, :, 0, :], ALU.subtract))
                    mark(tt(dd[:, :, 1, :], b[:, :, 1, :], ref, ALU.subtract), "level_diff")
                else:
                    b, dd = (x.rearrange("p (h t s) -> p h t s", t=TT, s=P) for x in (bT, dec))
                    link(tt(dd[:, :, 0, :], bc(b[:, :, 0, P - 1:P], [P, GH, P]), b[:, :, 0, :], ALU.subtract))
                    mark(dve.tensor_copy(dd[:, :, 1, :], b[:, :, 1, :]), "level_diff")

            om_mem = o_mem.rearrange("p (t c) -> p t c", c=DM)
            og3 = o_gla.rearrange("p (t c) -> p t c", c=DM)

            def gate_add(n, t):
                p = arrived(f"gate{GATES[n]}", t)
                dve.wait_ge(sem(f"bgate{n % 2}"), 16 * (n // 2 + 1))
                g = gate_buf[:, 1024 * (n % 2) + 512 * t:1024 * (n % 2) + 512 * t + 512]
                return tt(g, p[:, 512 * t:512 * t + 512], bgate[:, 512 * (n % 2):512 * (n % 2) + 512], ALU.add)

            def gate_take(n):
                link(gate_add(n, 0))
                mark(gate_add(n, 1), "taken_dve")

            def gate_apply(n, need):
                dve.wait_ge(sem("gate_sig"), need)
                i = GATES[n]
                o = (om3, og3, om_mem)[i // 2][:, :, 512 * (i % 2):512 * (i % 2) + 512]
                g = gate_buf[:, 1024 * (n % 2):1024 * (n % 2) + 1024].rearrange("p (t c) -> p t c", c=512)
                link(tt(o, o, g, ALU.mult))

            lv3 = levels.rearrange("p (l n) -> p l n", n=32)
            am3 = amat.rearrange("p (b n) -> p b n", n=P)
            ad3 = adiag.rearrange("p (b n) -> p b n", n=32)
            link(dve.memset(amat, 0.0))
            level_diff(0)
            for i in range(9):
                if i < EH:
                    p = scored()
                    s = soft[:, 512 * (i % 2):512 * (i % 2) + 512]
                    c = 340 + 2 * (i % 4)
                    zero = bc(masks[:, 0, 0:1], [P, 256])
                    link(scores(s, i, ((p[:, 0:256], s[:, 0:256], zero, c),), EQ ** -0.5, None))
                    taken_score(scores(s, i, ((p[:, 256:512], s[:, 256:512], zero, c + 1),), EQ ** -0.5, None))
                    minus(i, "mem")
                if 2 <= i < EH + 2:
                    attend("mem", i - 2, lambda t: om_mem[:, t, EV * (i - 2):EV * (i - 1)])
                p = scored()
                if i == 8:
                    taken_score(dve.tensor_copy(across, p[:, :]))
                elif i == 1:
                    taken_score(dve.tensor_copy(am3[0:64, :, 64:128], p[0:64, :].rearrange("p (b n) -> p b n", n=64)))
                elif i == 2:
                    src = p[:, 0:256].rearrange("p (b n) -> p b n", n=32)
                    link(dve.tensor_copy(am3[0:32, :, 32:64], src[0:32]))
                    taken_score(dve.tensor_copy(am3[64:96, :, 96:128], src[64:96]))
                else:
                    k = i - 3 if i else 5
                    mask = bc(lv3[:, k:k + 1, :], [P, 8, 32])
                    src = p[:, 0:256].rearrange("p (b n) -> p b n", n=32)
                    if i == 0:
                        taken_score(tt(ad3, src, mask, ALU.mult))
                    else:
                        w = wgate[:, 0:256]
                        taken_score(tt(w.rearrange("p (b n) -> p b n", n=32), src, mask, ALU.mult))
                        link(tt(adiag, adiag, w, ALU.add))
                if i < 8:
                    dve.wait_ge(sem("level_exp"), i + 1)
                    step(tt(qdec, qgT, dec, ALU.mult))
                    mark(tt(kdec, kgT, dec, ALU.mult), "level_ready")
                    dve.wait_ge(sem("dve_step"), count[0])
                    if i + 1 < 8:
                        level_diff(i + 1)
                if i == 7:
                    for k in range(4):
                        q = slice(32 * k, 32 * k + 32)
                        mark(dve.tensor_copy(am3[q, :, q], ad3[q]), "amat")
                if i in (3, 5, 7):
                    gate_take((i - 3) // 2)
                if i in (5, 7):
                    gate_apply((i - 5) // 2, (i - 5) // 2 + 1)
            for n in range(4):
                p = scored()
                taken_score(dve.tensor_copy(og3[:, n // 2, 512 * (n % 2):512 * (n % 2) + 512], p[:, :]))
            gate_take(3)
            for t in range(TT):
                link(tt(junk, og3[:, t, :], og3[:, t, :], ALU.mult))
                link(dve.tensor_reduce(st[:, 176 + 4 * t:180 + 4 * t], junk.rearrange("p (h c) -> p h c", c=GV), AX.X, ALU.add))
            mean(st[:, 176:184], st[:, 176:184], GV)
            inverse_root(176, 8)
            o8 = o_gla.rearrange("p (g c) -> p g c", c=GV)
            link(tt(o8, o8, bc(st[:, 184:192].unsqueeze(2), [P, 8, GV]), ALU.mult))
            link(tt(o_gla, o_gla, r_gla, ALU.mult))
            gate_apply(2, 3)
            gate_apply(3, 4)
            link(tt(o_mla, o_mla, o_mem, ALU.add))
            for t in range(TT):
                for n in (4, 5):
                    ins = gate_add(n, t)
                    mark(ins, "gate_in")
                for n in (4, 5):
                    c = 512 * (GATES[n] % 2)
                    g = gate_buf[:, 1024 * (n % 2) + 512 * t:1024 * (n % 2) + 512 * t + 512]
                    dve.wait_ge(sem("gate_sig"), 4 + 2 * t + n - 3)
                    link(tt(og3[:, t, c:c + 512], og3[:, t, c:c + 512], g, ALU.mult))
                    ins = tt(om3[:, t, c:c + 512], om3[:, t, c:c + 512], og3[:, t, c:c + 512], ALU.add)
                    mark(ins, "y_rows")

            def residual(name, i, t):
                p = arrived(name, t)
                x = xres[:, t, 512 * i:512 * i + 512]
                return tt(x, p[:, 512 * t:512 * t + 512], x, ALU.add)

            def residual_norm(names, dst):
                for t in range(TT):
                    for i in range(2):
                        mark(residual(names[i], i, t), "residual")
                    row_norm(t, xres[:, t, :], dst[:, DM * t:DM * t + DM], 0, "x")

            residual_norm(("wo0", "wo1"), xn2)

            R = srow[0:ST, :].rearrange("p (k n) -> p k n", n=128)
            lr, li, mag, cosr, sinr, kk, fre, fim, den, t1, t2 = (R[:, i, :] for i in (0, 1, 3, 4, 5, 6, 7, 8, 9, 10, 11))
            dve.wait_ge(sem("ssm_in"), 16 * 9)
            dve.wait_ge(sem("dt_ready"), 1)
            dtb = bc(srow[0:ST, 258:260].unsqueeze(2), [ST, 2, SN])
            h2 = lambda x: x.rearrange("p (a n) -> p a n", n=SN)
            link(tt(h2(mag), h2(lr), dtb, ALU.mult))
            link(tt(h2(sinr), h2(li), dtb, ALU.mult))
            mark(reduce_angle(sinr, cosr, ST), "theta")
            link(tt(t1, lr, lr, ALU.mult))
            link(tt(den, li, li, ALU.mult))
            link(tt(den, den, t1, ALU.add))
            link(dve.reciprocal(den, den))
            dve.wait_ge(sem("trig"), 1)
            link(tt(t1, mag, cosr, ALU.mult))
            link(tt(t2, mag, sinr, ALU.mult))
            link(dve.tensor_scalar(t1, t1, -1.0, None, ALU.add))
            link(tt(fre, t1, lr, ALU.mult))
            link(tt(kk, t2, li, ALU.mult))
            link(tt(fre, fre, kk, ALU.add))
            link(tt(fre, fre, den, ALU.mult))
            link(tt(fim, t2, lr, ALU.mult))
            link(tt(kk, t1, li, ALU.mult))
            link(tt(fim, fim, kk, ALU.subtract))
            mark(tt(fim, fim, den, ALU.mult), "lane_rows")

            dve.wait_ge(sem("turned_taken"), T_LANE)
            c4 = cs.rearrange("p (j r t) -> p j r t", r=2, t=CH)
            link(dve.memset(c4[:, :, 0, 0:1], 1.0))
            link(dve.memset(c4[:, :, 1, 0:1], 0.0))
            link(dve.tensor_copy(lam["ere"], lam["cos"]))
            link(dve.tensor_copy(lam["eim"], lam["sin"]))
            n = 1
            while n < CH:
                a, b = (tmp_cs[:, 2048 * i:2048 * i + 32 * n].rearrange("p (j t) -> p j t", t=n) for i in range(2))
                er, ei = (bc(lam[k].unsqueeze(2), [P, ST, n]) for k in ("ere", "eim"))
                pr, pi = c4[:, :, 0, 0:n], c4[:, :, 1, 0:n]
                link(tt(a, pr, er, ALU.mult))
                link(tt(b, pi, ei, ALU.mult))
                link(tt(c4[:, :, 0, n:2 * n], a, b, ALU.subtract))
                link(tt(a, pr, ei, ALU.mult))
                link(tt(b, pi, er, ALU.mult))
                link(tt(c4[:, :, 1, n:2 * n], a, b, ALU.add))
                link(tt(lam["sq"], lam["ere"], lam["ere"], ALU.mult))
                link(tt(lam["sq2"], lam["eim"], lam["eim"], ALU.mult))
                link(tt(lam["eim"], lam["ere"], lam["eim"], ALU.mult))
                link(dve.tensor_scalar(lam["eim"], lam["eim"], 2.0, None, ALU.mult))
                link(tt(lam["ere"], lam["sq"], lam["sq2"], ALU.subtract))
                n *= 2
            mark(dve.memset(cc, 0.0), "tables")

            for i in range(8):
                dve.wait_ge(sem("taken_act"), taken(f"up{i}")[1])
                u = hup[:, 1024 * i:1024 * i + 1024]
                mark(tt(u, u, u, ALU.mult), "ff_ready")

            dve.wait_ge(sem("turned_taken"), T_C)
            cr, ci = (tmp_cs[:, 1024 * i:1024 * i + 1024].rearrange("p (j c) -> p j c", c=32) for i in range(2))
            ta, tb = (tmp_cs[:, 2048 + 1024 * i:3072 + 1024 * i].rearrange("p (j c) -> p j c", c=32) for i in range(2))
            fr, fi = (bc(lam[k].unsqueeze(2), [P, ST, 32]) for k in ("fre", "fim"))
            for i in range(2):
                link(tt(ta, cr, (fr, fi)[i], ALU.mult))
                link(tt(tb, ci, (fi, fr)[i], ALU.mult))
                cv = cc[:, 1024 * i:1024 * i + 1024].rearrange("p (j c) -> p j c", c=32)
                for a in range(2):
                    q = slice(64 * a, 64 * a + 64)
                    w = slice(16 * a, 16 * a + 16)
                    if i == 0:
                        ins = tt(cv[q, :, w], ta[q, :, w], tb[q, :, w], ALU.subtract)
                    else:
                        ins = dve.scalar_tensor_tensor(cv[q, :, w], ta[q, :, w], -1.0, tb[q, :, w], ALU.mult, ALU.subtract)
                    mark(ins, "c_ready")

            residual_norm(("down0", "down1"), xn3)

            def z_silu(z):
                dve.wait_ge(sem("taken_act"), taken(z)[1])
                x = za if z == "za" else zs[:, 1024 * int(z[2]):1024 * int(z[2]) + 1024]
                mark(tt(x, x, raw, ALU.mult), "z_silu")

            def dqk(n):
                g = n % 3
                name, gn = (f"dq{g}", "q_norm_w_2") if n < 3 else (f"dk{g}", "k_norm_w_2")
                dve.wait_ge(sem("taken_act"), taken(name)[1])
                r16 = raw.rearrange("p (g c) -> p g c", c=DD)
                link(dve.tensor_reduce(st[:, 192:208], raw2.rearrange("p (g c) -> p g c", c=DD), AX.X, ALU.add))
                mean(st[:, 192:208], st[:, 192:208], DD)
                inverse_root(192, 16)
                link(tt(r16, r16, bc(st[:, 208:224].unsqueeze(2), [P, 16, DD]), ALU.mult))
                link(tt(r16, r16, bc(gain[gn][:, DD * g:DD * g + DD].unsqueeze(1), [P, 16, DD]), ALU.mult))
                r4 = raw.rearrange("p (t h c) -> p t h c", t=TT, c=DD)
                y1, y2 = r4[:, :, :, 0:8], r4[:, :, :, 8:16]
                cb, sb_ = (bc(rope[:, k, :, 32:40].unsqueeze(2), [P, TT, DH, 8]) for k in range(2))
                tm = [raw2[:, 128 * i:128 * i + 128].rearrange("p (t h c) -> p t h c", t=TT, c=8) for i in range(4)]
                step(tt(tm[0], y1, cb, ALU.mult))
                step(tt(tm[1], y2, sb_, ALU.mult))
                step(tt(tm[2], y2, cb, ALU.mult))
                link(tt(tm[3], y1, sb_, ALU.mult))
                link(tt(y1, tm[0], tm[1], ALU.subtract))
                mark(tt(y2, tm[2], tm[3], ALU.add), "dqk_rows")

            def ssm_out(i):
                u = uT[:, SEQ * i:SEQ * i + SEQ]
                p = scored()
                taken_score(dve.scalar_tensor_tensor(u, u, col("d_skip_2", i), p[:, 0:SEQ], ALU.mult, ALU.add))

            for j in range(ST):
                p = scored()
                w4 = p[:, :].rearrange("p (c t) -> p c t", t=CH)
                tab = c4[:, j]
                m1, m2 = wrot[:, 0:512], wrot[:, 512:1024]
                step(tt(m1.rearrange("p (c t) -> p c t", t=CH), w4, bc(tab[:, 0:1, :], [P, 4, CH]), ALU.mult))
                taken_score(tt(m2.rearrange("p (c t) -> p c t", t=CH), w4, bc(tab[:, 1:2, :], [P, 4, CH]), ALU.mult))
                dve.wait_ge(sem("dve_step"), count[0])
                step(tt(m1[:, 0:256], m1[:, 0:256], m2[:, 256:512], ALU.add))
                link(tt(m1[:, 256:512], m1[:, 256:512], m2[:, 0:256], ALU.subtract))
                g = gst[:, 512 * (j % 2):512 * (j % 2) + 512]
                mg = bc(lam["mag"][:, j:j + 1], [P, CH])
                if j >= 2:
                    dve.wait_ge(sem("h_ready"), 2 * (j - 1))
                step(dve.tensor_tensor_scan(g[:, 0:CH], mg, m1[:, 0:CH], 0.0, ALU.mult, ALU.add))
                link(dve.tensor_tensor_scan(g[:, 256:256 + CH], mg, m1[:, 256:256 + CH], 0.0, ALU.mult, ALU.add))
                gr, gi = g[:, CH - 1:CH], g[:, 256 + CH - 1:256 + CH]
                er, ei = lam["ere"][:, j:j + 1], lam["eim"][:, j:j + 1]
                step(tt(carry[:, 0:1], gi, ei, ALU.mult))
                link(tt(carry[:, 1:2], gr, ei, ALU.mult))
                step(dve.scalar_tensor_tensor(carry[:, 2:3], gr, er, carry[:, 0:1], ALU.mult, ALU.subtract))
                link(dve.scalar_tensor_tensor(carry[:, 3:4], gi, er, carry[:, 1:2], ALU.mult, ALU.add))
                step(dve.tensor_tensor_scan(g[:, CH:256], mg, m1[:, CH:256], carry[:, 2:3], ALU.mult, ALU.add))
                mark(dve.tensor_tensor_scan(g[:, 256 + CH:512], mg, m1[:, 256 + CH:512], carry[:, 3:4], ALU.mult, ALU.add), "g_ready")
                if j % 4 == 3 and j >= 7:
                    ssm_out(j // 4 - 1)
                if j in (16, 20, 24):
                    z_silu(("zs0", "zs1", "za")[(j - 16) // 4])
                if j == 30:
                    dqk(0)
            dqk(1)
            ssm_out(7)
            for i in range(2):
                y, z = uT[:, 1024 * i:1024 * i + 1024], gz[:, 1024 * i:1024 * i + 1024]
                link(tt(z, y, y, ALU.mult))
                link(dve.tensor_scalar(z, z, 0.044715, 1.0, ALU.mult, ALU.add))
                mark(tt(z, z, y, ALU.mult), "gelu_z")
            dqk(2)
            for i in range(2):
                dve.wait_ge(sem("gelu_sig"), i + 1)
                y, z = uT[:, 1024 * i:1024 * i + 1024], gz[:, 1024 * i:1024 * i + 1024]
                mark(tt(y, y, z, ALU.mult), "gelu_ready")
                link(tt(z, y, zs[:, 1024 * i:1024 * i + 1024], ALU.mult))
            for n in (3, 4, 5):
                dqk(n)

            for s in range(DH // 2 + 1):
                if s < DH // 2:
                    for src, at, w, mask, a in ((0, 384, 512, masks[:, 1:3, :].rearrange("p g s -> p (g s)"), 132),
                                                (0, 896, 256, masks[:, 3, :], 133)):
                        for e in range(2):
                            p, buf = scored(), dsoft[:, 1152 * e:1152 * e + 1152]
                            taken_score(scores(buf, 0, ((p[:, 0:w], buf[:, at:at + w], mask, a + 2 * e),), DD ** -0.5, None))
                    for e in range(2):
                        h = 2 * s + e
                        p, buf = scored(), dsoft[:, 1152 * e:1152 * e + 1152]
                        c = 340 + 2 * (h % 4)
                        taken_score(scores(buf, h, ((p[:, 0:384].rearrange("p (g s) -> p g s", s=128),
                                                     buf[:, 0:384].rearrange("p (g s) -> p g s", s=128), masks[:, 1:4, 128:256], c),),
                                           DD ** -0.5, None))
                        link(tt(st[:, c + 1:c + 2], st[:, 132 + 2 * e:133 + 2 * e], st[:, 133 + 2 * e:134 + 2 * e], ALU.max))
                        minus(h, "dil")
                    for h in (2 * s, 2 * s + 1):
                        dve.wait_ge(sem("dil_exp"), h + 1)
                        c, buf = 350 + 2 * (h % 4), dsoft[:, 1152 * (h % 2):1152 * (h % 2) + 1152]
                        link(dve.reciprocal(st[:, c + 10:c + 12], st[:, c:c + 2]))
                        step(dve.tensor_scalar(buf[:, 0:384], buf[:, 0:384], st[:, c + 10:c + 11], None, ALU.mult))
                        mark(dve.tensor_scalar(buf[:, 384:1152], buf[:, 384:1152], st[:, c + 11:c + 12], None, ALU.mult), "dil_norm")
                if s:
                    p, k = scored(), SEQ * (s - 1)
                    mark(tt(yaT[:, k:k + SEQ], p[:, 0:SEQ], za[:, k:k + SEQ], ALU.mult), "score_taken")
            dve.wait_ge(sem("taken_act"), taken("glu0")[1])
            mark(tt(yssT[:, 0:1024], sig_glu[:, 0:1024], gz[:, 0:1024], ALU.mult), "yss")
            dve.wait_ge(sem("taken_act"), taken("glu1")[1])
            mark(tt(yssT[:, 1024:2048], sig_glu[:, 1024:2048], gz[:, 1024:2048], ALU.mult), "yss")
            m3 = m_tok.rearrange("p (t c) -> p t c", c=DM)
            r3 = rsig.rearrange("p (t c) -> p t c", c=DM)
            s3 = asig.rearrange("p (t c) -> p t c", c=DM)
            for i in range(2):
                for t in range(TT):
                    p = arrived(f"ao{i}", t)
                    ins = tt(m3[:, t, 512 * i:512 * i + 512], p[:, 512 * t:512 * t + 512], s3[:, t, 512 * i:512 * i + 512], ALU.mult)
                    if t == 0:
                        link(ins)
                mark(ins, "taken_dve")
            for t in range(TT):
                for i in range(2):
                    p = arrived(f"so{i}", t)
                    r = r3[:, t, 512 * i:512 * i + 512]
                    ins = tt(r, p[:, 512 * t:512 * t + 512], r, ALU.mult)
                    mark(ins, "taken_dve") if t else link(ins)
                    m = m3[:, t, 512 * i:512 * i + 512]
                    mark(tt(m, m, r, ALU.add), "m_sum")
            for t in range(TT):
                for i in range(2):
                    mark(residual(f"wp{i}", i, t), "result")

        @block.tensor
        def _(pe):
            n_unit = {"turned": 0, "score": 0}
            turned_at = {}

            def unit(kind):
                n = n_unit[kind]
                n_unit[kind] += 1
                if n >= 2:
                    pe.wait_ge(sem(kind + "_taken"), n - 1)
                return bank[kind][n % 2]

            def turn(name, blocks):
                b = unit("turned")
                a = 0
                for x in blocks:
                    rows = x.shape[0]
                    ins = pe.transpose(b[0:x.shape[1], a:a + rows], x, ident[0:rows, 0:rows])
                    a += rows
                ins.then_inc(sem("turned_ready"), 1)
                turned_at[name] = n_unit["turned"]

            def is_turned(name):
                pe.wait_ge(sem("turned_taken"), turned_at[name])

            def matmuls(name, half):
                j = JOB[name]
                _, o, w, r0, rows, c0, cols = JOBS[j]
                p = pair[OUTS.index(o) % 2]
                if w is None:
                    return [(p[:, SEQ * h:SEQ * h + SEQ], wgate[0:GR, P * h:P * h + P], aT[0:GR, :], True, True)
                            for h in (2 * half, 2 * half + 1)]
                nk = rows // P
                ws = ring[:, STREAMED.index(j) % RING, 0:nk * cols].rearrange("p (k n) -> p k n", n=cols)
                base, total = 0, nk
                if o.startswith("kv"):
                    act_ = lambda k: ckvT[:, SEQ * k:SEQ * k + SEQ]
                elif o in ("mk", "mv0", "mv1"):
                    act_ = lambda k: memT[:, SEQ * k:SEQ * k + SEQ]
                elif o.startswith("down"):
                    base, total = KD * int(name[-1]), FF // P
                    act_ = lambda k: hup[:, SEQ * (base + k):SEQ * (base + k) + SEQ]
                elif o.startswith("glu"):
                    act_ = lambda k: uT[:, SEQ * k:SEQ * k + SEQ]
                elif o.startswith("so"):
                    act_ = lambda k: yssT[:, SEQ * k:SEQ * k + SEQ]
                elif o.startswith("ao"):
                    act_ = lambda k: yaT[:, SEQ * k:SEQ * k + SEQ]
                else:
                    act_ = lambda k: hT[:, k, :]
                if o in SPLIT_TOKENS:
                    return [(p[:, SEQ * c + P * half:SEQ * c + P * half + P], ws[:, k, P * c:P * c + P],
                             act_(k)[:, P * half:P * half + P], k == 0, k == nk - 1) for c in range(4) for k in range(nk)]
                if cols < P:
                    return [(p[0:cols, 0:SEQ], ws[:, k, :], act_(k), k == 0, k == nk - 1)
                            for k in range(nk // 2 * half, nk // 2 * (half + 1))]
                if o in CHANNEL_MAJOR:
                    return [(p[:, SEQ * c:SEQ * c + SEQ], ws[:, k, P * c:P * c + P], act_(k), k == 0, k == nk - 1)
                            for c in (2 * half, 2 * half + 1) for k in range(nk)]
                return [(p[:, 512 * half:512 * half + cols], act_(k)[:, P * half:P * half + P], ws[:, k, :], base + k == 0,
                         base + k == total - 1) for k in range(nk)]

            finished = [0]

            def half_job(name, half, sub=0, of=1):
                j = JOB[name]
                o = JOBS[j][1]
                if half == 0 and sub == 0:
                    if JOBS[j][2]:
                        n = STREAMED.index(j)
                        pe.wait_ge(sem(f"weights{n % RING}"), 16 * (n // RING + 1))
                    i = OUTS.index(o)
                    if i >= 2 and FIRST_JOB[o] == name:
                        by, v = taken(OUTS[i - 2])
                        pe.wait_ge(sem(by), v)
                mm = matmuls(name, half)
                n = len(mm)
                lo, hi = n * sub // of, n * (sub + 1) // of
                for o_, s, m, a, b in mm[lo:hi]:
                    ins = pe.matmul(o_, s, m, start=a, stop=b, skip_group_check=o.startswith("down"))
                if sub == of - 1:
                    assert HALVES[finished[0]] == (name, half), (HALVES[finished[0]], name, half)
                    finished[0] += 1
                    ins.then_inc(sem("half_done"), 1)

            def part(name, q):
                half_job(name, q // 2, q % 2, 2)

            def job(name):
                half_job(name, 0)
                half_job(name, 1)

            def fill(names, i, n):
                for q in range(n * i, n * i + n):
                    if q < 4 * len(names):
                        part(names[q // 4], q % 4)

            def turn_rows(name, x, t):
                for g in range(2):
                    turn(name, [x[:, DM * t + P * k:DM * t + P * k + P] for k in range(4 * g, 4 * g + 4)])

            def ktiles(x, w=DM):
                v = x.rearrange("p (t c) -> p t c", c=w)
                return [v[:, t, P * k:P * k + P] for k in range(w // P) for t in range(TT)]

            pe.wait_ge(sem("ident_in"), 16)
            pe.wait_ge(sem("rows_in"), 16 * len(COLS))
            turn("cols", [prow[:, :]])
            pe.wait_ge(sem("x_rows"), 1)
            turn_rows("x first", xn1, 0)
            pe.wait_ge(sem("x_rows"), 2)
            turn_rows("x", xn1, 1)
            is_turned("x first")
            half_job("ckv", 0)
            is_turned("x")
            half_job("ckv", 1)
            half_job("gq", 0)
            pe.wait_ge(sem("mem_rows"), 1)
            turn_rows("mem", mem_tok, 0)
            half_job("gq", 1)
            pe.wait_ge(sem("mem_rows"), 2)
            turn_rows("mem", mem_tok, 1)
            job("gk")
            job("ga")
            job("q0")
            pe.wait_ge(sem("ckv_rows"), 2)
            ck = ckv.rearrange("p (t c) -> p t c", c=RANK + ROPE)
            turn("ckv", [ck[:, t, P * k:P * k + P] for k in range(2) for t in range(TT)])
            pe.wait_ge(sem("kpe_rows"), 2)
            turn("kpe", [kpe[:, P * t:P * t + P] for t in range(TT)])
            pe.wait_ge(sem("taken_act"), taken("ga")[1])
            pe.wait_ge(sem("consts_in"), 16 * (8 + len(GAINS)))
            job("gg")
            for i in (1, 2):
                job(f"q{i}")
            is_turned("ckv")
            for i in range(4):
                job(f"kv{i}")
            q16 = q_tok.rearrange("p (t h c) -> p t h c", t=TT, c=QW)
            k16 = kv_tok.rearrange("p (t h c) -> p t h c", t=TT, c=NOPE + DV)

            def turn_heads(name, x, g):
                turn(name, [x[:, t, h, 0:NOPE] for h in (2 * g, 2 * g + 1) for t in range(TT)])

            pe.wait_ge(sem("q_rows"), 1)
            for g in range(4):
                turn_heads("qn", q16, g)
            half_job("gv0", 0)
            pe.wait_ge(sem("qpe_rows"), 1)
            for g in range(2):
                turn("qp", ktiles(qpe, MH * ROPE)[4 * g:4 * g + 4])
            half_job("gv0", 1)
            half_job("gv1", 0)
            pe.wait_ge(sem("k_rows"), 1)
            turn_heads("kn", k16, 0)
            turn_heads("kn", k16, 1)
            half_job("gv1", 1, 0, 4)
            turn_heads("kn", k16, 2)
            turn_heads("kn", k16, 3)
            half_job("gv1", 1, 1, 4)
            is_turned("kn")

            for h in range(MH + 2):
                if h == 0:
                    part("gv1", 3)
                else:
                    fill(["gr0", "gr1", "mq", "mk", "mv0"], h - 1, 2)
                if h < MH:
                    b = unit("score")
                    r = slice(64 * (h % 2), 64 * (h % 2) + 64)
                    for t in range(TT):
                        w = P * (t + 1)
                        o = b[:, P * t:P * t + w]
                        pe.matmul(o, qnT[:, SEQ * h + P * t:SEQ * h + P * t + P], knT[:, SEQ * h:SEQ * h + w], start=True, stop=False)
                        ins = pe.matmul(o, qpT[r, SEQ * (h // 2) + P * t:SEQ * (h // 2) + P * t + P], kpeT[r, 0:w], start=False, stop=True)
                    ins.then_inc(sem("score_ready"), 1)
                if 1 <= h <= MH:
                    pe.wait_ge(sem("mla_exp"), h)
                    s = soft[:, 512 * ((h - 1) % 2):512 * ((h - 1) % 2) + 384]
                    turn(f"mla{h - 1}", [s[:, 0:128], s[:, 128:256], s[:, 256:384]])
                if h >= 2:
                    i = h - 2
                    is_turned(f"mla{i}")
                    b = unit("score")
                    s = softT[:, 512 * (i % 2):512 * (i % 2) + 384]
                    v = lambda t: k16[:, t, i, NOPE:NOPE + DV]
                    pe.matmul(b[:, 0:128], s[:, 0:128], v(0), start=True, stop=True)
                    pe.matmul(b[:, 128:256], s[:, 128:256], v(0), start=True, stop=False)
                    pe.matmul(b[:, 128:256], s[:, 256:384], v(1), start=False, stop=True).then_inc(sem("score_ready"), 1)
            half_job("mv0", 1)
            for e in range(3):
                half_job("mv1", 0, e, 4)
            pe.wait_ge(sem("m_rows"), 2)
            turn("qm", ktiles(mq_tok, 256))
            turn("km", ktiles(mk_tok, 256))
            half_job("mv1", 0, 3, 4)
            is_turned("km")

            vm3 = vm.rearrange("p (t c) -> p t c", c=DM)
            vg3 = vg.rearrange("p (t c) -> p t c", c=DM)
            for i in range(9):
                fill(["mv1", "gate0", "gate1", "gate4", "gate5"], i + 1, 2)
                if i < EH:
                    b = unit("score")
                    r = slice(64 * (i % 2), 64 * (i % 2) + 64)
                    for t in range(TT):
                        ins = pe.matmul(b[:, SEQ * t:SEQ * t + SEQ], qmT[r, SEQ * (i // 2) + P * t:SEQ * (i // 2) + P * t + P],
                                        kmT[r, SEQ * (i // 2):SEQ * (i // 2) + SEQ], start=True, stop=True)
                    ins.then_inc(sem("score_ready"), 1)
                if 1 <= i <= EH:
                    pe.wait_ge(sem("mem_exp"), i)
                    s = soft[:, 512 * ((i - 1) % 2):512 * ((i - 1) % 2) + 512]
                    turn(f"mem{i - 1}", [s[:, P * k:P * k + P] for k in range(4)])
                if 2 <= i < EH + 2:
                    h = i - 2
                    is_turned(f"mem{h}")
                    pe.wait_ge(sem("taken_act"), taken("mv1")[1])
                    b = unit("score")
                    s = softT[:, 512 * (h % 2):512 * (h % 2) + 512]
                    for t in range(TT):
                        for k in range(2):
                            ins = pe.matmul(b[:, SEQ * t:SEQ * t + SEQ], s[:, 256 * t + P * k:256 * t + P * k + P],
                                            vm3[:, k, EV * h:EV * h + EV], start=k == 0, stop=k == 1)
                    ins.then_inc(sem("score_ready"), 1)
                if i:
                    pe.wait_ge(sem("level_ready"), i)
                ks, qs = (kdec, qdec) if i else (kgT, qgT)
                b = unit("score")
                if i == 8:
                    for h in range(GH):
                        ins = pe.matmul(b[:, P * h:P * h + P], ks[:, SEQ * h:SEQ * h + P], qs[:, SEQ * h + P:SEQ * h + 2 * P], start=True, stop=True)
                else:
                    w, blocks = {1: (64, ((0, 0, 64),)), 2: (32, ((0, 0, 32), (64, 64, 96)))}.get(
                        i, (32, tuple((32 * k, 32 * k, 32 * k) for k in range(4))))
                    for x in range(GH * TT):
                        for lane0, k0, q0 in blocks:
                            ins = pe.matmul(b[lane0:lane0 + w, w * x:w * x + w], ks[:, P * x + k0:P * x + k0 + w],
                                            qs[:, P * x + q0:P * x + q0 + w], start=True, stop=True)
                ins.then_inc(sem("score_ready"), 1)
            pe.wait_ge(sem("amat"), 4)
            for n in range(4):
                b = unit("score")
                t = n // 2
                for k in range(2):
                    h = 2 * (n % 2) + k
                    o = b[:, GV * k:GV * k + GV]
                    ins = pe.matmul(o, amat[:, P * (2 * h + t):P * (2 * h + t) + P], vg3[:, t, GV * h:GV * h + GV], start=True, stop=t == 0)
                    if t:
                        ins = pe.matmul(o, across[:, P * h:P * h + P], vg3[:, 0, GV * h:GV * h + GV], start=False, stop=True)
                ins.then_inc(sem("score_ready"), 1)
            half_job("gate2", 0)
            half_job("gate3", 0)
            half_job("gate2", 1)
            half_job("gate3", 1, 0, 2)
            pe.wait_ge(sem("y_rows"), 2)
            turn_rows("y", o_mla, 0)
            half_job("gate3", 1, 1, 2)
            is_turned("y")
            half_job("wo0", 0)
            half_job("wo1", 0, 0, 2)
            pe.wait_ge(sem("y_rows"), 4)
            turn_rows("y", o_mla, 1)
            half_job("wo1", 0, 1, 2)
            is_turned("y")
            half_job("wo0", 1)
            half_job("wo1", 1, 0, 2)
            pe.wait_ge(sem("x_rows"), 3)
            turn_rows("x", xn2, 0)
            half_job("wo1", 1, 1, 2)
            is_turned("x")

            half_job("up0", 0)
            pe.wait_ge(sem("x_rows"), 4)
            turn_rows("x", xn2, 1)
            half_job("up1", 0)
            is_turned("x")
            half_job("up0", 1)
            half_job("up1", 1)
            R = srow[0:ST, :].rearrange("p (k n) -> p k n", n=128)
            for i in range(2, 8):
                job(f"up{i}")
                if i == 2:
                    pe.wait_ge(sem("lane_rows"), 1)
                    turn("lane", [R[:, k, :] for k in (4, 5, 3, 7, 8)])
                    assert n_unit["turned"] == T_LANE, n_unit
                if i == 4:
                    pe.wait_ge(sem("bexp_ready"), 4)
                    for k in range(4):
                        turn("b", [bexp[:, 512 * k + P * m:512 * k + P * m + P] for m in range(4)])
            for k in range(3):
                pe.wait_ge(sem("ff_ready"), 2 * k + 2)
                job(f"down0{k}")
                if k == 0:
                    for m in range(4):
                        turn("c", [cnat[:, 512 * m + P * a:512 * m + P * a + P] for a in range(4)])
                    assert n_unit["turned"] == T_C, n_unit
                job(f"down1{k}")
            pe.wait_ge(sem("ff_ready"), 8)
            half_job("down03", 0)
            half_job("down13", 0)
            half_job("down03", 1)
            half_job("down13", 1, 0, 2)

            pe.wait_ge(sem("x_rows"), 5)
            turn_rows("x", xn3, 0)
            half_job("down13", 1, 1, 2)
            is_turned("x")
            half_job("us0", 0)
            pe.wait_ge(sem("x_rows"), 6)
            turn_rows("x", xn3, 1)
            half_job("us1", 0)
            is_turned("x")
            half_job("us0", 1)
            half_job("us1", 1)

            def states(k):
                b = unit("score")
                pe.wait_ge(sem("h_ready"), 2 * (4 * k + 4))
                for i in range(2):
                    for j in range(4 * k, 4 * k + 4):
                        a = 512 * (j % 8) + 256 * i
                        ins = pe.matmul(b[32 * (j % 4):32 * (j % 4) + 32, 0:SEQ], cc[:, 1024 * i + 32 * j:1024 * i + 32 * j + 32],
                                        hst[:, a:a + 256], start=i == 0, stop=i == 1)
                ins.then_inc(sem("score_ready"), 1)

            for j in range(ST):
                fill(["dv0", "dv1", "dv2", "zs0", "zs1", "za", "dq0", "dq1"], j, 1)
                if j % 4 == 0 and j >= 8:
                    states(j // 4 - 2)
                if j == 0:
                    pe.wait_ge(sem("taken_act"), taken("us1")[1])
                    pe.wait_ge(sem("c_ready"), 4)
                if j % 2:
                    two = [unit("score") for _ in range(2)]
                    for i in range(2):
                        for m, b in zip((j - 1, j), two):
                            r = slice(32 * (m % 4), 32 * (m % 4) + 32)
                            ins = pe.matmul(b[:, SEQ * i:SEQ * i + SEQ], bt[r, 1024 * i + P * (m // 4):1024 * i + P * (m // 4) + P],
                                            uT[r, SEQ * (m // 4):SEQ * (m // 4) + SEQ], start=True, stop=True)
                            if i:
                                ins.then_inc(sem("score_ready"), 1)

            def turn_dqk(n):
                pe.wait_ge(sem("dqk_rows"), n + 1)
                for k in range(2):
                    turn(f"dqk{n}", ktiles(raw, DW)[4 * k:4 * k + 4])

            half_job("dq2", 0)
            states(6)
            half_job("dq2", 1, 0, 2)
            turn_dqk(0)
            half_job("dq2", 1, 1, 2)
            half_job("dk0", 0)
            states(7)
            turn_dqk(1)
            half_job("dk0", 1)
            half_job("dk1", 0)
            turn_dqk(2)
            half_job("dk1", 1)
            half_job("dk2", 0)
            turn_dqk(3)
            half_job("dk2", 1)
            half_job("rs0", 0)
            turn_dqk(4)
            half_job("rs0", 1)
            half_job("rs1", 0)
            turn_dqk(5)
            half_job("rs1", 1)
            is_turned("dqk5")
            vd4 = vd.rearrange("p (g t c) -> p g t c", g=NDIL, t=TT)
            eighths = [0]

            def eighth(n=1):
                for _e in range(n):
                    e = eighths[0]
                    eighths[0] += 1
                    name = ("ra0", "ra1", "glu0", "glu1")[e // 8]
                    if e == 16:
                        pe.wait_ge(sem("gelu_ready"), 2)
                    half_job(name, e // 4 % 2, e % 4, 4)

            def pair_scores(products):
                two = [unit("score") for _ in range(2)]
                for n, (cols, g, t, w) in enumerate(products):
                    for e, b in enumerate(two):
                        r = slice(64 * e, 64 * e + 64)
                        a = 1024 * g + SEQ * s
                        ins = pe.matmul(b[:, cols], qdT[r, a + P * t:a + P * t + P], kdT[r, a:a + w], start=True, stop=True)
                        if n == len(products) - 1:
                            ins.then_inc(sem("score_ready"), 1)

            def dil_values(pair_):
                b = unit("score")
                for k in range(TT):
                    for g in range(NDIL):
                        for e in range(2):
                            a, h = 1152 * e + 384 * g, 2 * pair_ + e
                            o, p = (b[:, 0:SEQ], dsoftT[:, a:a + SEQ]) if k == 0 else (b[:, P:SEQ], dsoftT[:, a + SEQ:a + 384])
                            ins = pe.matmul(o[64 * e:64 * e + 64, :], vd4[:, g, k, DD * h:DD * h + DD], p,
                                            start=k == 0 and g == 0, stop=k == 1 and g == NDIL - 1)
                ins.then_inc(sem("score_ready"), 1)

            for s in range(DH // 2 + 1):
                if s < DH // 2:
                    pair_scores([(slice(256 * g, 256 * g + 256), g, 1, 256) for g in range(2)])
                    eighth()
                    pair_scores([(slice(0, 256), 2, 1, 256)])
                    eighth()
                    pair_scores([(slice(P * g, P * g + P), g, 0, P) for g in range(NDIL)])
                eighth()
                if s:
                    is_turned(f"dil{2 * s - 1}")
                    dil_values(s - 1)
                if s < DH // 2:
                    eighth()
                    for h in (2 * s, 2 * s + 1):
                        pe.wait_ge(sem("dil_norm"), h + 1)
                        p = dsoft[:, 1152 * (h % 2):1152 * (h % 2) + 1152]
                        for g in range(NDIL):
                            turn(f"dil{h}", [p[:, a:a + P] for a in (P * g, 384 + 256 * g, 512 + 256 * g)])
                            if (h % 2, g) in ((0, 1), (1, 0)):
                                eighth()
            eighth(32 - eighths[0])
            pe.wait_ge(sem("score_taken"), n_unit["score"])
            job("ao0")
            job("ao1")
            pe.wait_ge(sem("yss"), 2)
            half_job("so0", 0)
            half_job("so1", 0)
            half_job("so0", 1)
            half_job("so1", 1, 0, 2)
            pe.wait_ge(sem("m_sum"), 2)
            turn_rows("m", m_tok, 0)
            half_job("so1", 1, 1, 2)
            is_turned("m")
            half_job("wp0", 0)
            pe.wait_ge(sem("m_sum"), 4)
            turn_rows("m", m_tok, 1)
            half_job("wp1", 0)
            is_turned("m")
            half_job("wp0", 1)
            half_job("wp1", 1)


_INS = ["x", "mem", "positions", "g_mix", "w_in", "b_gate", "g_ckv", "w_ukv", "g_q_nope", "g_k_nope", "g_q_rope",
        "g_k_rope", "w_gla_gate", "b_gla_gate", "g_gla_out", "g_mem", "w_mem_kv", "g_q_mem", "g_k_mem", "w_o", "g_ffn",
        "w_up", "w_down", "positions_2", "norm_w_2", "w_in_2", "lam_re_2", "lam_im_2", "log_dt_2", "b_re_2", "b_im_2",
        "c_re_2", "c_im_2", "d_skip_2", "w_glu_2", "q_norm_w_2", "k_norm_w_2", "w_ssm_out_2", "w_attn_out_2", "w_o_2"]


def constants():
    p, k = np.arange(P)[:, None], np.arange(SEQ)[None, :]
    back = P + p - k
    masks = [np.where(back >= 0, 0.0, NEG)]
    for window, dil in ((128, 1), (512, 4), (2048, 16)):
        masks.append(np.where((back >= 0) & (back <= window) & (back % dil == 0), 0.0, NEG))
    j, i = np.arange(P)[:, None] % 32, np.arange(32)[None, :]
    levels = [((j // (2 * s) == i // (2 * s)) & (j % (2 * s) < s) & (i % (2 * s) >= s)) for s in LEVELS if s < 32]
    levels.append(i == j)
    one = np.float32(1)
    inv1 = one / (np.float32(10000.0) ** (np.arange(0, ROPE, 2, dtype=np.float32) / np.float32(ROPE)))
    inv2 = np.float32(500000.0) ** (-np.arange(0, RD, 2, dtype=np.float32) / np.float32(RD))
    inv = np.concatenate([inv1, inv2]).astype(np.float32)
    return {
        "c_ident": np.eye(P, dtype=np.float32),
        "c_masks": np.stack(masks, 1).astype(np.float32),
        "c_levels": np.stack(levels, 1).astype(np.float32),
        "c_inv": np.ascontiguousarray(np.broadcast_to(inv, (P, inv.size))),
    }


def kernel(**inputs):
    import numpy as _np
    import concourse.bacc as _bacc
    from concourse import mybir as _mybir
    from concourse.bass_utils import run_bass_kernel_spmd as _run

    nc = _bacc.Bacc("TRN2", target_bir_lowering=False, num_devices=1)
    arrays, aps = {}, {}
    for name in _INS:
        arrays[f"in_{name}"] = _np.ascontiguousarray(inputs[name])
    for name, a in constants().items():
        arrays[f"in_{name}"] = a
    for name, a in arrays.items():
        aps[name[3:]] = nc.dram_tensor(name, a.shape, _mybir.dt.from_np(a.dtype), kind="ExternalInput").ap()
    out = nc.dram_tensor("out", (1, SEQ, DM), F32, kind="ExternalOutput").ap()
    build(nc, aps, out)
    r = _run(nc, [arrays], core_ids=[0])
    return r.results[0]["out"]
```
